# Optimizing a Trainium2 kernel written in Bass

```python
import math
import jax
import jax.numpy as jnp
from jax import lax
import numpy as np

D_MODEL = 1024
BATCH = 1
SEQ = 256
DEPTH = 1
DEC_BATCH = 8
DEC_SEQ = 8
PAST_LEN = 1024
PAGE_SIZE = 128

HEAD_DIM = 64
A_Q_HEADS = D_MODEL // HEAD_DIM
A_KV_HEADS = A_Q_HEADS // 4
A_GROUP = A_Q_HEADS // A_KV_HEADS
WINDOW = 128
R_HEADS = 8
R_DK = D_MODEL // (2 * R_HEADS)
R_DV = D_MODEL // R_HEADS
R_CHUNK = 128
ROPE_BASE = 10000.0
C_CHUNK = 128
C_GROUPS = 8
C_GROUP_WIDTH = D_MODEL // C_GROUPS
N_EXPERTS = 32
TOP_K = 4
D_FF = D_MODEL
SWIGLU_LIMIT = 7.0
SWIGLU_ALPHA = 1.702
MOE_BLOCK = 128
EPS = 1e-6
IN_SPLITS = (A_Q_HEADS * HEAD_DIM, A_KV_HEADS * HEAD_DIM, A_KV_HEADS * HEAD_DIM,
             R_HEADS * R_DK, R_HEADS * R_DK, R_HEADS * R_DV, R_HEADS * R_DV,
             D_MODEL, D_MODEL, 3 * D_MODEL)

kernel_name = 'hybrid_swa_retention_gmlp_moe_step'

def _split_points():
    return [int(s) for s in np.cumsum(IN_SPLITS)[:-1]]

def rmsnorm(x, g):
    xf = x.astype(jnp.float32)
    y = xf * lax.rsqrt(jnp.mean(xf * xf, axis=-1, keepdims=True) + EPS)
    return (y * g.astype(jnp.float32)).astype(x.dtype)

def layernorm(x, g, b):
    xf = x.astype(jnp.float32)
    mu = jnp.mean(xf, axis=-1, keepdims=True)
    var = jnp.mean(jnp.square(xf - mu), axis=-1, keepdims=True)
    y = (xf - mu) * lax.rsqrt(var + EPS)
    return (y * g.astype(jnp.float32) + b.astype(jnp.float32)).astype(x.dtype)

def head_norm(x, g):
    B, L, H, dv = x.shape
    mu = jnp.mean(x, axis=-1, keepdims=True)
    var = jnp.mean(jnp.square(x - mu), axis=-1, keepdims=True)
    y = ((x - mu) * lax.rsqrt(var + EPS)).reshape(B, L, H * dv)
    return y * g.astype(jnp.float32)

def rope(x, pos):
    d = x.shape[-1]
    inv_freq = ROPE_BASE ** (-jnp.arange(0, d, 2, dtype=jnp.float32) / d)
    ang = pos.astype(jnp.float32)[:, None] * inv_freq[None, :]
    cos = jnp.cos(ang)[None, :, None, :]
    sin = jnp.sin(ang)[None, :, None, :]
    xf = x.astype(jnp.float32)
    x1, x2 = xf[..., : d // 2], xf[..., d // 2:]
    return jnp.concatenate([x1 * cos - x2 * sin, x2 * cos + x1 * sin], axis=-1)

def sink_attention(q, k, v, mask, sinks):
    s = jnp.einsum('bnqhgd,bnkhd->bnhgqk', q.astype(jnp.float32), k.astype(jnp.float32)) * (HEAD_DIM ** -0.5)
    s = jnp.where(mask[None, :, None, None], s, -jnp.inf)
    sink = sinks.astype(jnp.float32)[None, None, :, :, None, None]
    m = jnp.maximum(jnp.max(s, axis=-1, keepdims=True), sink)
    p = jnp.exp(s - m)
    denom = jnp.sum(p, axis=-1, keepdims=True) + jnp.exp(sink - m)
    return jnp.einsum('bnhgqk,bnkhd->bnqhgd', (p / denom).astype(v.dtype), v)

def window_attention_prompt(q, k, v, sinks):
    B, L = q.shape[:2]
    nb = L // WINDOW
    qb = q.reshape(B, nb, WINDOW, A_KV_HEADS, A_GROUP, HEAD_DIM)

    def band(t):
        tb = t.reshape(B, nb, WINDOW, A_KV_HEADS, HEAD_DIM)
        prev = jnp.concatenate([jnp.zeros_like(tb[:, :1]), tb[:, :-1]], axis=1)
        return jnp.concatenate([prev, tb], axis=2)

    i = jnp.arange(WINDOW)[:, None]
    j = jnp.arange(2 * WINDOW)[None, :]
    rel = i + WINDOW - j
    in_band = (rel >= 0) & (rel < WINDOW)
    valid = (jnp.arange(nb)[:, None, None] > 0) | (j >= WINDOW)[None]
    mask = in_band[None] & valid
    o = sink_attention(qb, band(k), band(v), mask, sinks)
    return o.reshape(B, L, A_Q_HEADS * HEAD_DIM)

def window_attention_step(q, k, v, k_buf, v_buf, sinks):
    B, L = q.shape[:2]
    W = k_buf.shape[1]
    kk = jnp.concatenate([k_buf.astype(k.dtype), k], axis=1)[:, None]
    vv = jnp.concatenate([v_buf.astype(v.dtype), v], axis=1)[:, None]
    q_pos = PAST_LEN + jnp.arange(L)
    k_pos = jnp.concatenate([PAST_LEN - W + jnp.arange(W), q_pos])
    d = q_pos[:, None] - k_pos[None, :]
    mask = ((d >= 0) & (d < WINDOW))[None]
    o = sink_attention(q[:, None], kk, vv, mask, sinks)
    return o.reshape(B, L, A_Q_HEADS * HEAD_DIM)

def retention(q, k, v, s0):
    B, L, H, dk = q.shape
    dv = v.shape[-1]
    C = math.gcd(L, R_CHUNK)
    nc = L // C
    log_gamma = jnp.log1p(-jnp.exp2(-5.0 - jnp.arange(H, dtype=jnp.float32)))
    idx = jnp.arange(C, dtype=jnp.float32)
    diff = idx[:, None] - idx[None, :]
    intra = jnp.where(diff[None] >= 0, jnp.exp(jnp.maximum(diff, 0.0)[None] * log_gamma[:, None, None]), 0.0)
    q_decay = jnp.exp((idx + 1.0)[:, None] * log_gamma[None, :])
    k_decay = jnp.exp((C - 1.0 - idx)[:, None] * log_gamma[None, :])
    c_decay = jnp.exp(C * log_gamma)

    def to_chunks(t):
        return jnp.moveaxis(t.astype(jnp.float32).reshape(B, nc, C, H, t.shape[-1]), 1, 0)

    def step(S, xs):
        qc, kc, vc = xs
        a = jnp.einsum('bihd,bjhd->bhij', qc, kc) * intra
        o = jnp.einsum('bhij,bjhe->bihe', a, vc) + jnp.einsum('bihd,bhde->bihe', qc, S) * q_decay[None, :, :, None]
        S = S * c_decay[None, :, None, None] + jnp.einsum('bjhd,bjhe->bhde', kc * k_decay[None, :, :, None], vc)
        return S, o

    S, o = lax.scan(step, s0.astype(jnp.float32), (to_chunks(q), to_chunks(k), to_chunks(v)))
    o = jnp.moveaxis(o, 0, 1).reshape(B, L, H, dv)
    return o, S

def chunk_gmlp(u, v, ws, bs):
    B, L, D = v.shape
    nc = -(-L // C_CHUNK)
    pad = nc * C_CHUNK - L
    vp = jnp.pad(v, ((0, 0), (0, pad), (0, 0))).reshape(B, nc, C_CHUNK, C_GROUPS, C_GROUP_WIDTH)
    causal = jnp.tril(jnp.ones((C_CHUNK, C_CHUNK), dtype=bool))
    w = jnp.where(causal[None], ws, 0.0).astype(v.dtype)
    mixed = jnp.einsum('gts,bnsgc->bntgc', w, vp) + bs.T.astype(v.dtype)[None, None, :, :, None]
    mixed = mixed.reshape(B, nc * C_CHUNK, D)[:, :L]
    return u * mixed

def moe(x, router_w, router_b, w1, b1, w2, b2):
    T, D = x.shape
    logits = (x @ router_w).astype(jnp.float32) + router_b.astype(jnp.float32)
    top_v, top_i = lax.top_k(logits, TOP_K)
    gates = jax.nn.softmax(top_v, axis=-1)
    n_assign = T * TOP_K
    flat_e = top_i.reshape(-1).astype(jnp.int32)
    flat_t = jnp.arange(n_assign, dtype=jnp.int32) // TOP_K
    flat_g = gates.reshape(-1)
    order = jnp.argsort(flat_e)
    se, st, sg = flat_e[order], flat_t[order], flat_g[order]
    counts = jnp.bincount(flat_e, length=N_EXPERTS)
    padded = (counts + MOE_BLOCK - 1) // MOE_BLOCK * MOE_BLOCK
    pend = jnp.cumsum(padded)
    pstart = pend - padded
    ustart = jnp.cumsum(counts) - counts
    dest = pstart[se] + jnp.arange(n_assign, dtype=jnp.int32) - ustart[se]
    n_blocks = -(-n_assign // MOE_BLOCK) + N_EXPERTS
    n_rows = n_blocks * MOE_BLOCK
    tok_buf = jnp.full((n_rows,), T, dtype=jnp.int32).at[dest].set(st)
    gate_buf = jnp.zeros((n_rows,), jnp.float32).at[dest].set(sg)
    block_e = jnp.clip(jnp.searchsorted(pend, jnp.arange(n_blocks) * MOE_BLOCK, side='right'), 0, N_EXPERTS - 1)
    x_pad = jnp.concatenate([x, jnp.zeros((1, D), x.dtype)], axis=0)
    xb = x_pad[tok_buf].reshape(n_blocks, MOE_BLOCK, D)

    def expert_block(args):
        xblk, e = args
        hdn = xblk @ w1[e] + b1[e]
        g, up = hdn[:, :D_FF], hdn[:, D_FF:]
        g = jnp.minimum(g, SWIGLU_LIMIT)
        up = jnp.clip(up, -SWIGLU_LIMIT, SWIGLU_LIMIT)
        act = (up + 1.0) * (g * jax.nn.sigmoid(g * SWIGLU_ALPHA))
        return act @ w2[e] + b2[e]

    yb = lax.map(expert_block, (xb, block_e)).reshape(n_rows, D)
    y = jnp.zeros((T + 1, D), yb.dtype).at[tok_buf].add(yb * gate_buf[:, None].astype(yb.dtype))
    return y[:T]

def block(x, c, pos0, k_buf, v_buf, s0, ln_mix_g, ln_ffn_g, w_ada, b_ada, w_in, b_gate,
          q_norm_g, k_norm_g, attn_sinks, ret_norm_g, gm_ln_g, gm_ln_b, gm_ws, gm_bs, w_out,
          router_w, router_b, moe_w1, moe_b1, moe_w2, moe_b2):
    B, L, D = x.shape
    mod = jax.nn.silu(c) @ w_ada + b_ada
    sh1, sc1, g1, sh2, sc2, g2 = [m[:, None, :] for m in jnp.split(mod, 6, axis=-1)]
    h = rmsnorm(x, ln_mix_g) * (1.0 + sc1) + sh1
    z = h @ w_in
    aq, ak, av, rq, rk, rv, rg, cu, cv, mg = jnp.split(z, _split_points(), axis=-1)

    aq = rmsnorm(aq.reshape(B, L, A_KV_HEADS, A_GROUP, HEAD_DIM), q_norm_g)
    ak = rmsnorm(ak.reshape(B, L, A_KV_HEADS, HEAD_DIM), k_norm_g)
    av = av.reshape(B, L, A_KV_HEADS, HEAD_DIM)
    sinks = attn_sinks.reshape(A_KV_HEADS, A_GROUP)
    if k_buf is None:
        oa = window_attention_prompt(aq, ak, av, sinks)
        keep = max(L - WINDOW, 0)
        new_k, new_v = ak[:, keep:], av[:, keep:]
    else:
        oa = window_attention_step(aq, ak, av, k_buf, v_buf, sinks)
        new_k, new_v = ak, av

    pos = pos0 + jnp.arange(L)
    rq = rope(rq.reshape(B, L, R_HEADS, R_DK), pos)
    rk = rope(rk.reshape(B, L, R_HEADS, R_DK), pos) * (R_DK ** -0.5)
    rv = rv.reshape(B, L, R_HEADS, R_DV)
    if s0 is None:
        s0 = jnp.zeros((B, R_HEADS, R_DK, R_DV), jnp.float32)
    ob, s_new = retention(rq, rk, rv, s0)
    ob = head_norm(ob, ret_norm_g).astype(x.dtype) * jax.nn.silu(rg)

    cu = jax.nn.gelu(cu)
    cv = layernorm(jax.nn.gelu(cv), gm_ln_g, gm_ln_b)
    oc = chunk_gmlp(cu, cv, gm_ws, gm_bs)

    ga, gb, gc = jnp.split(jax.nn.sigmoid(mg + b_gate), 3, axis=-1)
    x = x + g1 * ((ga * oa + gb * ob + gc * oc) @ w_out)

    h2 = rmsnorm(x, ln_ffn_g) * (1.0 + sc2) + sh2
    f = moe(h2.reshape(B * L, D), router_w, router_b, moe_w1, moe_b1, moe_w2, moe_b2).reshape(B, L, D)
    x = x + g2 * f
    return x, new_k, new_v, s_new.astype(x.dtype), cv

def setup_inputs(seed: int = 0) -> dict:
    key = jax.random.key(seed)
    ks = iter(jax.random.split(key, 40))

    def nrm(shape, scale):
        return jax.random.normal(next(ks), shape, jnp.float32) * scale

    D = D_MODEL
    w_buf = min(WINDOW, PAST_LEN)
    d_in = sum(IN_SPLITS)
    return {
        'x_prompt': nrm((BATCH, SEQ, D), 1.0),
        'x_sample': nrm((DEC_BATCH, DEC_SEQ, D), 1.0),
        'c_prompt': nrm((BATCH, D), 1.0),
        'c_sample': nrm((DEC_BATCH, D), 1.0),
        'cache_attn_k': nrm((DEPTH, DEC_BATCH, w_buf, A_KV_HEADS, HEAD_DIM), 1.0),
        'cache_attn_v': nrm((DEPTH, DEC_BATCH, w_buf, A_KV_HEADS, HEAD_DIM), 1.0),
        'state_retention': nrm((DEPTH, DEC_BATCH, R_HEADS, R_DK, R_DV), 0.5),
        'ln_mix_g': 1.0 + nrm((DEPTH, D), 0.02),
        'ln_ffn_g': 1.0 + nrm((DEPTH, D), 0.02),
        'w_ada': nrm((DEPTH, D, 6 * D), 0.5 * D ** -0.5),
        'b_ada': nrm((DEPTH, 6 * D), 0.02),
        'w_in': nrm((DEPTH, D, d_in), D ** -0.5),
        'b_gate': nrm((DEPTH, 3 * D), 0.1),
        'q_norm_g': 1.0 + nrm((DEPTH, HEAD_DIM), 0.02),
        'k_norm_g': 1.0 + nrm((DEPTH, HEAD_DIM), 0.02),
        'attn_sinks': nrm((DEPTH, A_Q_HEADS), 0.5),
        'ret_norm_g': 1.0 + nrm((DEPTH, D), 0.02),
        'gm_ln_g': 1.0 + nrm((DEPTH, D), 0.02),
        'gm_ln_b': nrm((DEPTH, D), 0.02),
        'gm_ws': nrm((DEPTH, C_GROUPS, C_CHUNK, C_CHUNK), C_CHUNK ** -0.5),
        'gm_bs': 1.0 + nrm((DEPTH, C_GROUPS, C_CHUNK), 0.02),
        'w_out': nrm((DEPTH, D, D), D ** -0.5),
        'router_w': nrm((DEPTH, D, N_EXPERTS), D ** -0.5),
        'router_b': nrm((DEPTH, N_EXPERTS), 0.01),
        'moe_w1': nrm((DEPTH, N_EXPERTS, D, 2 * D_FF), D ** -0.5),
        'moe_b1': nrm((DEPTH, N_EXPERTS, 2 * D_FF), 0.01),
        'moe_w2': nrm((DEPTH, N_EXPERTS, D_FF, D), D_FF ** -0.5),
        'moe_b2': nrm((DEPTH, N_EXPERTS, D), 0.01),
    }

def reference(x_prompt, x_sample, c_prompt, c_sample, cache_attn_k, cache_attn_v, state_retention,
              ln_mix_g, ln_ffn_g, w_ada, b_ada, w_in, b_gate, q_norm_g, k_norm_g, attn_sinks,
              ret_norm_g, gm_ln_g, gm_ln_b, gm_ws, gm_bs, w_out, router_w, router_b,
              moe_w1, moe_b1, moe_w2, moe_b2):
    xp, xs = x_prompt, x_sample
    pk, pv, ps, sk, sv, ss, sg = [], [], [], [], [], [], []
    for l in range(DEPTH):
        lw = (ln_mix_g[l], ln_ffn_g[l], w_ada[l], b_ada[l], w_in[l], b_gate[l], q_norm_g[l], k_norm_g[l],
              attn_sinks[l], ret_norm_g[l], gm_ln_g[l], gm_ln_b[l], gm_ws[l], gm_bs[l], w_out[l],
              router_w[l], router_b[l], moe_w1[l], moe_b1[l], moe_w2[l], moe_b2[l])
        xp, k_p, v_p, s_p, _ = block(xp, c_prompt, 0, None, None, None, *lw)
        xs, k_s, v_s, s_s, g_s = block(xs, c_sample, PAST_LEN, cache_attn_k[l], cache_attn_v[l],
                                       state_retention[l], *lw)
        pk.append(k_p)
        pv.append(v_p)
        ps.append(s_p)
        sk.append(k_s)
        sv.append(v_s)
        ss.append(s_s)
        sg.append(g_s)
    return (xp, xs, jnp.stack(pk), jnp.stack(pv), jnp.stack(ps), jnp.stack(sk), jnp.stack(sv), jnp.stack(ss), jnp.stack(sg))


_drawn_inputs = setup_inputs


def setup_inputs(seed=0):
    import zlib

    import numpy as np

    out = dict(_drawn_inputs(seed))
    spreads = {}
    factors = {'cache_attn_k': 2.859,
     'ln_ffn_g': 3.441,
     'b_gate': 4.664,
     'q_norm_g': 21.714,
     'k_norm_g': 8.02,
     'attn_sinks': 200.0,
     'ret_norm_g': 7.629,
     'gm_ln_g': 24.006,
     'gm_ln_b': 24.16,
     'gm_bs': 8.0,
     'router_b': 7.165,
     'moe_b1': 8.0,
     'moe_b2': 64.0}
    for name, (base, spread) in spreads.items():
        noise = np.random.default_rng([zlib.crc32(name.encode()), seed]).standard_normal(out[name].shape)
        drawn = base * np.exp(spread * noise) if base else spread * noise
        out[name] = jnp.asarray(drawn.astype(out[name].dtype))
    for name, factor in factors.items():
        out[name] = (out[name] * factor).astype(out[name].dtype)
    return out
```

```python
import numpy as np
import concourse.bass as bass
from concourse import mybir
from concourse.alu_op_type import AluOpType as ALU

ACT = mybir.ActivationFunctionType
AX = mybir.AxisListType
FP32 = mybir.dt.float32
I32 = mybir.dt.int32
U32 = mybir.dt.uint32

P = 128
D = 1024
KD = D // P
HALF = 512
BATCH_S, STEPS = 8, 8
SEQ = 256
TOKENS = SEQ + BATCH_S * STEPS
ROWS = [P, P, TOKENS - 2 * P]
HD, QH, KVH = 64, 16, 4
GROUP = QH // KVH
RH, RDK, RDV = 8, 64, 128
GG = 8
NEXP, TOPK = 32, 4
LIMIT = 7.0
PAST = 1024
EPS = 1e-6
MASKED = -1e30

SLOTS = 6
ADA_UNITS, IN_UNITS, OUT_UNITS = 12, 19, 2
FIRST_OUT = ADA_UNITS + IN_UNITS
DENSE_UNITS = FIRST_OUT + OUT_UNITS
EXPERT_UNITS = 6
CU0, CU1, CV0, CV1, RQ, RK, RV0, RV1, GC0, GC1, RG0, RG1, GB0, GB1, AQ0, AQ1, AKV, GA0, GA1 = range(IN_UNITS)
IN_ORDER = [9, 10, 11, 12, 3, 4, 5, 6, 17, 18, 7, 8, 15, 16, 0, 1, 2, 13, 14]

BLOCK = 64
MAX_BLOCKS = 64

CONST_WIDTHS = [("ident", 128), ("causal", 128), ("blockcausal", 64), ("select", 4 * 192),
                ("cos", 3 * 32), ("sin", 3 * 32), ("decay", 3 * 16), ("chunk_decay", 16),
                ("iota", 64), ("window", 256), ("cache_mask", 128), ("new_mask", 8 * 64),
                ("before", 128), ("ones", 128), ("of_batch", 8)]
CONST_AT = {}
CONST_COLS = 0
for _name, _width in CONST_WIDTHS:
    CONST_AT[_name] = (CONST_COLS, CONST_COLS + _width)
    CONST_COLS += _width

PARAM_WIDTHS = [("k_gain", 256), ("sinks", 16), ("sink_rows", 1), ("q_gain", 1), ("router_b", 32),
                ("mix_bias", 8), ("mix_bias_s", 8)]
PARAM_AT = {}
PARAM_COLS = 0
for _name, _width in PARAM_WIDTHS:
    PARAM_AT[_name] = (PARAM_COLS, PARAM_COLS + _width)
    PARAM_COLS += _width

AUX_FIRST, AUX_BANKS = 5, 3
AUX = [f"mix{t}{h}" for t in range(3) for h in range(2)]
for _t in range(2):
    for _h in range(2):
        AUX += [f"rqT{_t}{_h}", f"rkT{_t}{_h}", f"ra{_t}{_h}", f"ro{_t}{_h}"]
    AUX += [f"rs{_t}{_h}" for _h in range(2)]
AUX += ["rqT2", "rkT2", "ra2", "ro2"]
AUX += [f"rs2{b}{h}" for b in range(BATCH_S) for h in range(2)]
AUX += ["rback0", "rback1"]
AUX += [f"kT{_t}" for _t in range(3)]
for _t in range(2):
    AUX += [f"qT{_t}{q}" for q in range(4)]
    for _g in range(KVH):
        AUX += [f"sc{_t}{_g}{k}" for k in range(_t + 1)] + [f"pT{_t}{_g}{k}" for k in range(_t + 1)] + [f"pv{_t}{_g}"]
AUX += ["qT20", "qT21"]
for _b in range(BATCH_S):
    AUX += [f"sc2{_b}", f"pT2{_b}", f"pv2{_b}"]
AUX += ["oback0", "oback1"]
AUX += [f"g1{s}{h}" for s in "ps" for h in range(2)]
AUX += [f"g2{s}{h}" for s in "ps" for h in range(2)]
AUX += ["lg0", "lg1", "lg2", "pos0", "pos1", "pos2", "cnt", "gT", "b2a0", "b2a1", "b2b0", "b2b1", "b2c0", "b2c1"]
AUX_AT = {name: n for n, name in enumerate(AUX)}


def hybrid_step_kernel(nc, ins, outs):
    from contextlib import ExitStack
    with ExitStack() as ctx:
        build(nc, ctx, ins, outs)


def build(nc, ctx, ins, outs):
    def sb(name, shape, dt=FP32):
        return ctx.enter_context(nc.sbuf_tensor(name, shape, dt))

    def sem(name):
        return ctx.enter_context(nc.semaphore(name))

    ring = sb("ring", [P, SLOTS, 4096])
    xT = sb("xT", [P, KD, TOKENS])
    U = sb("U", [P, 3, D])
    V = sb("V", [P, 3, D])
    R = sb("R", [P, 3, D])
    W = sb("W", [P, 3, D])
    T = sb("T", [P, 3, D])
    mod = sb("mod", [P, ADA_UNITS, 128])
    consts = sb("consts", [P, CONST_COLS])
    params = sb("params", [P, PARAM_COLS])
    stat = sb("stat", [P, 96])
    ARENA = 5888
    arena = sb("arena", [P, ARENA])
    table_i = sb("table_i", [1, MAX_BLOCKS + 1 + NEXP], I32)
    top_i = sb("top_i", [P, 8], U32)
    ps = ctx.enter_context(nc.psum_tensor("ps", [P, 8, HALF], FP32))

    def const(name):
        a, b = CONST_AT[name]
        return consts[:, a:b]

    def param(name):
        a, b = PARAM_AT[name]
        return params[:, a:b]

    ident = const("ident")
    select = const("select").rearrange("p (j m) -> p j m", j=4)
    cos = const("cos").rearrange("p (t f) -> p t f", t=3)
    sin = const("sin").rearrange("p (t f) -> p t f", t=3)
    decay = const("decay").rearrange("p (t h) -> p t h", t=3)
    new_mask = const("new_mask").rearrange("p (b k) -> p b k", b=BATCH_S)
    ones = const("ones")

    def cut(at, *shape):
        size = int(np.prod(shape))
        assert at + size <= ARENA, (at, size)
        v = arena[:, at:at + size]
        if len(shape) == 2:
            v = v.rearrange("p (a b) -> p a b", a=shape[0])
        if len(shape) == 3:
            v = v.rearrange("p (a b c) -> p a b c", a=shape[0], b=shape[1])
        return v

    silu_c = cut(0, KD, 32)
    mod_bias = cut(256, ADA_UNITS, 128)
    ln_gain = cut(1792, D)
    ln_ffn = cut(4096, D)
    gm_gain = cut(0, D)
    gm_bias = cut(1024, D)
    mixT = cut(2048, GG, 128)
    mixT_s = cut(3072, GG, 64)
    mix_tmp = cut(3584, D)
    gate_bias = cut(4608, D)
    rqT = cut(0, RH, 128)
    rkT = cut(1024, RH, 128)
    ra = cut(2048, 2, HALF)
    state = cut(3072, RH, RDV)
    kd = cut(4096, HALF)
    ro_s = cut(4608, HALF)
    ret_gain = cut(0, D)
    squares = cut(1024, D)
    kTa = cut(0, KVH, TOKENS)
    probs = cut(1280, 4, 256)
    pT = cut(2304, 2, HALF)
    oT = cut(3328, QH, BATCH_S * STEPS)
    cache = cut(4352, 2, 768)
    qTa = xT[:, :, :].rearrange("p k t -> p (k t)")[:, 0:QH * P].rearrange("p (h t) -> p h t", h=QH)
    qTs = xT[:, :, :].rearrange("p k t -> p (k t)")[:, 0:QH * 64].rearrange("p (b h t) -> p b h t", b=BATCH_S, h=QH)
    router_w = cut(0, KD, NEXP)
    select_e = cut(256, 3, NEXP)
    gate_e = cut(352, 3, NEXP)
    slot_of = cut(448, 3, NEXP)
    rtmp = cut(544, 3, NEXP)
    slot_base = cut(640, MAX_BLOCKS)
    expert_of = cut(704, MAX_BLOCKS)
    n_of = cut(768, NEXP)
    cum_of = cut(800, NEXP)
    pick = cut(832, 3, BLOCK)
    pick_gate = cut(1024, 3, 2, BLOCK)
    sel_now = cut(1408, 2, 3)
    xgT = cut(1536, 4, 2, BLOCK)
    actT = cut(2048, 4, 2, BLOCK)
    gateT = cut(2560, 3 * P)
    y_blk = cut(2944, HALF)
    g_cut = cut(3456, HALF)
    g_act = cut(3968, HALF)
    u_cut = cut(4480, HALF)
    h_act = cut(4992, HALF)
    b1_rows = W[:, 0, :]
    passed = W[:, 0:2, :].rearrange("p a (g e) -> p (a g) e", e=NEXP)
    b2_sb = W[:, 2, :]
    xg_s = W[:, 2, 0:HALF]
    gates_T = xT[0:NEXP, 0, :]

    unit_in = [sem(f"unit_in{s}") for s in range(SLOTS)]
    unit_used = sem("unit_used")
    c_in, x_in, consts_in, params_in, mod_bias_in, ln_mix_in = map(sem, (
        "c_in", "x_in", "consts_in", "params_in", "mod_bias_in", "ln_mix_in"))
    gm_in, gate_bias_in, ret_gain_in, ln_ffn_in, x_again_in, router_in, b2_in = map(sem, (
        "gm_in", "gate_bias_in", "ret_gain_in", "ln_ffn_in", "x_again_in", "router_in", "b2_in"))
    state_in = [sem(f"state_in{i}") for i in range(2)]
    cache_in = [sem(f"cache_in{i}") for i in range(2)]
    b1_in = [sem(f"b1_in{i}") for i in range(2)]
    stored, kv_stored, gmlp_stored, retention_stored, stat_clean, inter_ready, scaled = map(sem, ("stored", "kv_stored", "gmlp_stored", "retention_stored", "stat_clean", "inter_ready", "scaled"))
    silu_done, mod_ready, bcast_ready, squared, mean_sq, sqrt_done = map(sem, (
        "silu_done", "mod_ready", "bcast_ready", "squared", "mean_sq", "sqrt_done"))
    h_ready, tr_ready, xT_ready, z_ready, z_used = map(sem, ("h_ready", "tr_ready", "xT_ready", "z_ready", "z_used"))
    aux_ready = sem("aux_ready")
    aux_used = [sem(f"aux_used{i}") for i in range(AUX_BANKS)]
    dve_step, pool_step, act_step = sem("dve_step"), sem("pool_step"), sem("act_step")
    var_ready, cv_ready, mixw_ready, gmlp_done, gate_biased, gate_ready = map(sem, (
        "var_ready", "cv_ready", "mixw_ready", "gmlp_done", "gate_biased", "gate_ready"))
    branch_merged, roped, scores_masked, state_ready, kd_ready, inter_added, head_centred, head_squared, silu_scaled, new_state = map(sem, (
        "branch_merged", "roped", "scores_masked", "state_ready", "kd_ready", "inter_added", "head_centred", "head_squared", "silu_scaled", "new_state"))
    state_stored = sem("state_stored")
    ret_scaled, qk_normed, max_ready, exp_done, probs_ready, v_free = map(sem, (
        "ret_scaled", "qk_normed", "max_ready", "exp_done", "probs_ready", "v_free"))
    x1_ready, top_ready, top_exp, routed, table_ready, moe_init = map(sem, (
        "x1_ready", "top_ready", "top_exp", "routed", "table_ready", "moe_init"))
    (picked, gates_picked, gathered, xg_ready, g_ready, g_cut_ready, g_act_ready, u_ready, act_ready, actT_done,
     actT_ready, gateT_done, gateT_ready, y_done, y_ready, added, final_ready, moe_step) = map(sem, (
        "picked", "gates_picked", "gathered", "xg_ready", "g_ready", "g_cut_ready", "g_act_ready", "u_ready",
        "act_ready", "actT_done", "actT_ready", "gateT_done", "gateT_ready", "y_done", "y_ready", "added",
        "final_ready", "moe_step"))
    scattered, xg_rows, turned = sem("scattered"), sem("xg_rows"), sem("turned")

    block = ctx.enter_context(nc.Block())

    def aux_bank(name):
        return ps[:, AUX_FIRST + AUX_AT[name] % AUX_BANKS, :]

    def aux_filled(eng, name):
        eng.wait_ge(aux_ready, AUX_AT[name] + 1)

    def aux_taken(eng, name):
        n = AUX_AT[name]
        eng.wait_ge(aux_used[n % AUX_BANKS], n // AUX_BANKS + 1)

    def used(name):
        return aux_used[AUX_AT[name] % AUX_BANKS]

    def unit_arrived(eng, u):
        eng.wait_ge(unit_in[u % SLOTS], 16 * (u // SLOTS + 1))

    def z_banks(idx):
        s = idx % 2
        return [(ps[:, s, :], 0, 0, HALF), (ps[:, 2 + s, :], 1, 0, HALF),
                (ps[0:64, 4, 0:256], 2, 0, 256), (ps[64:128, 4, 0:256], 2, 256, 256)]

    TR_BANKS = [4, 5, 6, 7, 4]
    TR_PARTS = [(2, 0, 8), (0, 0, 4), (0, 4, 4), (1, 0, 4), (1, 4, 4)]

    @block.sync
    def _(sp):
        def load_unit(u):
            if ADA_UNITS > u - SLOTS >= 0:
                sp.wait_ge(unit_used, u - SLOTS + 1)
            elif u >= SLOTS:
                sp.wait_ge(z_ready, 3 * (u - SLOTS - ADA_UNITS + 1))
            sp.dma_start(ring[:, u % SLOTS, :], ins["w_dense"][u, :, :]).then_inc(unit_in[u % SLOTS], 16)

        sp.dma_start(silu_c, ins["c"]).then_inc(c_in, 16)
        for u in range(2):
            load_unit(u)
        sp.dma_start(R[:, 0:2, :], ins["x_prompt"].rearrange("(t p) d -> p t d", p=P)).then_inc(x_in, 16)
        sp.dma_start(R[0:64, 2, :], ins["x_sample"]).then_inc(x_in, 16)
        sp.dma_start(consts[:, :], ins["consts"]).then_inc(consts_in, 16)
        for u in range(2, DENSE_UNITS):
            load_unit(u)

        for j in range(EXPERT_UNITS):
            slot = (DENSE_UNITS + j) % SLOTS
            sp.wait_ge(z_ready, 3 * (DENSE_UNITS + j - SLOTS - ADA_UNITS + 1))
            sp.dma_start(ring[:, slot, :], ins["w_moe"][0, j, :, :]).then_inc(unit_in[slot], 16)
        sp.wait_ge(table_ready, 1)
        for n in range(2):
            sp.dma_start(W[0:1, n, :], ins["b1"][0:1, n, :]).then_inc(b1_in[n], 16)
        with sp.Fori(1, NEXP) as e:
            before = sp.value_load(table_i[0:1, bass.ds(MAX_BLOCKS + 1 + e, 1)], min_val=1, max_val=MAX_BLOCKS)
            for j in range(EXPERT_UNITS):
                slot = (DENSE_UNITS + j) % SLOTS
                sp.wait_ge(unit_used, EXPERT_UNITS * before + (ADA_UNITS - EXPERT_UNITS + 1 + j))
                sp.dma_start(ring[:, slot, :], ins["w_moe"][bass.ds(e, 1), j, :, :].rearrange("a p n -> p (a n)")).then_inc(unit_in[slot], 16)
                if j in (1, 3):
                    sp.dma_start(W[0:1, j // 2, :], ins["b1"][bass.ds(e, 1), j // 2, :]).then_inc(b1_in[j // 2], 16)
        sp.wait_ge(final_ready, 3)
        sp.dma_start(outs["y_prompt"].rearrange("(t p) d -> p t d", p=P), R[:, 0:2, :]).then_inc(stored, 16)
        sp.dma_start(outs["y_sample"], R[0:64, 2, :]).then_inc(stored, 16)
        sp.wait_ge(stored, 32)
        sp.wait_ge(kv_stored, 64)
        sp.wait_ge(gmlp_stored, 16)
        sp.wait_ge(retention_stored, 16)
        sp.wait_ge(state_stored, 16 * BATCH_S)


    @block.gpsimd
    def _(pool):
        pool.dma_start(params[:, :], ins["params"]).then_inc(params_in, 16)
        bias_v = ins["b_ada"].rearrange("(n j c) -> j n c", j=4, c=128)
        for j in range(4):
            pool.dma_start(mod_bias[32 * j:32 * j + 32, :, :], bias_v[j].partition_broadcast(32)).then_inc(mod_bias_in, 16)
        pool.dma_start(ln_gain, ins["ln_mix_g"].partition_broadcast(P)).then_inc(ln_mix_in, 16)
        pool.wait_ge(h_ready, 3)
        pool.dma_start(gm_gain, ins["gm_ln_g"].partition_broadcast(P)).then_inc(gm_in, 16)
        pool.dma_start(gm_bias, ins["gm_ln_b"].partition_broadcast(P)).then_inc(gm_in, 16)
        pool.dma_start(mixT, ins["mixT"]).then_inc(gm_in, 16)
        pool.dma_start(mixT_s[0:64], ins["mixT_s"]).then_inc(gm_in, 16)
        pool.dma_start(gate_bias, ins["b_gate"][2].partition_broadcast(P)).then_inc(gate_bias_in, 16)
        pool.wait_ge(gm_in, 64)
        pool.wait_ge(consts_in, 16)
        nc.gpsimd.tensor_tensor(mixT, mixT, const("causal").unsqueeze(1).to_broadcast([P, GG, 128]), ALU.mult).then_inc(mixw_ready, 1)
        nc.gpsimd.tensor_tensor(mixT_s[0:64], mixT_s[0:64], const("blockcausal")[0:64].unsqueeze(1).to_broadcast([64, GG, 64]), ALU.mult).then_inc(mixw_ready, 1)

        def add_gate_bias(buf, first, n):
            pool.wait_ge(gate_bias_in, 16 * (n + 1))
            pool.wait_ge(z_used, 4 * (first + 2))
            for t, r in enumerate(ROWS):
                nc.gpsimd.tensor_tensor(buf[0:r, t, :], buf[0:r, t, :], gate_bias[0:r], ALU.add).then_inc(gate_biased, 1)

        pool.wait_ge(cv_ready, 3)
        pool.dma_start(outs["sample_gmlp_v"], V[0:64, 2, :]).then_inc(gmlp_stored, 16)
        add_gate_bias(V, GC0, 0)
        pool.wait_ge(branch_merged, 3)
        for b in range(BATCH_S):
            if b >= 2:
                pool.wait_ge(new_state, 2 * (b - 1))
            pool.dma_start(V[0:64, b % 2, :].rearrange("p (h e) -> p h e", h=RH),
                           ins["state"][b].rearrange("h d e -> d h e")).then_inc(state_in[b % 2], 16)
            if b == 0:
                pool.wait_ge(roped, 3)
            if b >= 1:
                aux_filled(pool, f"rs2{b - 1}1")
            nc.gpsimd.tensor_scalar(kd[0:64], R[0:64, 2, HALF:D], const("of_batch")[0:64, b:b + 1], None, ALU.mult).then_inc(kd_ready, 1)
            if b >= 1:
                pool.wait_ge(new_state, 2 * b)
                pool.dma_start(outs["sample_retention"][b - 1].rearrange("h d e -> d h e"),
                               V[0:64, 2, :].rearrange("p (h e) -> p h e", h=RH)).then_inc(state_stored, 16)
        pool.wait_ge(new_state, 2 * BATCH_S)
        pool.dma_start(outs["sample_retention"][BATCH_S - 1].rearrange("h d e -> d h e"),
                       V[0:64, 2, :].rearrange("p (h e) -> p h e", h=RH)).then_inc(state_stored, 16)
        pool.dma_start(outs["prompt_retention"].rearrange("h d e -> d h e"), state[0:64]).then_inc(retention_stored, 16)
        pool.dma_start(ret_gain, ins["ret_norm_g"].partition_broadcast(P)).then_inc(ret_gain_in, 16)
        pool.wait_ge(state_stored, 16 * BATCH_S)
        pool.sem_inc(v_free, 1)
        aux_taken(pool, "rback1")
        pool.dma_start(gate_bias[:, :], ins["b_gate"][1].partition_broadcast(P)).then_inc(gate_bias_in, 16)
        pool.wait_ge(z_used, 4 * (RG0 + 2))
        pool.wait_ge(ret_gain_in, 16)
        for t, r in enumerate(ROWS):
            nc.gpsimd.tensor_tensor(V[0:r, t, :], V[0:r, t, :], ret_gain[0:r], ALU.mult).then_inc(silu_scaled, 1)
        add_gate_bias(W, GB0, 1)
        pool.wait_ge(gate_biased, 6)
        pool.wait_ge(branch_merged, 6)
        pool.dma_start(T[:, 0, :], ins["b_gate"][0].partition_broadcast(P)).then_inc(gate_bias_in, 16)

        def load_cache(b):
            pool.dma_start(cache[0:64, b % 2, 0:512].rearrange("p (h r) -> p h r", h=KVH), ins["cache_kT"][b]).then_inc(cache_in[b % 2], 16)
            pool.dma_start(cache[:, b % 2, 512:768], ins["cache_v"][b]).then_inc(cache_in[b % 2], 16)

        for b in range(2):
            load_cache(b)
        pool.wait_ge(gate_bias_in, 48)
        pool.wait_ge(z_used, 4 * (GA1 + 1))
        for t, r in enumerate(ROWS):
            nc.gpsimd.tensor_tensor(W[0:r, t, :], W[0:r, t, :], T[0:r, 0, :], ALU.add).then_inc(gate_biased, 1)
        pool.wait_ge(qk_normed, 3)
        pool.dma_start(outs["prompt_k"], V[:, 1, 0:256]).then_inc(kv_stored, 16)
        pool.dma_start(outs["prompt_v"], V[:, 1, 256:512]).then_inc(kv_stored, 16)
        pool.dma_start(outs["sample_k"], V[0:64, 2, 0:256]).then_inc(kv_stored, 16)
        pool.dma_start(outs["sample_v"], V[0:64, 2, 256:512]).then_inc(kv_stored, 16)
        for b in range(2, BATCH_S):
            aux_taken(pool, f"pv2{b - 2}")
            load_cache(b)
        aux_taken(pool, "oback1")
        pool.dma_start(R[:, 0:2, :], ins["x_prompt"].rearrange("(t p) d -> p t d", p=P)).then_inc(x_again_in, 16)
        pool.dma_start(R[0:64, 2, :], ins["x_sample"]).then_inc(x_again_in, 16)
        pool.dma_start(ln_ffn, ins["ln_ffn_g"].partition_broadcast(P)).then_inc(ln_ffn_in, 16)
        pool.dma_start(router_w, ins["router_w"]).then_inc(router_in, 16)
        pool.wait_ge(h_ready, 6)
        pool.dma_start(b2_sb[0:NEXP], ins["b2"]).then_inc(b2_in, 16)

    @block.scalar
    def _(act):
        A = nc.scalar.activation

        def sqrt_of(cols, n, r=P):
            act.wait_ge(mean_sq, n)
            A(cols, cols, ACT.Sqrt).then_inc(sqrt_done, 1)

        def take_transposed(n):
            for q, (t, k0, nk) in enumerate(TR_PARTS):
                act.wait_ge(tr_ready, 5 * n + q + 1)
                r = ROWS[t]
                A(xT[:, k0:k0 + nk, t * P:t * P + r], ps[:, TR_BANKS[q], :].rearrange("p (k m) -> p k m", m=r), ACT.Copy).then_inc(xT_ready, 1)

        def take_z(idx, buf, c0, func):
            for n, (src, t, c, w) in enumerate(z_banks(idx)):
                act.wait_ge(z_ready, 3 * idx + min(n, 2) + 1)
                A(buf[0:ROWS[t], t, c0 + c:c0 + c + w], src, func).then_inc(z_used, 1)

        def gate(buf, n):
            for t, r in enumerate(ROWS):
                act.wait_ge(gate_biased, 3 * n + t + 1)
                A(buf[0:r, t, :], buf[0:r, t, :], ACT.Sigmoid).then_inc(gate_ready, 1)

        act.wait_ge(c_in, 16)
        A(silu_c, silu_c, ACT.Silu).then_inc(silu_done, 1)
        act.wait_ge(x_in, 32)
        act.wait_ge(stat_clean, 1)
        for t in (2, 0, 1):
            A(W[0:ROWS[t], t, :], R[0:ROWS[t], t, :], ACT.Square, accum_out=stat[0:ROWS[t], t:t + 1]).then_inc(squared, 1)
        sqrt_of(stat[:, 0:3], 1)
        take_transposed(0)
        for h in range(2):
            take_z(CU0 + h, U, HALF * h, ACT.Gelu_apprx_tanh)
        for h in range(2):
            take_z(CV0 + h, V, HALF * h, ACT.Gelu_apprx_tanh)
        sqrt_of(stat[:, 8:11], 2)
        take_z(RQ, R, 0, ACT.Copy)
        take_z(RK, R, HALF, ACT.Copy)
        act.wait_ge(h_ready, 3)
        for h in range(2):
            take_z(RV0 + h, W, HALF * h, ACT.Copy)
        aux_filled(act, "mix21")
        act.wait_ge(gmlp_stored, 16)
        for h in range(2):
            take_z(GC0 + h, V, HALF * h, ACT.Copy)
        gate(V, 0)
        for t in range(2):
            for h in range(2):
                for src, dst in (("rqT", rqT), ("rkT", rkT)):
                    name = f"{src}{t}{h}"
                    aux_filled(act, name)
                    A(dst[0:64, 4 * h:4 * h + 4, :], aux_bank(name)[0:64].rearrange("p (h m) -> p h m", h=4), ACT.Copy).then_inc(used(name), 1)
                name = f"ro{t}{h}"
                aux_filled(act, name)
                A(T[:, t, HALF * h:HALF * h + HALF], aux_bank(name), ACT.Copy).then_inc(used(name), 1)
        for name, dst in (("rqT2", rqT), ("rkT2", rkT)):
            aux_filled(act, name)
            A(dst[0:64, :, 0:64], aux_bank(name)[0:64].rearrange("p (h m) -> p h m", h=8), ACT.Copy).then_inc(used(name), 1)
        aux_filled(act, "ro2")
        A(ro_s, aux_bank("ro2"), ACT.Copy).then_inc(used("ro2"), 1)
        for h in range(2):
            name = f"rback{h}"
            aux_filled(act, name)
            A(T[0:64, 2, HALF * h:HALF * h + HALF], aux_bank(name)[0:64], ACT.Copy).then_inc(used(name), 1)
        act.wait_ge(v_free, 1)
        for h in range(2):
            take_z(RG0 + h, V, HALF * h, ACT.Silu)
        for h in range(2):
            take_z(GB0 + h, W, HALF * h, ACT.Copy)
        gate(W, 1)
        for t, r in enumerate(ROWS):
            act.wait_ge(head_centred, t + 1)
            if t:
                act.wait_ge(mean_sq, 2 + t)
            A(squares[0:r], T[0:r, t, :], ACT.Square).then_inc(head_squared, 1)
            sqrt_of(stat[:, 16:24], 3 + t)
        for h in range(2):
            take_z(AQ0 + h, R, HALF * h, ACT.Copy)
        act.wait_ge(ret_scaled, 3)
        take_z(AKV, V, 0, ACT.Copy)
        act.wait_ge(branch_merged, 6)
        for h in range(2):
            take_z(GA0 + h, W, HALF * h, ACT.Copy)
        gate(W, 2)
        for t in range(3):
            sqrt_of(stat[:, 24:44], 6 + t)

        def take_kT(t):
            name = f"kT{t}"
            aux_filled(act, name)
            A(kTa[0:64, :, t * P:t * P + ROWS[t]], aux_bank(name)[0:64, 0:4 * ROWS[t]].rearrange("p (h m) -> p h m", h=4), ACT.Copy).then_inc(used(name), 1)

        def take_qT(t):
            n = 2 if t == 2 else 4
            for q in range(n):
                name = f"qT{t}{q}"
                aux_filled(act, name)
                heads = slice(q * (QH // n), (q + 1) * (QH // n))
                if t == 2:
                    dst = qTs[0:64].rearrange("p b h t -> p h b t")[:, heads]
                    src = aux_bank(name)[0:64].rearrange("p (h b t) -> p h b t", b=BATCH_S, t=STEPS)
                else:
                    dst = qTa[0:64, heads, :]
                    src = aux_bank(name)[0:64].rearrange("p (h m) -> p h m", m=P)
                A(dst, src, ACT.Copy, scale=param("q_gain")[0:64]).then_inc(used(name), 1)

        softmaxes = [0]

        def softmax(count, width, sink):
            softmaxes[0] += 1
            act.wait_ge(max_ready, softmaxes[0])
            for h in range(count):
                A(probs[:, h, 0:width], probs[:, h, 0:width], ACT.Exp, bias=stat[:, 48 + h:49 + h], accum_out=stat[:, 52 + h:53 + h])
            A(stat[:, 56:56 + count], stat[:, 60:60 + count], ACT.Exp).then_inc(exp_done, 1)

        for t in range(3):
            take_kT(t)
        for t in range(2):
            take_qT(t)
            for g in range(KVH):
                softmax(4, P * (t + 1), None)
                for k in range(t + 1):
                    name = f"pT{t}{g}{k}"
                    aux_filled(act, name)
                    A(pT[:, k, :], aux_bank(name), ACT.Copy).then_inc(used(name), 1)
        take_qT(2)
        for b in range(BATCH_S):
            softmax(1, 192, None)
            name = f"pT2{b}"
            aux_filled(act, name)
            A(pT[0:64, 1, 0:P], aux_bank(name)[0:64, P:2 * P], ACT.Copy)
            A(pT[:, 0, 0:P], aux_bank(name)[:, 0:P], ACT.Copy).then_inc(used(name), 1)
            name = f"pv2{b}"
            aux_filled(act, name)
            A(oT[0:64, :, b * STEPS:(b + 1) * STEPS], aux_bank(name)[0:64, 0:P].rearrange("p (h t) -> p h t", h=QH), ACT.Copy).then_inc(used(name), 1)
        for h in range(2):
            name = f"oback{h}"
            aux_filled(act, name)
            A(T[0:64, 2, HALF * h:HALF * h + HALF], aux_bank(name)[0:64], ACT.Copy).then_inc(used(name), 1)
        take_transposed(1)
        for s, rows, t in (("p", P, 0), ("s", 64, 2)):
            for h in range(2):
                name = f"g1{s}{h}"
                aux_filled(act, name)
                A(V[0:rows, t, HALF * h:HALF * h + HALF], aux_bank(name)[0:rows], ACT.Copy).then_inc(used(name), 1)
        for h in range(2):
            take_z(IN_UNITS + h, W, HALF * h, ACT.Copy)
        for t in (2, 0, 1):
            act.wait_ge(x1_ready, {2: 1, 0: 2, 1: 3}[t])
            A(W[0:ROWS[t], t, :], R[0:ROWS[t], t, :], ACT.Square, accum_out=stat[0:ROWS[t], t:t + 1]).then_inc(squared, 1)
        sqrt_of(stat[:, 0:3], 9)
        take_transposed(2)
        for s, rows, t in (("p", P, 0), ("s", 64, 2)):
            for h in range(2):
                name = f"g2{s}{h}"
                aux_filled(act, name)
                A(V[0:rows, t, HALF * h:HALF * h + HALF], aux_bank(name)[0:rows], ACT.Copy).then_inc(used(name), 1)
        for t in range(3):
            act.wait_ge(top_ready, t + 1)
            A(stat[:, 72:76], stat[:, 64:68], ACT.Exp, bias=stat[:, 76:77], accum_out=stat[:, 77:78]).then_inc(top_exp, 1)
        aux_filled(act, "gT")
        A(gates_T[:, 0:TOKENS], aux_bank("gT")[0:NEXP, 0:TOKENS], ACT.Copy).then_inc(used("gT"), 1)
        for t, r in enumerate(ROWS):
            for h in range(2):
                name = f"b2{'abc'[t]}{h}"
                aux_filled(act, name)
                A(U[0:r, t, HALF * h:HALF * h + HALF], aux_bank(name)[0:r], ACT.Copy).then_inc(used(name), 1)

        def take_gathered(i):
            act.wait_ge(gathered, i)
            A(xg_s, ps[:, 3, :], ACT.Copy).then_inc(xg_rows, 1)

        def take_turned(i):
            act.wait_ge(turned, i)
            A(xgT, ps[:, 3, :].rearrange("p (c a s) -> p c a s", c=4, a=2), ACT.Copy).then_inc(xg_ready, 1)

        take_gathered(1)
        take_turned(1)
        act.wait_ge(moe_init, 1)
        act.sem_inc(y_ready, 1)
        act.sem_inc(gateT_ready, 1)
        n_blocks = act.value_load(table_i[0:1, MAX_BLOCKS:MAX_BLOCKS + 1], min_val=NEXP, max_val=MAX_BLOCKS - 1)
        with act.Fori(1, n_blocks + 1) as i:
            act.wait_ge(g_cut_ready, i)
            A(g_act, g_cut, ACT.Gelu_apprx_sigmoid).then_inc(g_act_ready, 1)
            take_gathered(i + 1)
            act.wait_ge(actT_done, i)
            A(actT, ps[:, 4, :].rearrange("p (c a s) -> p c a s", c=4, a=2), ACT.Copy).then_inc(actT_ready, 1)
            act.wait_ge(gateT_done, i)
            act.wait_ge(scattered, 3 * i)
            A(gateT[:, 0:TOKENS], ps[:, 5, 0:TOKENS], ACT.Copy).then_inc(gateT_ready, 1)
            take_turned(i + 1)
            act.wait_ge(unit_used, EXPERT_UNITS * i + ADA_UNITS)
            A(y_blk, ps[:, 2, :], ACT.Copy).then_inc(y_ready, 1)

    @block.vector
    def _(dve):
        X = nc.vector
        counts = {}

        def done(ins, signal=dve_step):
            counts[signal.name] = counts.get(signal.name, 0) + 1
            ins.then_inc(signal, 1)
            dve.wait_ge(signal, counts[signal.name])

        def rows(v, r, *shape):
            return v[0:r].to_broadcast([r, *shape])

        done(X.memset(stat[:, :], 1.0), stat_clean)
        dve.wait_ge(mod_bias_in, 64)
        for m in range(3):
            dve.wait_ge(unit_used, 4 * m + 4)
            done(X.tensor_tensor(mod[:, 4 * m:4 * m + 4, :], ps[:, m, :].rearrange("p (n c) -> p n c", n=4),
                                 mod_bias[:, 4 * m:4 * m + 4, :], ALU.add), mod_ready)

        def root_mean_square(n):
            done(X.tensor_scalar(stat[:, 0:3], stat[:, 0:3], 1.0 / D, EPS, ALU.mult, ALU.add), mean_sq)
            dve.wait_ge(sqrt_done, n)
            done(X.reciprocal(stat[:, 4:7], stat[:, 0:3]))

        def modulated(gain, n):
            for q, t in enumerate((2, 0, 1)):
                r = ROWS[t]
                base = 4 if t == 2 else 0
                done(X.scalar_tensor_tensor(out=W[0:r, t, :], in0=R[0:r, t, :], scalar=stat[0:r, 4 + t:5 + t], in1=gain[0:r], op0=ALU.mult, op1=ALU.mult))
                if q < 2:
                    dve.wait_ge(bcast_ready, 2 * n + q + 1)
                scale = ps[0:r, base:base + 2, :].rearrange("p a b -> p (a b)")
                shift = ps[0:r, base + 2:base + 4, :].rearrange("p a b -> p (a b)")
                done(X.scalar_tensor_tensor(out=W[0:r, t, :], in0=scale, scalar=1.0, in1=W[0:r, t, :], op0=ALU.add, op1=ALU.mult))
                done(X.tensor_tensor(T[0:r, t, :], W[0:r, t, :], shift, ALU.add), h_ready)

        dve.wait_ge(squared, 3)
        root_mean_square(1)
        dve.wait_ge(ln_mix_in, 16)
        modulated(ln_gain, 0)

        stats6 = stat[:, 80:92].rearrange("p (a b) -> p a b", a=2)
        dve.wait_ge(z_used, 4 * (CV1 + 1))
        for t, r in enumerate(ROWS):
            for h in range(2):
                done(X.bn_stats(stats6[0:r, h, :], V[0:r, t, HALF * h:HALF * h + HALF]))
            done(X.bn_aggr(stat[0:r, 92:94], stats6[0:r]))
            done(X.tensor_copy(stat[0:r, 12 + t:13 + t], stat[0:r, 92:93]))
            done(X.tensor_scalar(stat[0:r, 8 + t:9 + t], stat[0:r, 93:94], EPS, None, ALU.add), mean_sq if t == 2 else dve_step)
        dve.wait_ge(sqrt_done, 2)
        done(X.reciprocal(stat[:, 8:11], stat[:, 8:11]))
        dve.wait_ge(gm_in, 64)
        for t, r in enumerate(ROWS):
            done(X.tensor_scalar(V[0:r, t, :], V[0:r, t, :], stat[0:r, 12 + t:13 + t], stat[0:r, 8 + t:9 + t], ALU.subtract, ALU.mult))
            done(X.tensor_tensor(V[0:r, t, :], V[0:r, t, :], gm_gain[0:r], ALU.mult))
            done(X.tensor_tensor(V[0:r, t, :], V[0:r, t, :], gm_bias[0:r], ALU.add), cv_ready)
        dve.wait_ge(params_in, 16)
        for t, r in enumerate(ROWS):
            bias = param("mix_bias_s" if t == 2 else "mix_bias")
            for h in range(2):
                name = f"mix{t}{h}"
                aux_filled(dve, name)
                tmp = mix_tmp[0:r, 0:HALF]
                X.tensor_tensor(tmp.rearrange("p (g c) -> p g c", g=4), aux_bank(name)[0:r].rearrange("p (g c) -> p g c", g=4),
                                bias[0:r, 4 * h:4 * h + 4].unsqueeze(2).to_broadcast([r, 4, 128]), ALU.add).then_inc(used(name), 1)
                aux_taken(dve, name)
                done(X.tensor_tensor(U[0:r, t, HALF * h:HALF * h + HALF], U[0:r, t, HALF * h:HALF * h + HALF], tmp, ALU.mult))

        dve.wait_ge(z_used, 4 * (RK + 1))
        for t, r in enumerate(ROWS):
            v = R[0:r, t, :].rearrange("p (h a f) -> p h a f", h=16, a=2)
            x1, x2 = v[:, :, 0, :], v[:, :, 1, :]
            c = cos[0:r, t, :].unsqueeze(1).to_broadcast([r, 16, 32])
            s = sin[0:r, t, :].unsqueeze(1).to_broadcast([r, 16, 32])
            tm = T[0:r, 2 if t < 2 else 1, :]
            ta = tm[:, 0:512].rearrange("p (h f) -> p h f", h=16)
            tb = tm[:, 512:1024].rearrange("p (h f) -> p h f", h=16)
            done(X.tensor_tensor(ta, x1, s, ALU.mult))
            done(X.tensor_tensor(tb, x2, s, ALU.mult))
            done(X.tensor_tensor(x1, x1, c, ALU.mult))
            done(X.tensor_tensor(x2, x2, c, ALU.mult))
            done(X.tensor_tensor(x1, x1, tb, ALU.subtract))
            done(X.tensor_tensor(x2, x2, ta, ALU.add))
            full = R[0:r, t, :].rearrange("p (h f) -> p h f", h=16)
            done(X.tensor_tensor(full, full, decay[0:r, t, :].unsqueeze(2).to_broadcast([r, 16, 64]), ALU.mult), roped)
        for t, r in enumerate(ROWS):
            dve.wait_ge(gate_ready, t + 1)
            done(X.tensor_tensor(U[0:r, t, :], U[0:r, t, :], V[0:r, t, :], ALU.mult), branch_merged)

        causal4 = const("causal").unsqueeze(1).to_broadcast([P, 4, 128])
        for t in range(2):
            for h in range(2):
                name = f"ra{t}{h}"
                aux_filled(dve, name)
                X.tensor_tensor(ra[:, h, :].rearrange("p (h m) -> p h m", h=4), aux_bank(name).rearrange("p (h m) -> p h m", h=4), causal4, ALU.mult).then_inc(used(name), 1)
            for h in range(2):
                name = f"rs{t}{h}"
                aux_filled(dve, name)
                st = state[0:64, 4 * h:4 * h + 4, :]
                src = aux_bank(name)[0:64].rearrange("p (h m) -> p h m", h=4)
                dec = const("chunk_decay")[0:64, 4 * h:4 * h + 4].unsqueeze(2).to_broadcast([64, 4, RDV])
                if t == 0:
                    X.tensor_tensor(st, src, dec, ALU.mult).then_inc(used(name), 1)
                else:
                    X.tensor_tensor(st, src, st, ALU.add).then_inc(used(name), 1)
                    aux_taken(dve, name)
                    done(X.tensor_tensor(st, st, dec, ALU.mult), state_ready)
        aux_filled(dve, "ra2")
        X.tensor_tensor(ra[0:64, 0, :].rearrange("p (h m) -> p h m", h=8), aux_bank("ra2")[0:64].rearrange("p (h m) -> p h m", h=8),
                        const("blockcausal")[0:64].unsqueeze(1).to_broadcast([64, 8, 64]), ALU.mult).then_inc(used("ra2"), 1)
        for b in range(BATCH_S):
            if b:
                dve.wait_ge(state_stored, 16 * b)
            for h in range(2):
                name = f"rs2{b}{h}"
                aux_filled(dve, name)
                st = V[0:64, b % 2, HALF * h:HALF * h + HALF]
                new = V[0:64, 2, HALF * h:HALF * h + HALF]
                X.tensor_tensor(new, aux_bank(name)[0:64], st, ALU.add).then_inc(used(name), 1)
                aux_taken(dve, name)
                n4 = new.rearrange("p (h e) -> p h e", h=4)
                done(X.tensor_tensor(n4, n4, const("chunk_decay")[0:64, 8 + 4 * h:12 + 4 * h].unsqueeze(2).to_broadcast([64, 4, RDV]), ALU.mult), new_state)
        aux_taken(dve, "ro2")
        dve.wait_ge(inter_ready, 1)
        done(X.tensor_tensor(ro_s, ps[:, 1, :], ro_s, ALU.add), inter_added)
        aux_taken(dve, "rback0")
        aux_taken(dve, "rback1")
        dve.wait_ge(retention_stored, 16)
        for t, r in enumerate(ROWS):
            o3 = T[0:r, t, :].rearrange("p (h e) -> p h e", h=RH)
            done(X.tensor_reduce(stat[0:r, 16:24], o3, AX.X, ALU.add))
            done(X.tensor_scalar(stat[0:r, 16:24], stat[0:r, 16:24], 1.0 / RDV, None, ALU.mult))
            done(X.tensor_tensor(o3, o3, stat[0:r, 16:24].unsqueeze(2).to_broadcast([r, RH, RDV]), ALU.subtract), head_centred)
            dve.wait_ge(head_squared, t + 1)
            done(X.tensor_reduce(stat[0:r, 16:24], squares[0:r].rearrange("p (h e) -> p h e", h=RH), AX.X, ALU.add))
            done(X.tensor_scalar(stat[0:r, 16:24], stat[0:r, 16:24], 1.0 / RDV, EPS, ALU.mult, ALU.add), mean_sq)
            dve.wait_ge(sqrt_done, 3 + t)
            done(X.reciprocal(stat[0:r, 16:24], stat[0:r, 16:24]))
            done(X.tensor_tensor(o3, o3, stat[0:r, 16:24].unsqueeze(2).to_broadcast([r, RH, RDV]), ALU.mult))
            dve.wait_ge(silu_scaled, t + 1)
            done(X.tensor_tensor(T[0:r, t, :], T[0:r, t, :], V[0:r, t, :], ALU.mult), ret_scaled)
            dve.wait_ge(gate_ready, 3 + t + 1)
            done(X.tensor_tensor(T[0:r, t, :], T[0:r, t, :], W[0:r, t, :], ALU.mult))
            done(X.tensor_tensor(U[0:r, t, :], U[0:r, t, :], T[0:r, t, :], ALU.add), branch_merged)

        dve.wait_ge(z_used, 4 * (AKV + 1))
        for t, r in enumerate(ROWS):
            q3 = R[0:r, t, :].rearrange("p (h e) -> p h e", h=QH)
            k3 = V[0:r, t, 0:256].rearrange("p (h e) -> p h e", h=KVH)
            sq = T[0:r, 1, :]
            done(X.tensor_tensor(sq, R[0:r, t, :], R[0:r, t, :], ALU.mult))
            done(X.tensor_reduce(stat[0:r, 24:40], sq.rearrange("p (h e) -> p h e", h=QH), AX.X, ALU.add))
            done(X.tensor_tensor(sq[:, 0:256], V[0:r, t, 0:256], V[0:r, t, 0:256], ALU.mult))
            done(X.tensor_reduce(stat[0:r, 40:44], sq[:, 0:256].rearrange("p (h e) -> p h e", h=KVH), AX.X, ALU.add))
            done(X.tensor_scalar(stat[0:r, 24:40], stat[0:r, 24:40], HD * EPS, None, ALU.add))
            done(X.tensor_scalar(stat[0:r, 40:44], stat[0:r, 40:44], 1.0 / HD, EPS, ALU.mult, ALU.add), mean_sq)
            dve.wait_ge(sqrt_done, 6 + t)
            done(X.reciprocal(stat[0:r, 24:44], stat[0:r, 24:44]))
            done(X.tensor_tensor(q3, q3, stat[0:r, 24:40].unsqueeze(2).to_broadcast([r, QH, HD]), ALU.mult))
            done(X.tensor_tensor(k3, k3, stat[0:r, 40:44].unsqueeze(2).to_broadcast([r, KVH, HD]), ALU.mult))
            done(X.tensor_tensor(V[0:r, t, 0:256], V[0:r, t, 0:256], param("k_gain")[0:r], ALU.mult), qk_normed)
        dve.wait_ge(gate_biased, 9)

        softmaxes = [0]

        def softmax(count, width, sink):
            softmaxes[0] += 1
            done(X.tensor_reduce(stat[:, 60:60 + count], probs[:, 0:count, 0:width], AX.X, ALU.max))
            done(X.tensor_tensor(stat[:, 60:60 + count], stat[:, 60:60 + count], sink, ALU.max))
            done(X.tensor_scalar(stat[:, 48:48 + count], stat[:, 60:60 + count], -1.0, None, ALU.mult))
            done(X.tensor_tensor(stat[:, 60:60 + count], sink, stat[:, 60:60 + count], ALU.subtract), max_ready)
            dve.wait_ge(exp_done, softmaxes[0])
            done(X.tensor_tensor(stat[:, 52:52 + count], stat[:, 52:52 + count], stat[:, 56:56 + count], ALU.add))
            done(X.reciprocal(stat[:, 68:68 + count], stat[:, 52:52 + count]))
            done(X.tensor_tensor(probs[:, 0:count, 0:width], probs[:, 0:count, 0:width],
                                 stat[:, 68:68 + count].unsqueeze(2).to_broadcast([P, count, width]), ALU.mult), probs_ready)

        window = const("window")
        for t in range(2):
            for g in range(KVH):
                if t == 0:
                    name = f"sc0{g}0"
                    aux_filled(dve, name)
                    X.tensor_tensor(probs[:, :, 0:P], aux_bank(name).rearrange("p (h k) -> p h k", h=4),
                                    window[:, P:2 * P].unsqueeze(1).to_broadcast([P, 4, P]), ALU.add).then_inc(used(name), 1)
                    aux_taken(dve, name)
                else:
                    for k in range(2):
                        name = f"sc1{g}{k}"
                        aux_filled(dve, name)
                        X.tensor_tensor(probs[:, 2 * k:2 * k + 2, :], aux_bank(name).rearrange("p (h k) -> p h k", h=2),
                                        window.unsqueeze(1).to_broadcast([P, 2, 2 * P]), ALU.add).then_inc(used(name), 1)
                        aux_taken(dve, name)
                softmax(4, P * (t + 1), param("sinks")[:, 4 * g:4 * g + 4])
                name = f"pv{t}{g}"
                aux_filled(dve, name)
                X.tensor_copy(T[:, t, 256 * g:256 * g + 256], aux_bank(name)[:, 0:256]).then_inc(used(name), 1)
                aux_taken(dve, name)
        for b in range(BATCH_S):
            name = f"sc2{b}"
            aux_filled(dve, name)
            done(X.tensor_tensor(probs[:, 0, 0:P], aux_bank(name)[:, 0:P], const("cache_mask"), ALU.add))
            X.tensor_tensor(probs[:, 0, P:192], aux_bank(name)[:, P:192], new_mask[:, b, :], ALU.add).then_inc(used(name), 1)
            aux_taken(dve, name)
            softmax(1, 192, param("sink_rows"))
        aux_taken(dve, "oback0")
        aux_taken(dve, "oback1")
        for t, r in enumerate(ROWS):
            dve.wait_ge(gate_ready, 6 + t + 1)
            done(X.tensor_tensor(T[0:r, t, :], T[0:r, t, :], W[0:r, t, :], ALU.mult))
            done(X.tensor_tensor(U[0:r, t, :], U[0:r, t, :], T[0:r, t, :], ALU.add), branch_merged)

        dve.wait_ge(x_again_in, 32)
        dve.wait_ge(z_used, 4 * (IN_UNITS + 2))
        for name in ("g1p0", "g1p1", "g1s0", "g1s1"):
            aux_taken(dve, name)
        for t in (2, 0, 1):
            r = ROWS[t]
            done(X.tensor_tensor(W[0:r, t, :], W[0:r, t, :], V[0:r, 2 if t == 2 else 0, :], ALU.mult))
            done(X.tensor_tensor(R[0:r, t, :], R[0:r, t, :], W[0:r, t, :], ALU.add), x1_ready)
        dve.wait_ge(squared, 6)
        root_mean_square(9)
        dve.wait_ge(ln_ffn_in, 16)
        modulated(ln_ffn, 1)

        dve.wait_ge(params_in, 16)
        done(X.memset(select_e, 0.0))
        done(X.memset(gate_e, 0.0))
        iota = const("iota")
        for t, r in enumerate(ROWS):
            name = f"lg{t}"
            aux_filled(dve, name)
            lg = rtmp[0:r, 0, :]
            X.tensor_tensor(lg, aux_bank(name)[0:r, 0:NEXP], param("router_b")[0:r], ALU.add).then_inc(used(name), 1)
            aux_taken(dve, name)
            done(X.max(stat[0:r, 64:72], lg))
            done(X.max_index(top_i[0:r], stat[0:r, 64:72], lg))
            done(X.tensor_copy(stat[0:r, 80:88], top_i[0:r]))
            done(X.tensor_scalar(stat[0:r, 76:77], stat[0:r, 64:65], -1.0, None, ALU.mult), top_ready)
            dve.wait_ge(top_exp, t + 1)
            done(X.reciprocal(stat[0:r, 77:78], stat[0:r, 77:78]))
            done(X.tensor_scalar(stat[0:r, 72:76], stat[0:r, 72:76], stat[0:r, 77:78], None, ALU.mult))
            for k in range(TOPK):
                hot = rtmp[0:r, 1, :]
                done(X.tensor_scalar(hot, iota[0:r, 0:NEXP], stat[0:r, 80 + k:81 + k], None, ALU.is_equal))
                done(X.tensor_tensor(select_e[0:r, t, :], select_e[0:r, t, :], hot, ALU.add))
                done(X.scalar_tensor_tensor(out=gate_e[0:r, t, :], in0=hot, scalar=stat[0:r, 72 + k:73 + k], in1=gate_e[0:r, t, :],
                                            op0=ALU.mult, op1=ALU.add), routed if k == TOPK - 1 else dve_step)
        done(X.memset(slot_of, -1.0))
        for t, r in enumerate(ROWS):
            name = f"pos{t}"
            aux_filled(dve, name)
            s = slot_of[0:r, t, :]
            X.scalar_tensor_tensor(out=s, in0=aux_bank(name)[0:r, 0:NEXP], scalar=1.0, in1=select_e[0:r, t, :], op0=ALU.add, op1=ALU.mult).then_inc(used(name), 1)
            aux_taken(dve, name)
            done(X.tensor_scalar(s, s, 1.0, None, ALU.subtract))
        aux_filled(dve, "cnt")
        counted = rtmp[:, 1, :]
        X.tensor_copy(counted, aux_bank("cnt")[:, 0:NEXP]).then_inc(used("cnt"), 1)
        aux_taken(dve, "cnt")
        done(X.tensor_scalar(n_of, counted, float(BLOCK), 1.0, ALU.is_gt, ALU.add))
        for m in range(2, TOKENS // BLOCK):
            done(X.scalar_tensor_tensor(out=n_of, in0=counted, scalar=float(BLOCK * m), in1=n_of, op0=ALU.is_gt, op1=ALU.add))
        done(X.tensor_tensor_scan(out=cum_of, data0=ones[:, 0:NEXP], data1=n_of, initial=0.0, op0=ALU.mult, op1=ALU.add))
        shape = [P, MAX_BLOCKS, NEXP]
        done(X.tensor_tensor(passed, iota.unsqueeze(2).to_broadcast(shape), cum_of.unsqueeze(1).to_broadcast(shape), ALU.is_ge))
        done(X.tensor_reduce(expert_of, passed, AX.X, ALU.add))
        done(X.tensor_scalar(expert_of, expert_of, float(NEXP - 1), None, ALU.min))
        done(X.tensor_tensor(passed, passed, n_of.unsqueeze(1).to_broadcast(shape), ALU.mult))
        done(X.tensor_reduce(slot_base, passed, AX.X, ALU.add))
        done(X.tensor_tensor(slot_base, iota, slot_base, ALU.subtract))
        done(X.tensor_scalar(slot_base, slot_base, float(BLOCK), None, ALU.mult))
        done(X.tensor_copy(table_i[0:1, 0:MAX_BLOCKS], expert_of[0:1, :]))
        done(X.tensor_copy(table_i[0:1, MAX_BLOCKS:MAX_BLOCKS + 1], cum_of[0:1, NEXP - 1:NEXP]))
        done(X.tensor_tensor(table_i[0:1, MAX_BLOCKS + 1:MAX_BLOCKS + 1 + NEXP], cum_of[0:1, :], n_of[0:1, :], ALU.subtract), table_ready)
        done(X.memset(y_blk, 0.0), added)
        done(X.memset(gateT, 0.0), moe_init)


        def pick_tokens(at, e, waited):
            X.tensor_scalar(sel_now[:, 0, :], slot_of[:, :, bass.ds(e, 1)].rearrange("p t a -> p (t a)"), slot_base[:, bass.ds(at, 1)], None, ALU.subtract).then_inc(moe_step, 1)
            X.tensor_copy(sel_now[:, 1, :], gate_e[:, :, bass.ds(e, 1)].rearrange("p t a -> p (t a)")).then_inc(moe_step, 1)
            dve.wait_ge(moe_step, waited)
            X.tensor_tensor(pick, iota.unsqueeze(1).to_broadcast([P, 3, BLOCK]), sel_now[:, 0, :].unsqueeze(2).to_broadcast([P, 3, BLOCK]), ALU.is_equal).then_inc(picked, 1)

        pick_tokens(0, 0, 2)
        n_blocks = dve.value_load(table_i[0:1, MAX_BLOCKS:MAX_BLOCKS + 1], min_val=NEXP, max_val=MAX_BLOCKS - 1)
        with dve.Fori(1, n_blocks + 1) as i:
            dve.wait_ge(picked, i)
            dve.wait_ge(unit_used, EXPERT_UNITS * i + ADA_UNITS - EXPERT_UNITS)
            X.tensor_tensor(pick_gate, pick.unsqueeze(2).to_broadcast([P, 3, 2, BLOCK]),
                            sel_now[:, 1, :].unsqueeze(2).unsqueeze(3).to_broadcast([P, 3, 2, BLOCK]), ALU.mult).then_inc(gates_picked, 1)
            e_next = dve.value_load(table_i[0:1, bass.ds(i, 1)], min_val=0, max_val=NEXP - 1)
            dve.wait_ge(gates_picked, i)
            dve.wait_ge(gathered, i)
            pick_tokens(i, e_next, 2 * i + 2)
            dve.wait_ge(unit_used, EXPERT_UNITS * i + ADA_UNITS - 4)
            X.tensor_scalar(g_cut, ps[:, 0, :], LIMIT, None, ALU.min).then_inc(g_cut_ready, 1)
            dve.wait_ge(unit_used, EXPERT_UNITS * i + ADA_UNITS - 2)
            X.tensor_scalar(u_cut, ps[:, 1, :], LIMIT, -LIMIT, ALU.min, ALU.max).then_inc(dve_step, 1)
            dve.wait_ge(dve_step, i + counts["dve_step"])
            dve.wait_ge(g_act_ready, i)
            X.scalar_tensor_tensor(out=h_act, in0=u_cut, scalar=1.0, in1=g_act, op0=ALU.add, op1=ALU.mult).then_inc(act_ready, 1)
            for t, r in enumerate(ROWS):
                dve.wait_ge(scattered, 3 * i + t - 2)
                both = U[0:r, t, :].rearrange("p (a b) -> p a b", a=2)
                X.tensor_tensor(both, ps[0:r, 6:8, :], both, ALU.add).then_inc(added, 1)
        for t, r in enumerate(ROWS):
            dve.wait_ge(scattered, 3 * n_blocks + t + 1)
            both = U[0:r, t, :].rearrange("p (a b) -> p a b", a=2)
            X.tensor_tensor(both, ps[0:r, 6:8, :], both, ALU.add).then_inc(added, 1)
            dve.wait_ge(added, 3 * n_blocks + t + 2)
            X.tensor_tensor(U[0:r, t, :], U[0:r, t, :], V[0:r, 2 if t == 2 else 0, :], ALU.mult).then_inc(scaled, 1)
            dve.wait_ge(scaled, t + 1)
            X.tensor_tensor(R[0:r, t, :], R[0:r, t, :], U[0:r, t, :], ALU.add).then_inc(final_ready, 1)

    @block.tensor
    def _(pe):
        mm = nc.tensor.matmul

        def tr(out, in_, r, **kw):
            return nc.tensor.transpose(out, in_, ident[0:r, 0:r], **kw)

        def aux_free(name):
            n = AUX_AT[name]
            if n >= AUX_BANKS:
                pe.wait_ge(aux_used[n % AUX_BANKS], n // AUX_BANKS)

        pe.wait_ge(silu_done, 1)
        for n in range(ADA_UNITS):
            unit_arrived(pe, n)
            wv = ring[:, n % SLOTS, :].rearrange("p (k c) -> p k c", k=KD)
            for k in range(KD):
                for j in range(4):
                    last = mm(ps[32 * j:32 * j + 32, n // 4, (n % 4) * 128:(n % 4) * 128 + 128], silu_c[:, k, :],
                              wv[:, k, 128 * j:128 * j + 128], start=(k == 0), stop=(k == KD - 1), skip_group_check=True)
            last.then_inc(unit_used, 1)

        def spread(n, bank, cols, r):
            for j in range(4):
                last = mm(bank[0:r, 128 * j:128 * j + 128], select[:, j, cols:cols + r], mod[:, n, :], start=True, stop=True)
            return last

        def spread_norm(shift, scale):
            for base, cols, r in ((4, P, 64), (0, 0, P)):
                for h in range(2):
                    spread(scale + h, ps[:, base + h, :], cols, r)
                for h in range(2):
                    last = spread(shift + h, ps[:, base + 2 + h, :], cols, r)
                last.then_inc(bcast_ready, 1)

        def transpose_all(buf, ready, n):
            for q, (t, k0, nk) in enumerate(TR_PARTS):
                if q in (0, 1, 3):
                    ready(t)
                if q == 4:
                    pe.wait_ge(xT_ready, 5 * n + 1)
                r = ROWS[t]
                for k in range(nk):
                    last = tr(ps[:, TR_BANKS[q], k * r:k * r + r], buf[0:r, t, (k0 + k) * P:(k0 + k + 1) * P], r)
                last.then_inc(tr_ready, 1)

        def project(idx):
            unit_arrived(pe, ADA_UNITS + idx)
            if idx >= 2:
                pe.wait_ge(z_used, 4 * (idx - 1))
            wv = ring[:, (ADA_UNITS + idx) % SLOTS, :].rearrange("p (k c) -> p k c", k=KD)
            banks = z_banks(idx)
            for t in range(2):
                for k in range(KD):
                    last = mm(banks[t][0], xT[:, k, t * P:t * P + P], wv[:, k, :], start=(k == 0), stop=(k == KD - 1))
                last.then_inc(z_ready, 1)
            if idx >= 1:
                pe.wait_ge(z_used, 4 * idx)
            for k in range(KD):
                for a in range(2):
                    last = mm(banks[2 + a][0], xT[:, k, 2 * P:TOKENS], wv[:, k, 256 * a:256 * a + 256],
                              start=(k == 0), stop=(k == KD - 1), skip_group_check=True)
            last.then_inc(z_ready, 1)

        pe.wait_ge(consts_in, 16)
        pe.wait_ge(mod_ready, 3)
        spread_norm(0, 2)
        transpose_all(T, lambda t: pe.wait_ge(h_ready, {2: 1, 0: 2, 1: 3}[t]), 0)
        pe.wait_ge(xT_ready, 5)

        for idx in (CU0, CU1, CV0, CV1, RQ, RK, RV0, RV1):
            project(idx)

        pe.wait_ge(mixw_ready, 2)
        for t, r in enumerate(ROWS):
            pe.wait_ge(cv_ready, t + 1)
            w = mixT_s if t == 2 else mixT
            for h in range(2):
                name = f"mix{t}{h}"
                aux_free(name)
                for g in range(4 * h, 4 * h + 4):
                    last = mm(aux_bank(name)[0:r, (g % 4) * P:(g % 4) * P + P], w[0:r, g, :], V[0:r, t, g * P:(g + 1) * P], start=True, stop=True)
                last.then_inc(aux_ready, 1)
        project(GC0)
        project(GC1)

        for t in range(2):
            pe.wait_ge(roped, 1 + 2 * t)
            for h in range(2):
                for kind, c0 in (("rqT", 0), ("rkT", HALF)):
                    name = f"{kind}{t}{h}"
                    aux_free(name)
                    for n in range(4):
                        c = c0 + (4 * h + n) * RDK
                        last = tr(aux_bank(name)[0:64, n * P:n * P + P], R[:, t, c:c + RDK], P)
                    last.then_inc(aux_ready, 1)
                name = f"ra{t}{h}"
                aux_free(name)
                aux_taken(pe, f"rqT{t}{h}")
                aux_taken(pe, f"rkT{t}{h}")
                for n in range(4):
                    last = mm(aux_bank(name)[:, n * P:n * P + P], rkT[0:64, 4 * h + n, :], rqT[0:64, 4 * h + n, :], start=True, stop=True)
                last.then_inc(aux_ready, 1)
                name = f"ro{t}{h}"
                aux_free(name)
                aux_taken(pe, f"ra{t}{h}")
                if t == 1:
                    aux_taken(pe, f"rs0{h}")
                pe.wait_ge(z_used, 4 * (RV1 + 1))
                for n in range(4):
                    hh = 4 * h + n
                    out = aux_bank(name)[:, n * P:n * P + P]
                    last = mm(out, ra[:, h, n * P:n * P + P], W[:, t, hh * RDV:(hh + 1) * RDV], start=True, stop=(t == 0))
                    if t == 1:
                        last = mm(out, rqT[0:64, hh, :], state[0:64, hh, :], start=False, stop=True)
                last.then_inc(aux_ready, 1)
            for h in range(2):
                name = f"rs{t}{h}"
                aux_free(name)
                for n in range(4):
                    hh = 4 * h + n
                    last = mm(aux_bank(name)[0:64, n * P:n * P + P], R[:, t, HALF + hh * RDK:HALF + (hh + 1) * RDK],
                              W[:, t, hh * RDV:(hh + 1) * RDV], start=True, stop=True)
                last.then_inc(aux_ready, 1)
        pe.wait_ge(roped, 3)
        for name, c0 in (("rqT2", 0), ("rkT2", HALF)):
            aux_free(name)
            for n in range(RH):
                last = tr(aux_bank(name)[0:64, n * 64:n * 64 + 64], R[0:64, 2, c0 + n * RDK:c0 + (n + 1) * RDK], 64)
            last.then_inc(aux_ready, 1)
        aux_free("ra2")
        aux_taken(pe, "rqT2")
        aux_taken(pe, "rkT2")
        for n in range(RH):
            last = mm(aux_bank("ra2")[0:64, n * 64:n * 64 + 64], rkT[0:64, n, 0:64], rqT[0:64, n, 0:64], start=True, stop=True)
        last.then_inc(aux_ready, 1)
        aux_free("ro2")
        aux_taken(pe, "ra2")
        for n in range(RH):
            last = mm(aux_bank("ro2")[:, n * 64:n * 64 + 64], W[0:64, 2, n * RDV:(n + 1) * RDV], ra[0:64, 0, n * 64:n * 64 + 64], start=True, stop=True)
        last.then_inc(aux_ready, 1)
        pe.wait_ge(z_used, 4 * (GC1 + 1))
        for b in range(BATCH_S):
            pe.wait_ge(state_in[b % 2], 16 * (b // 2 + 1))
            for n in range(RH):
                last = mm(ps[:, 1, n * 64 + b * STEPS:n * 64 + (b + 1) * STEPS],
                          V[0:64, b % 2, n * RDV:(n + 1) * RDV], rqT[0:64, n, b * STEPS:(b + 1) * STEPS], start=True, stop=True)
            if b == BATCH_S - 1:
                last.then_inc(inter_ready, 1)
            pe.wait_ge(kd_ready, b + 1)
            for h in range(2):
                name = f"rs2{b}{h}"
                aux_free(name)
                for n in range(4):
                    hh = 4 * h + n
                    last = mm(aux_bank(name)[0:64, n * P:n * P + P], kd[0:64, hh * RDK:(hh + 1) * RDK],
                              W[0:64, 2, hh * RDV:(hh + 1) * RDV], start=True, stop=True)
                last.then_inc(aux_ready, 1)
        pe.wait_ge(inter_added, 1)
        for h in range(2):
            name = f"rback{h}"
            aux_free(name)
            for n in range(4):
                hh = 4 * h + n
                last = tr(aux_bank(name)[0:64, n * P:n * P + P], ro_s[:, hh * 64:hh * 64 + 64], P)
            last.then_inc(aux_ready, 1)
        for idx in (RG0, RG1, GB0, GB1, AQ0, AQ1, AKV, GA0, GA1):
            project(idx)

        for t, r in enumerate(ROWS):
            pe.wait_ge(qk_normed, t + 1)
            name = f"kT{t}"
            aux_free(name)
            for g in range(KVH):
                last = tr(aux_bank(name)[0:64, g * r:g * r + r], V[0:r, t, g * HD:(g + 1) * HD], r)
            last.then_inc(aux_ready, 1)

        def transpose_queries(t):
            n, r = (2, 64) if t == 2 else (4, P)
            for q in range(n):
                name = f"qT{t}{q}"
                aux_free(name)
                for m in range(QH // n):
                    h = q * (QH // n) + m
                    last = tr(aux_bank(name)[0:64, m * r:m * r + r], R[0:r, t, h * HD:(h + 1) * HD], r)
                last.then_inc(aux_ready, 1)
            for q in range(n):
                aux_taken(pe, f"qT{t}{q}")

        softmaxes = 0
        for t in range(3):
            aux_taken(pe, f"kT{t}")
        for t in range(2):
            transpose_queries(t)
            for g in range(KVH):
                for k in range(t + 1):
                    name = f"sc{t}{g}{k}"
                    aux_free(name)
                    n, width = (4, P) if t == 0 else (2, 2 * P)
                    for m in range(n):
                        last = mm(aux_bank(name)[:, m * width:(m + 1) * width], qTa[0:64, 4 * g + n * k + m, :],
                                  kTa[0:64, g, 0:width], start=True, stop=True)
                    last.then_inc(aux_ready, 1)
                softmaxes += 1
                pe.wait_ge(probs_ready, softmaxes)
                for k in range(t + 1):
                    name = f"pT{t}{g}{k}"
                    aux_free(name)
                    for h in range(GROUP):
                        last = tr(aux_bank(name)[:, h * P:h * P + P], probs[:, h, k * P:k * P + P], P)
                    last.then_inc(aux_ready, 1)
                name = f"pv{t}{g}"
                aux_free(name)
                for k in range(t + 1):
                    aux_taken(pe, f"pT{t}{g}{k}")
                for h in range(GROUP):
                    for k in range(t + 1):
                        last = mm(aux_bank(name)[:, h * HD:(h + 1) * HD], pT[:, k, h * P:h * P + P],
                                  V[:, k, 256 + g * HD:256 + (g + 1) * HD], start=(k == 0), stop=(k == t))
                last.then_inc(aux_ready, 1)
        transpose_queries(2)
        for b in range(BATCH_S):
            name = f"sc2{b}"
            aux_free(name)
            pe.wait_ge(cache_in[b % 2], 32 * (b // 2 + 1))
            keys = cache[0:64, b % 2, 0:512].rearrange("p (h r) -> p h r", h=KVH)
            for g in range(KVH):
                q = qTs[0:64, b, GROUP * g:GROUP * (g + 1), :].rearrange("p h t -> p (h t)")
                mm(aux_bank(name)[32 * g:32 * g + 32, 0:P], q, keys[:, g, :], start=True, stop=True, skip_group_check=True)
                last = mm(aux_bank(name)[32 * g:32 * g + 32, P:192], q, kTa[0:64, g, SEQ:TOKENS], start=True, stop=True, skip_group_check=True)
            last.then_inc(aux_ready, 1)
            softmaxes += 1
            pe.wait_ge(probs_ready, softmaxes)
            name = f"pT2{b}"
            aux_free(name)
            tr(aux_bank(name)[:, 0:P], probs[:, 0, 0:P], P)
            tr(aux_bank(name)[0:64, P:2 * P], probs[:, 0, P:192], P).then_inc(aux_ready, 1)
            name = f"pv2{b}"
            aux_free(name)
            aux_taken(pe, f"pT2{b}")
            for g in range(KVH):
                out = aux_bank(name)[0:64, 32 * g:32 * g + 32]
                mm(out, cache[:, b % 2, 512 + g * HD:512 + (g + 1) * HD], pT[:, 0, 32 * g:32 * g + 32], start=True, stop=False)
                last = mm(out, V[0:64, 2, 256 + g * HD:256 + (g + 1) * HD], pT[0:64, 1, 32 * g:32 * g + 32], start=False, stop=True)
            last.then_inc(aux_ready, 1)
        for h in range(2):
            name = f"oback{h}"
            aux_free(name)
            aux_taken(pe, f"pv2{BATCH_S - 1}")
            for m in range(8):
                last = tr(aux_bank(name)[0:64, m * HD:(m + 1) * HD], oT[0:64, 8 * h + m, :], 64)
            last.then_inc(aux_ready, 1)

        transpose_all(U, lambda t: pe.wait_ge(branch_merged, 6 + t + 1), 1)
        pe.wait_ge(xT_ready, 10)

        def spread_gate(kind, first):
            for s, cols, r in (("p", 0, P), ("s", P, 64)):
                for h in range(2):
                    name = f"{kind}{s}{h}"
                    aux_free(name)
                    spread(first + h, aux_bank(name), cols, r).then_inc(aux_ready, 1)

        spread_gate("g1", 4)
        project(IN_UNITS)
        project(IN_UNITS + 1)
        pe.wait_ge(z_used, 4 * (IN_UNITS + 2))
        for name in ("g1p0", "g1p1", "g1s0", "g1s1"):
            aux_taken(pe, name)
        spread_norm(6, 8)
        transpose_all(T, lambda t: pe.wait_ge(h_ready, {2: 4, 0: 5, 1: 6}[t]), 2)
        pe.wait_ge(xT_ready, 15)
        spread_gate("g2", 10)

        pe.wait_ge(router_in, 16)
        for t, r in enumerate(ROWS):
            name = f"lg{t}"
            aux_free(name)
            for k in range(KD):
                last = mm(aux_bank(name)[0:r, 0:NEXP], xT[:, k, t * P:t * P + r], router_w[:, k, :], start=(k == 0), stop=(k == KD - 1))
            last.then_inc(aux_ready, 1)
        pe.wait_ge(routed, 3)
        for t, r in enumerate(ROWS):
            name = f"pos{t}"
            aux_free(name)
            for s in range(t + 1):
                w = const("before") if s == t else ones
                last = mm(aux_bank(name)[0:r, 0:NEXP], w[0:ROWS[s], 0:r], select_e[0:ROWS[s], s, :], start=(s == 0), stop=(s == t))
            last.then_inc(aux_ready, 1)
        aux_free("cnt")
        for s, r in enumerate(ROWS):
            last = mm(aux_bank("cnt")[:, 0:NEXP], ones[0:r, :], select_e[0:r, s, :], start=(s == 0), stop=(s == 2))
        last.then_inc(aux_ready, 1)
        aux_free("gT")
        for t, r in enumerate(ROWS):
            last = tr(aux_bank("gT")[0:NEXP, t * P:t * P + r], gate_e[0:r, t, :], r)
        last.then_inc(aux_ready, 1)
        aux_taken(pe, "gT")
        pe.wait_ge(b2_in, 16)
        for t, r in enumerate(ROWS):
            for h in range(2):
                name = f"b2{'abc'[t]}{h}"
                aux_free(name)
                mm(aux_bank(name)[0:r], gates_T[:, t * P:t * P + r], b2_sb[0:NEXP, HALF * h:HALF * h + HALF], start=True, stop=True).then_inc(aux_ready, 1)
        for t in range(3):
            for h in range(2):
                aux_taken(pe, f"b2{'abc'[t]}{h}")

        def gather(n):
            pe.wait_ge(picked, n)
            for t, r in enumerate(ROWS):
                for a in range(2):
                    last = mm(ps[64 * a:64 * a + 64, 3, :], pick[0:r, t, :], T[0:r, t, HALF * a:HALF * a + HALF],
                              start=(t == 0), stop=(t == 2), skip_group_check=True)
            last.then_inc(gathered, 1)

        def turn(n):
            pe.wait_ge(xg_rows, n)
            for c in range(4):
                last = tr(ps[:, 3, c * P:(c + 1) * P], xg_s[:, c * P:(c + 1) * P], P)
            last.then_inc(turned, 1)

        def scatter(n, t):
            pe.wait_ge(added, 3 * n + t - 2)
            for a in range(2):
                last = mm(ps[:, 6 + a, :], gateT[64 * a:64 * a + 64, t * P:(t + 1) * P], y_blk[64 * a:64 * a + 64, :], start=True, stop=True)
            last.then_inc(scattered, 1)

        def unit(j):
            slot = (DENSE_UNITS + j) % SLOTS
            return slot, (DENSE_UNITS + j) // SLOTS

        pe.wait_ge(moe_init, 1)
        gather(1)
        turn(1)
        n_blocks = pe.value_load(table_i[0:1, MAX_BLOCKS:MAX_BLOCKS + 1], min_val=NEXP, max_val=MAX_BLOCKS - 1)
        with pe.Fori(1, n_blocks + 1) as i:
            e = pe.value_load(table_i[0:1, bass.ds(i - 1, 1)], min_val=0, max_val=NEXP - 1)
            pe.wait_ge(xg_ready, i)
            for half in range(2):
                for j in (2 * half, 2 * half + 1):
                    slot, before = unit(j)
                    pe.wait_ge(unit_in[slot], 16 * e + (16 * before + 16))
                    wv = ring[:, slot, :].rearrange("p (k c) -> p k c", k=4)
                    for k in range(4):
                        for a in range(2):
                            last = mm(ps[64 * a:64 * a + 64, half, :], xgT[:, k, j % 2, :], wv[:, k, HALF * a:HALF * a + HALF],
                                      start=(j % 2 == 0 and k == 0), stop=False, skip_group_check=True)
                    if j % 2 == 0:
                        last.then_inc(unit_used, 1)
                pe.wait_ge(b1_in[half], 16 * e + 16)
                for a in range(2):
                    last = mm(ps[64 * a:64 * a + 64, half, :], ones[0:1, 0:64], W[0:1, half, HALF * a:HALF * a + HALF],
                              start=False, stop=True, skip_group_check=True)
                last.then_inc(unit_used, 1)
            pe.wait_ge(y_ready, i)
            pe.wait_ge(gateT_ready, i)
            scatter(i, 0)
            gather(i + 1)
            pe.wait_ge(act_ready, i)
            for c in range(4):
                last = tr(ps[:, 4, c * P:(c + 1) * P], h_act[:, c * P:(c + 1) * P], P)
            last.then_inc(actT_done, 1)
            pe.wait_ge(gates_picked, i)
            for t, r in enumerate(ROWS):
                last = tr(ps[:, 5, t * P:t * P + r], pick_gate[0:r, t, :, :], r)
            last.then_inc(gateT_done, 1)
            scatter(i, 1)
            scatter(i, 2)
            pe.wait_ge(actT_ready, i)
            for j in (4, 5):
                slot, before = unit(j)
                pe.wait_ge(unit_in[slot], 16 * e + (16 * before + 16))
                wv = ring[:, slot, :].rearrange("p (k c) -> p k c", k=4)
                for k in range(4):
                    for a in range(2):
                        last = mm(ps[64 * a:64 * a + 64, 2, :], actT[:, k, j - 4, :], wv[:, k, HALF * a:HALF * a + HALF],
                                  start=(j == 4 and k == 0), stop=(j == 5 and k == 3), skip_group_check=True)
                last.then_inc(unit_used, 1)
                if j == 4:
                    turn(i + 1)
        pe.wait_ge(y_ready, n_blocks + 1)
        pe.wait_ge(gateT_ready, n_blocks + 1)
        for t in range(3):
            scatter(n_blocks + 1, t)


def shape_constants():
    c = {name: np.zeros((P, width), np.float32) for name, width in CONST_WIDTHS}
    p = np.arange(P)
    c["ident"][:] = np.eye(P)
    c["causal"][:] = p[:, None] <= p[None, :]
    q = np.arange(64)
    c["blockcausal"][:64] = (q[:, None] // STEPS == q[None, :] // STEPS) & (q[:, None] <= q[None, :])
    sel = np.zeros((P, 4, 192), np.float32)
    for j in range(4):
        sel[32 * j, j, :P] = 1
        sel[32 * j + 1 + q // STEPS, j, P + q] = 1
    c["select"][:] = sel.reshape(P, -1)
    pos = np.concatenate([np.arange(SEQ), PAST + q % STEPS, np.zeros(64)]).astype(np.float32)
    freq = np.float32(10000.0) ** (-np.arange(0, RDK, 2, dtype=np.float32) / np.float32(RDK))
    angle = (pos[:, None] * freq[None, :].astype(np.float32)).astype(np.float32).astype(np.float64).reshape(3, P, 32)
    c["cos"][:] = np.cos(angle).transpose(1, 0, 2).reshape(P, -1)
    c["sin"][:] = np.sin(angle).transpose(1, 0, 2).reshape(P, -1)
    gamma = 1.0 - 2.0 ** (-5.0 - np.arange(RH))
    in_chunk = np.concatenate([np.arange(P), np.arange(P), q % STEPS, np.zeros(64)])
    up = gamma[None] ** (in_chunk[:, None] + 1)
    decay = np.concatenate([up, RDK ** -0.5 / up], 1).reshape(3, P, 16)
    c["decay"][:] = decay.transpose(1, 0, 2).reshape(P, -1)
    c["chunk_decay"][:] = np.concatenate([gamma ** P, gamma ** STEPS])
    c["iota"][:] = np.arange(64)
    rel = p[:, None] + P - np.arange(2 * P)[None, :]
    c["window"][:] = np.where((rel >= 0) & (rel < P), 0, MASKED)
    step = p % STEPS
    c["cache_mask"][:] = np.where(p[None, :] > step[:, None], 0, MASKED)
    own = (q[None, None, :] // STEPS == np.arange(BATCH_S)[None, :, None]) & (q[None, None, :] % STEPS <= step[:, None, None])
    c["new_mask"][:] = np.where(own, 0, MASKED).reshape(P, -1)
    c["before"][:] = p[:, None] < p[None, :]
    c["ones"][:] = 1
    c["of_batch"][:64] = q[:, None] // STEPS == np.arange(BATCH_S)[None, :]
    return np.concatenate([c[name] for name, _ in CONST_WIDTHS], 1)


def lay_out(x):
    x = {k: np.asarray(v) for k, v in x.items()}
    f = np.float32
    c = np.zeros((32, D), f)
    c[0:1] = x["c_prompt"]
    c[1:1 + BATCH_S] = x["c_sample"]

    def units(w):
        return w.reshape(KD, P, -1, HALF).transpose(2, 1, 0, 3).reshape(-1, P, KD * HALF)

    w_in = units(x["w_in"][0])[IN_ORDER]
    w1 = x["moe_w1"][0].reshape(NEXP, 2, 4, P, 2, D).transpose(0, 4, 1, 3, 2, 5).reshape(NEXP, 4, P, 4 * D)
    w2 = x["moe_w2"][0].reshape(NEXP, 2, 4, P, D).transpose(0, 1, 3, 2, 4).reshape(NEXP, 2, P, 4 * D)
    params = {name: np.zeros((P, width), f) for name, width in PARAM_WIDTHS}
    params["k_gain"][:] = np.tile(x["k_norm_g"][0], KVH)
    params["sinks"][:] = x["attn_sinks"][0]
    params["sink_rows"][:, 0] = np.repeat(x["attn_sinks"][0], STEPS)
    params["q_gain"][:, 0] = np.tile(x["q_norm_g"][0], 2)
    params["router_b"][:] = x["router_b"][0]
    params["mix_bias"][:] = x["gm_bs"][0].T
    params["mix_bias_s"][:] = np.tile(x["gm_bs"][0].T[:STEPS], (P // STEPS, 1))
    ws = x["gm_ws"][0].transpose(2, 0, 1)
    return {
        "c": np.ascontiguousarray(c.T.reshape(KD, P, 32).transpose(1, 0, 2)),
        "x_prompt": x["x_prompt"][0], "x_sample": x["x_sample"].reshape(-1, D),
        "consts": shape_constants(),
        "params": np.concatenate([params[name] for name, _ in PARAM_WIDTHS], 1),
        "w_dense": np.concatenate([units(x["w_ada"][0]), w_in, units(x["w_out"][0])]),
        "w_moe": np.concatenate([w1, w2], 1),
        "b_ada": x["b_ada"][0], "b1": x["moe_b1"][0].reshape(NEXP, 2, D), "b2": x["moe_b2"][0],
        "b_gate": x["b_gate"][0].reshape(3, D),
        "ln_mix_g": x["ln_mix_g"][0], "ln_ffn_g": x["ln_ffn_g"][0], "ret_norm_g": x["ret_norm_g"][0],
        "gm_ln_g": x["gm_ln_g"][0], "gm_ln_b": x["gm_ln_b"][0],
        "mixT": np.ascontiguousarray(ws),
        "mixT_s": np.ascontiguousarray(np.tile(ws[:STEPS, :, :STEPS], (BATCH_S, 1, BATCH_S))),
        "state": x["state_retention"][0],
        "cache_kT": np.ascontiguousarray(x["cache_attn_k"][0].transpose(0, 3, 2, 1)),
        "cache_v": x["cache_attn_v"][0].reshape(BATCH_S, P, KVH * HD),
        "router_w": np.ascontiguousarray(x["router_w"][0].reshape(KD, P, NEXP).transpose(1, 0, 2)),
    }


OUT_SHAPES = {
    "y_prompt": (SEQ, D), "y_sample": (BATCH_S * STEPS, D), "prompt_k": (P, KVH * HD), "prompt_v": (P, KVH * HD),
    "prompt_retention": (RH, RDK, RDV), "sample_k": (BATCH_S * STEPS, KVH * HD), "sample_v": (BATCH_S * STEPS, KVH * HD),
    "sample_retention": (BATCH_S, RH, RDK, RDV), "sample_gmlp_v": (BATCH_S * STEPS, D),
}


def kernel(**inputs):
    import concourse.bacc as bacc
    from concourse.bass_utils import run_bass_kernel_spmd

    arrays = lay_out(inputs)
    nc = bacc.Bacc("TRN2", target_bir_lowering=False, num_devices=1)
    ins = {name: nc.dram_tensor("in_" + name, a.shape, mybir.dt.from_np(a.dtype), kind="ExternalInput").ap() for name, a in arrays.items()}
    outs = {name: nc.dram_tensor("out_" + name, shape, FP32, kind="ExternalOutput").ap() for name, shape in OUT_SHAPES.items()}
    hybrid_step_kernel(nc, ins, outs)
    r = run_bass_kernel_spmd(nc, [{"in_" + name: a for name, a in arrays.items()}], core_ids=[0]).results[0]
    got = {name: r["out_" + name] for name in OUT_SHAPES}
    return (got["y_prompt"].reshape(1, SEQ, D), got["y_sample"].reshape(BATCH_S, STEPS, D),
            got["prompt_k"].reshape(1, 1, P, KVH, HD), got["prompt_v"].reshape(1, 1, P, KVH, HD),
            got["prompt_retention"].reshape(1, 1, RH, RDK, RDV),
            got["sample_k"].reshape(1, BATCH_S, STEPS, KVH, HD), got["sample_v"].reshape(1, BATCH_S, STEPS, KVH, HD),
            got["sample_retention"].reshape(1, BATCH_S, RH, RDK, RDV),
            got["sample_gmlp_v"].reshape(1, BATCH_S, STEPS, D))
```

```python
import numpy as np
import concourse.bass as bass
from concourse import mybir
from concourse.alu_op_type import AluOpType as ALU

ACT = mybir.ActivationFunctionType
AX = mybir.AxisListType
FP32 = mybir.dt.float32
I32 = mybir.dt.int32
U32 = mybir.dt.uint32

P = 128
D = 1024
KD = D // P
HALF = 512
BATCH_S, STEPS = 8, 8
SEQ = 256
TOKENS = SEQ + BATCH_S * STEPS
ROWS = [P, P, TOKENS - 2 * P]
HD, QH, KVH = 64, 16, 4
GROUP = QH // KVH
RH, RDK, RDV = 8, 64, 128
GG = 8
NEXP, TOPK = 32, 4
LIMIT = 7.0
PAST = 1024
EPS = 1e-6
MASKED = -1e30

SLOTS = 6
DENSE_SLOTS = 3
EXPERT_UNITS = 6
ADA_UNITS, IN_UNITS, OUT_UNITS = 12, 19, 2
DENSE_UNITS = ADA_UNITS + IN_UNITS + OUT_UNITS
AQ0, AQ1, AKV, CU0, CU1, CV0, CV1, RQ, RK, RV0, RV1, GA0, GA1, GC0, GC1, RG0, RG1, GB0, GB1 = range(IN_UNITS)
IN_ORDER = [0, 1, 2, 9, 10, 11, 12, 3, 4, 5, 6, 13, 14, 17, 18, 7, 8, 15, 16]
ADA_FIRST = 4
DENSE_ORDER = [("ada", 0), ("ada", 1), ("ada", 2), ("ada", 3), ("proj", AQ0), ("proj", AQ1), ("proj", AKV),
               ("ada", 4), ("ada", 5), ("ada", 6), ("proj", CU0), ("ada", 7), ("proj", CU1), ("ada", 8),
               ("ada", 9), ("proj", CV0), ("ada", 10), ("proj", CV1), ("ada", 11)]
DENSE_ORDER += [("proj", idx) for idx in range(RQ, IN_UNITS + OUT_UNITS)]


def ada_unit(n):
    return DENSE_ORDER.index(("ada", n))


def proj_unit(idx):
    return DENSE_ORDER.index(("proj", idx))


BLOCK = 64
MAX_BLOCKS = 64

CONST_WIDTHS = [("ident", 128), ("causal", 128), ("blockcausal", 64), ("select", 4 * 192),
                ("cos", 3 * 32), ("sin", 3 * 32), ("decay", 3 * 16), ("chunk_decay", 16),
                ("iota", 64), ("window", 256), ("cache_mask", 128), ("new_mask", 8 * 64),
                ("before", 128), ("ones", 128), ("of_batch", 8)]
CONST_AT = {}
CONST_COLS = 0
for _name, _width in CONST_WIDTHS:
    CONST_AT[_name] = (CONST_COLS, CONST_COLS + _width)
    CONST_COLS += _width

PARAM_WIDTHS = [("k_gain", 256), ("sinks", 16), ("sink_rows", 1), ("q_gain", 1), ("router_b", 32),
                ("mix_bias", 8), ("mix_bias_s", 8)]
PARAM_AT = {}
PARAM_COLS = 0
for _name, _width in PARAM_WIDTHS:
    PARAM_AT[_name] = (PARAM_COLS, PARAM_COLS + _width)
    PARAM_COLS += _width

AUX_FIRST, AUX_BANKS = 5, 3
AUX = [f"ada{n}" for n in range(6)] + ["kT0", "kT1", "kT2"]
for _t in range(2):
    AUX += [f"qT{_t}{q}" for q in range(4)]
    for _g in range(KVH):
        AUX += [f"sc{_t}{_g}{k}" for k in range(_t + 1)]
        AUX += [f"ada{6 + 4 * _t + _g}"] if 4 * _t + _g < 6 else []
        AUX += [f"pT{_t}{_g}{k}" for k in range(_t + 1)] + [f"pv{_t}{_g}"]
AUX += ["qT20", "qT21"]
for _b in range(BATCH_S):
    AUX += [f"sc2{_b}", f"pT2{_b}", f"pv2{_b}"]
AUX += ["oback0", "oback1"]
AUX += [f"mix{t}{h}" for t in range(3) for h in range(2)]
for _t in range(2):
    for _h in range(2):
        AUX += [f"rqT{_t}{_h}", f"rkT{_t}{_h}", f"ra{_t}{_h}", f"ro{_t}{_h}"]
    AUX += [f"rs{_t}{_h}" for _h in range(2)]
AUX += ["rqT2", "rkT2", "ra2", "ro2"]
for _b in range(BATCH_S):
    AUX += [f"ri{_b}", f"rs2{_b}0", f"rs2{_b}1"]
AUX += ["rback0", "rback1"]
AUX += [f"g1{s}{h}" for s in "ps" for h in range(2)]
AUX += [f"g2{s}{h}" for s in "ps" for h in range(2)]
AUX += ["lg0", "lg1", "lg2", "pos0", "pos1", "pos2", "cnt", "gT", "b2a0", "b2a1", "b2b0", "b2b1", "b2c0", "b2c1"]
AUX_AT = {name: n for n, name in enumerate(AUX)}


def hybrid_step_kernel(nc, ins, outs):
    from contextlib import ExitStack
    with ExitStack() as ctx:
        build(nc, ctx, ins, outs)


def build(nc, ctx, ins, outs):
    def sb(name, shape, dt=FP32):
        return ctx.enter_context(nc.sbuf_tensor(name, shape, dt))

    def sem(name):
        return ctx.enter_context(nc.semaphore(name))

    ring = sb("ring", [P, SLOTS, 4096])
    xT = sb("xT", [P, KD, TOKENS])
    R = sb("R", [P, 3, D])
    T = sb("T", [P, 3, D])
    U = sb("U", [P, 3, D])
    V = sb("V", [P, 3, D])
    W = sb("W", [P, 3, D])
    spare = ring[:, DENSE_SLOTS:SLOTS, :].rearrange("p s c -> p (s c)")
    XQK, XV, XC, XG = (spare[:, n * 3 * D:(n + 1) * 3 * D].rearrange("p (t d) -> p t d", t=3) for n in range(4))
    mod = sb("mod", [P, ADA_UNITS, 128])
    consts = sb("consts", [P, CONST_COLS])
    params = sb("params", [P, PARAM_COLS])
    stat = sb("stat", [P, 96])
    ARENA = 5888
    arena = sb("arena", [P, ARENA])
    table_i = sb("table_i", [1, MAX_BLOCKS + 1 + NEXP], I32)
    top_i = sb("top_i", [P, 8], U32)
    ps = ctx.enter_context(nc.psum_tensor("ps", [P, 8, HALF], FP32))

    def const(name):
        a, b = CONST_AT[name]
        return consts[:, a:b]

    def param(name):
        a, b = PARAM_AT[name]
        return params[:, a:b]

    ident = const("ident")
    select = const("select").rearrange("p (j m) -> p j m", j=4)
    cos = const("cos").rearrange("p (t f) -> p t f", t=3)
    sin = const("sin").rearrange("p (t f) -> p t f", t=3)
    decay = const("decay").rearrange("p (t h) -> p t h", t=3)
    new_mask = const("new_mask").rearrange("p (b k) -> p b k", b=BATCH_S)
    ones = const("ones")

    def cut(at, *shape):
        size = int(np.prod(shape))
        assert at + size <= ARENA, (at, size)
        v = arena[:, at:at + size]
        if len(shape) == 2:
            v = v.rearrange("p (a b) -> p a b", a=shape[0])
        if len(shape) == 3:
            v = v.rearrange("p (a b c) -> p a b c", a=shape[0], b=shape[1])
        return v

    silu_c = XG[:, 0, 0:KD * 32].rearrange("p (k b) -> p k b", k=KD)
    mod_bias = V[:, :, HALF:D]
    ln_gain = cut(1792, D)
    ln_ffn = cut(4096, D)
    gm_gain = cut(0, D)
    gm_bias = cut(1024, D)
    mixT = cut(2048, GG, 128)
    mixT_s = cut(3072, GG, 64)
    mix_tmp = cut(3584, D)
    gate_bias = cut(5120, HALF)
    gate_bias_a = U[:, 2, :]
    rqT = cut(0, RH, 128)
    rkT = cut(1024, RH, 128)
    ra = cut(2048, 2, HALF)
    state = cut(3072, RH, RDV)
    kd = cut(4096, HALF)
    ro_s = cut(4608, HALF)
    ret_gain = cut(0, D)
    squares = cut(1024, D)
    kTa = cut(0, KVH, TOKENS)
    probs = cut(1280, 4, 256)
    pT = cut(2304, 2, HALF)
    oT = cut(3328, QH, BATCH_S * STEPS)
    cache = cut(4352, 2, 768)
    qTa = U[:, 0:2, :].rearrange("p a d -> p (a d)").rearrange("p (h t) -> p h t", h=QH)
    qTs = U[:, 0, :].rearrange("p (b h t) -> p b h t", b=BATCH_S, h=QH)
    router_w = cut(0, KD, NEXP)
    select_e = cut(256, 3, NEXP)
    gate_e = cut(352, 3, NEXP)
    slot_of = cut(448, 3, NEXP)
    rtmp = cut(544, 3, NEXP)
    slot_base = cut(640, MAX_BLOCKS)
    expert_of = cut(704, MAX_BLOCKS)
    n_of = cut(768, NEXP)
    cum_of = cut(800, NEXP)
    pick = cut(832, 3, BLOCK)
    pick_gate = cut(1024, 3, 2, BLOCK)
    sel_now = cut(1408, 2, 3)
    xgT = cut(1536, 4, 2, BLOCK)
    actT = cut(2048, 4, 2, BLOCK)
    gateT = cut(2560, 3 * P)
    y_blk = cut(2944, HALF)
    g_cut = cut(3456, HALF)
    g_act = cut(3968, HALF)
    u_cut = cut(4480, HALF)
    h_act = cut(4992, HALF)
    b1_rows = W[:, 0, :]
    passed = W[:, 0:2, :].rearrange("p a (g e) -> p (a g) e", e=NEXP)
    b2_sb = W[:, 2, :]
    xg_s = W[:, 2, 0:HALF]
    gates_T = xT[0:NEXP, 0, :]

    unit_in = [sem(f"unit_in{s}") for s in range(SLOTS)]
    unit_used = sem("unit_used")
    c_in, x_in, consts_in, params_in, mod_bias_in, ln_mix_in = map(sem, (
        "c_in", "x_in", "consts_in", "params_in", "mod_bias_in", "ln_mix_in"))
    gm_in, gate_bias_in, ret_gain_in, ln_ffn_in, x_again_in, router_in, b2_in = map(sem, (
        "gm_in", "gate_bias_in", "ret_gain_in", "ln_ffn_in", "x_again_in", "router_in", "b2_in"))
    state_in = [sem(f"state_in{i}") for i in range(2)]
    cache_in = [sem(f"cache_in{i}") for i in range(2)]
    b1_in = [sem(f"b1_in{i}") for i in range(2)]
    stored, kv_stored, gmlp_stored, retention_stored, stat_clean, ga_used, gmlp_merged, scaled, merged = map(sem, ("stored", "kv_stored", "gmlp_stored", "retention_stored", "stat_clean", "ga_used", "gmlp_merged", "scaled", "merged"))
    silu_done, ada_biased, bcast_ready, squared, mean_sq, sqrt_done = map(sem, (
        "silu_done", "ada_biased", "bcast_ready", "squared", "mean_sq", "sqrt_done"))
    h_ready, tr_ready, xT_ready, z_ready, z_used = map(sem, ("h_ready", "tr_ready", "xT_ready", "z_ready", "z_used"))
    aux_ready = sem("aux_ready")
    aux_used = [sem(f"aux_used{i}") for i in range(AUX_BANKS)]
    dve_step, pool_step, act_step = sem("dve_step"), sem("pool_step"), sem("act_step")
    var_ready, cv_ready, mixw_ready, gmlp_done, gate_biased, gate_ready = map(sem, (
        "var_ready", "cv_ready", "mixw_ready", "gmlp_done", "gate_biased", "gate_ready"))
    roped, scores_masked, state_ready, kd_ready, inter_added, head_centred, head_squared, silu_scaled, new_state = map(sem, (
        "roped", "scores_masked", "state_ready", "kd_ready", "inter_added", "head_centred", "head_squared", "silu_scaled", "new_state"))
    state_stored = sem("state_stored")
    ret_scaled, qk_normed, max_ready, exp_done, probs_ready, v_free = map(sem, (
        "ret_scaled", "qk_normed", "max_ready", "exp_done", "probs_ready", "v_free"))
    x1_ready, top_ready, top_exp, routed, table_ready, moe_init = map(sem, (
        "x1_ready", "top_ready", "top_exp", "routed", "table_ready", "moe_init"))
    (picked, gates_picked, gathered, xg_ready, g_ready, g_cut_ready, g_act_ready, u_ready, act_ready, actT_done,
     actT_ready, gateT_done, gateT_ready, y_done, y_ready, added, final_ready, moe_step) = map(sem, (
        "picked", "gates_picked", "gathered", "xg_ready", "g_ready", "g_cut_ready", "g_act_ready", "u_ready",
        "act_ready", "actT_done", "actT_ready", "gateT_done", "gateT_ready", "y_done", "y_ready", "added",
        "final_ready", "moe_step"))
    scattered, xg_rows, turned = sem("scattered"), sem("xg_rows"), sem("turned")

    block = ctx.enter_context(nc.Block())

    def aux_bank(name):
        return ps[:, AUX_FIRST + AUX_AT[name] % AUX_BANKS, :]

    def aux_filled(eng, name):
        eng.wait_ge(aux_ready, AUX_AT[name] + 1)

    def aux_taken(eng, name):
        n = AUX_AT[name]
        eng.wait_ge(aux_used[n % AUX_BANKS], n // AUX_BANKS + 1)

    def used(name):
        return aux_used[AUX_AT[name] % AUX_BANKS]

    def unit_arrived(eng, u):
        eng.wait_ge(unit_in[u % DENSE_SLOTS], 16 * (u // DENSE_SLOTS + 1))

    def unit_consumed(eng, u):
        kind, n = DENSE_ORDER[u]
        if kind == "ada":
            eng.wait_ge(aux_ready, AUX_AT[f"ada{n}"] + 1)
        else:
            eng.wait_ge(z_ready, 3 * (n + 1))

    def z_banks(idx):
        s = idx % 2
        return [(ps[:, s, :], 0, 0, HALF), (ps[:, 2 + s, :], 1, 0, HALF),
                (ps[0:64, 4, 0:256], 2, 0, 256), (ps[64:128, 4, 0:256], 2, 256, 256)]

    TR_BANKS = [4, 5, 6, 7, 4]
    TR_NORM = [(2, 0, 8), (0, 0, 4), (0, 4, 4), (1, 0, 4), (1, 4, 4)]
    TR_MERGED = [(0, 0, 4), (0, 4, 4), (1, 0, 4), (1, 4, 4), (2, 0, 8)]

    @block.sync
    def _(sp):
        def load_unit(u):
            if u >= DENSE_SLOTS:
                unit_consumed(sp, u - DENSE_SLOTS)
            sp.dma_start(ring[:, u % DENSE_SLOTS, :], ins["w_dense"][u, :, :]).then_inc(unit_in[u % DENSE_SLOTS], 16)

        sp.dma_start(silu_c, ins["c"]).then_inc(c_in, 16)
        load_unit(0)
        sp.dma_start(R[:, 0:2, :], ins["x_prompt"].rearrange("(t p) d -> p t d", p=P)).then_inc(x_in, 16)
        sp.dma_start(R[0:64, 2, :], ins["x_sample"]).then_inc(x_in, 16)
        load_unit(1)
        sp.dma_start(consts[:, :], ins["consts"]).then_inc(consts_in, 16)
        for u in range(2, DENSE_UNITS):
            load_unit(u)

        for j in (0, 3, 4, 5, 1, 2):
            if j < DENSE_SLOTS:
                unit_consumed(sp, DENSE_UNITS - DENSE_SLOTS + j)
            elif j == DENSE_SLOTS:
                sp.wait_ge(merged, 3)
            sp.dma_start(ring[:, j, :], ins["w_moe"][0, j, :, :]).then_inc(unit_in[j], 16)
        sp.wait_ge(table_ready, 1)
        for n in range(2):
            sp.dma_start(W[0:1, n, :], ins["b1"][0:1, n, :]).then_inc(b1_in[n], 16)
        with sp.Fori(1, NEXP) as e:
            before = sp.value_load(table_i[0:1, bass.ds(MAX_BLOCKS + 1 + e, 1)], min_val=1, max_val=MAX_BLOCKS)
            for j in range(EXPERT_UNITS):
                sp.wait_ge(unit_used, EXPERT_UNITS * before + j)
                sp.dma_start(ring[:, j, :], ins["w_moe"][bass.ds(e, 1), j, :, :].rearrange("a p n -> p (a n)")).then_inc(unit_in[j], 16)
                if j in (1, 3):
                    sp.dma_start(W[0:1, j // 2, :], ins["b1"][bass.ds(e, 1), j // 2, :]).then_inc(b1_in[j // 2], 16)
        sp.wait_ge(final_ready, 3)
        sp.dma_start(outs["y_prompt"].rearrange("(t p) d -> p t d", p=P), R[:, 0:2, :]).then_inc(stored, 16)
        sp.dma_start(outs["y_sample"], R[0:64, 2, :]).then_inc(stored, 16)
        sp.wait_ge(stored, 32)
        sp.wait_ge(kv_stored, 64)
        sp.wait_ge(gmlp_stored, 16)
        sp.wait_ge(retention_stored, 16)
        sp.wait_ge(state_stored, 16 * BATCH_S)


    @block.gpsimd
    def _(pool):
        bias_v = ins["b_ada"].rearrange("(m n j c) -> j m n c", m=3, j=4, c=128)
        for j in range(4):
            for m in range(3):
                pool.dma_start(mod_bias[32 * j:32 * j + 32, m, :].rearrange("p (n c) -> p n c", n=4),
                               bias_v[j, m].partition_broadcast(32)).then_inc(mod_bias_in, 16)
        pool.dma_start(ln_gain, ins["ln_mix_g"].partition_broadcast(P)).then_inc(ln_mix_in, 16)
        pool.dma_start(params[:, :], ins["params"]).then_inc(params_in, 16)
        pool.dma_start(gate_bias_a, ins["b_gate"][0].partition_broadcast(P)).then_inc(gate_bias_in, 16)

        def load_cache(b):
            pool.dma_start(cache[0:64, b % 2, 0:512].rearrange("p (h r) -> p h r", h=KVH), ins["cache_kT"][b]).then_inc(cache_in[b % 2], 16)
            pool.dma_start(cache[:, b % 2, 512:768], ins["cache_v"][b]).then_inc(cache_in[b % 2], 16)

        for b in range(2):
            load_cache(b)
        pool.wait_ge(qk_normed, 3)
        pool.dma_start(outs["prompt_k"], V[:, 1, 0:256]).then_inc(kv_stored, 16)
        pool.dma_start(outs["prompt_v"], V[:, 1, 256:512]).then_inc(kv_stored, 16)
        pool.dma_start(outs["sample_k"], V[0:64, 2, 0:256]).then_inc(kv_stored, 16)
        pool.dma_start(outs["sample_v"], V[0:64, 2, 256:512]).then_inc(kv_stored, 16)
        for b in range(2, BATCH_S):
            aux_filled(pool, f"pv2{b - 2}")
            load_cache(b)

        aux_filled(pool, "oback1")
        pool.dma_start(gm_gain, ins["gm_ln_g"].partition_broadcast(P)).then_inc(gm_in, 16)
        pool.dma_start(gm_bias, ins["gm_ln_b"].partition_broadcast(P)).then_inc(gm_in, 16)
        pool.dma_start(mixT, ins["mixT"]).then_inc(gm_in, 16)
        pool.dma_start(mixT_s[0:64], ins["mixT_s"]).then_inc(gm_in, 16)

        def load_gate_bias(row, half):
            pool.dma_start(gate_bias, ins["b_gate"][row, HALF * half:HALF * half + HALF].partition_broadcast(P)).then_inc(gate_bias_in, 16)

        def add_gate_bias(buf, half, chunk, n):
            pool.wait_ge(gate_bias_in, 16 * n)
            pool.wait_ge(z_used, 4 * (chunk + 1))
            for t, r in enumerate(ROWS):
                v = buf[0:r, t, HALF * half:HALF * half + HALF]
                nc.gpsimd.tensor_tensor(v, v, gate_bias[0:r], ALU.add).then_inc(gate_biased, 1)
            pool.wait_ge(gate_biased, 3 * n)

        def load_state(b):
            pool.dma_start(V[0:64, b % 2, :].rearrange("p (h e) -> p h e", h=RH),
                           ins["state"][b].rearrange("h d e -> d h e")).then_inc(state_in[b % 2], 16)

        pool.wait_ge(gate_bias_in, 16)
        load_gate_bias(2, 0)
        pool.wait_ge(kv_stored, 64)
        for b in range(2):
            load_state(b)
        pool.wait_ge(gm_in, 64)
        pool.wait_ge(consts_in, 16)
        nc.gpsimd.tensor_tensor(mixT, mixT, const("causal").unsqueeze(1).to_broadcast([P, GG, 128]), ALU.mult).then_inc(mixw_ready, 1)
        nc.gpsimd.tensor_tensor(mixT_s[0:64], mixT_s[0:64], const("blockcausal")[0:64].unsqueeze(1).to_broadcast([64, GG, 64]), ALU.mult).then_inc(mixw_ready, 1)
        pool.wait_ge(z_used, 4 * (GA1 + 1))
        for t, r in enumerate(ROWS):
            nc.gpsimd.tensor_tensor(XG[0:r, t, :], XG[0:r, t, :], gate_bias_a[0:r], ALU.add).then_inc(gate_biased, 1)
        pool.wait_ge(cv_ready, 3)
        pool.dma_start(outs["sample_gmlp_v"], XC[0:64, 2, :]).then_inc(gmlp_stored, 16)
        add_gate_bias(R, 0, GC0, 2)
        load_gate_bias(2, 1)
        add_gate_bias(R, 1, GC1, 3)
        load_gate_bias(1, 0)
        for b in range(BATCH_S):
            if b >= 2:
                pool.wait_ge(new_state, 2 * (b - 1))
                load_state(b)
            if b == 0:
                pool.wait_ge(roped, 3)
            else:
                aux_filled(pool, f"rs2{b - 1}1")
            nc.gpsimd.tensor_scalar(kd[0:64], XQK[0:64, 2, HALF:D], const("of_batch")[0:64, b:b + 1], None, ALU.mult).then_inc(kd_ready, 1)
            if b >= 1:
                pool.wait_ge(new_state, 2 * b)
                pool.dma_start(outs["sample_retention"][b - 1].rearrange("h d e -> d h e"),
                               V[0:64, 2, :].rearrange("p (h e) -> p h e", h=RH)).then_inc(state_stored, 16)
        pool.wait_ge(new_state, 2 * BATCH_S)
        pool.dma_start(outs["sample_retention"][BATCH_S - 1].rearrange("h d e -> d h e"),
                       V[0:64, 2, :].rearrange("p (h e) -> p h e", h=RH)).then_inc(state_stored, 16)
        pool.dma_start(ret_gain, ins["ret_norm_g"].partition_broadcast(P)).then_inc(ret_gain_in, 16)
        pool.dma_start(outs["prompt_retention"].rearrange("h d e -> d h e"), state[0:64]).then_inc(retention_stored, 16)
        add_gate_bias(XC, 0, GB0, 4)
        load_gate_bias(1, 1)
        pool.wait_ge(z_used, 4 * (RG1 + 1))
        pool.wait_ge(ret_gain_in, 16)
        for t, r in enumerate(ROWS):
            nc.gpsimd.tensor_tensor(XG[0:r, t, :], XG[0:r, t, :], ret_gain[0:r], ALU.mult).then_inc(silu_scaled, 1)
        add_gate_bias(XC, 1, GB1, 5)
        pool.wait_ge(gmlp_merged, 3)
        pool.dma_start(R[:, 0:2, :], ins["x_prompt"].rearrange("(t p) d -> p t d", p=P)).then_inc(x_again_in, 16)
        pool.dma_start(R[0:64, 2, :], ins["x_sample"]).then_inc(x_again_in, 16)
        pool.wait_ge(merged, 3)
        pool.dma_start(ln_ffn, ins["ln_ffn_g"].partition_broadcast(P)).then_inc(ln_ffn_in, 16)
        pool.dma_start(router_w, ins["router_w"]).then_inc(router_in, 16)
        pool.wait_ge(h_ready, 6)
        pool.dma_start(b2_sb[0:NEXP], ins["b2"]).then_inc(b2_in, 16)

    @block.scalar
    def _(act):
        A = nc.scalar.activation

        def sqrt_of(cols, n, r=P):
            act.wait_ge(mean_sq, n)
            A(cols, cols, ACT.Sqrt).then_inc(sqrt_done, 1)

        def take_transposed(n, parts):
            for q, (t, k0, nk) in enumerate(parts):
                act.wait_ge(tr_ready, 5 * n + q + 1)
                r = ROWS[t]
                A(xT[:, k0:k0 + nk, t * P:t * P + r], ps[:, TR_BANKS[q], :].rearrange("p (k m) -> p k m", m=r), ACT.Copy).then_inc(xT_ready, 1)

        into = {AQ0: (R, 0, ACT.Copy), AQ1: (R, HALF, ACT.Copy), AKV: (V, 0, ACT.Copy),
                CU0: (W, 0, ACT.Gelu_apprx_tanh), CU1: (W, HALF, ACT.Gelu_apprx_tanh),
                CV0: (XC, 0, ACT.Gelu_apprx_tanh), CV1: (XC, HALF, ACT.Gelu_apprx_tanh),
                RQ: (XQK, 0, ACT.Copy), RK: (XQK, HALF, ACT.Copy), RV0: (XV, 0, ACT.Copy), RV1: (XV, HALF, ACT.Copy),
                GA0: (XG, 0, ACT.Copy), GA1: (XG, HALF, ACT.Copy), GC0: (R, 0, ACT.Copy), GC1: (R, HALF, ACT.Copy),
                RG0: (XG, 0, ACT.Silu), RG1: (XG, HALF, ACT.Silu), GB0: (XC, 0, ACT.Copy), GB1: (XC, HALF, ACT.Copy),
                IN_UNITS: (W, 0, ACT.Copy), IN_UNITS + 1: (W, HALF, ACT.Copy)}
        z_pieces = iter(range(3 * (IN_UNITS + OUT_UNITS)))

        def take_pieces(count):
            for _ in range(count):
                n = next(z_pieces)
                idx, t = divmod(n, 3)
                buf, c0, func = into[idx]
                if n == 3 * RG0:
                    act.wait_ge(ga_used, 3)
                if n == 3 * GB0:
                    act.wait_ge(gmlp_stored, 16)
                for src, tile, c, w in z_banks(idx):
                    if tile == t:
                        act.wait_ge(z_ready, n + 1)
                        A(buf[0:ROWS[t], t, c0 + c:c0 + c + w], src, func).then_inc(z_used, 1)

        def gate(buf, biased, per_tile):
            for t, r in enumerate(ROWS):
                act.wait_ge(gate_biased, biased + t + 1)
                A(buf[0:r, t, :], buf[0:r, t, :], ACT.Sigmoid).then_inc(gate_ready, 1)

        act.wait_ge(c_in, 16)
        A(silu_c, silu_c, ACT.Silu).then_inc(silu_done, 1)
        act.wait_ge(x_in, 32)
        act.wait_ge(stat_clean, 1)
        for t in (2, 0, 1):
            A(W[0:ROWS[t], t, :], R[0:ROWS[t], t, :], ACT.Square, accum_out=stat[0:ROWS[t], t:t + 1]).then_inc(squared, 1)
        sqrt_of(stat[:, 0:3], 1)
        take_transposed(0, TR_NORM)
        take_pieces(9)
        for t in range(3):
            sqrt_of(stat[:, 24:44], 2 + t)

        def take_kT(t):
            name = f"kT{t}"
            aux_filled(act, name)
            A(kTa[0:64, :, t * P:t * P + ROWS[t]], aux_bank(name)[0:64, 0:4 * ROWS[t]].rearrange("p (h m) -> p h m", h=4), ACT.Copy).then_inc(used(name), 1)

        def take_qT(t):
            n = 2 if t == 2 else 4
            for q in range(n):
                name = f"qT{t}{q}"
                aux_filled(act, name)
                heads = slice(q * (QH // n), (q + 1) * (QH // n))
                if t == 2:
                    dst = qTs[0:64].rearrange("p b h t -> p h b t")[:, heads]
                    src = aux_bank(name)[0:64].rearrange("p (h b t) -> p h b t", b=BATCH_S, t=STEPS)
                else:
                    dst = qTa[0:64, heads, :]
                    src = aux_bank(name)[0:64].rearrange("p (h m) -> p h m", m=P)
                A(dst, src, ACT.Copy, scale=param("q_gain")[0:64]).then_inc(used(name), 1)

        softmaxes = [0]

        def softmax(count, width):
            softmaxes[0] += 1
            act.wait_ge(max_ready, softmaxes[0])
            for h in range(count):
                A(probs[:, h, 0:width], probs[:, h, 0:width], ACT.Exp, bias=stat[:, 48 + h:49 + h], accum_out=stat[:, 52 + h:53 + h])
            A(stat[:, 56:56 + count], stat[:, 60:60 + count], ACT.Exp).then_inc(exp_done, 1)

        for t in range(3):
            take_kT(t)
        for t in range(2):
            take_qT(t)
            for g in range(KVH):
                softmax(4, P * (t + 1))
                take_pieces(2)
                for k in range(t + 1):
                    name = f"pT{t}{g}{k}"
                    aux_filled(act, name)
                    A(pT[:, k, :], aux_bank(name), ACT.Copy).then_inc(used(name), 1)
        take_qT(2)
        for b in range(BATCH_S):
            softmax(1, 192)
            take_pieces(1)
            name = f"pT2{b}"
            aux_filled(act, name)
            A(pT[0:64, 1, 0:P], aux_bank(name)[0:64, P:2 * P], ACT.Copy)
            A(pT[:, 0, 0:P], aux_bank(name)[:, 0:P], ACT.Copy).then_inc(used(name), 1)
            name = f"pv2{b}"
            aux_filled(act, name)
            A(oT[0:64, :, b * STEPS:(b + 1) * STEPS], aux_bank(name)[0:64, 0:P].rearrange("p (h t) -> p h t", h=QH), ACT.Copy).then_inc(used(name), 1)
        for h in range(2):
            name = f"oback{h}"
            aux_filled(act, name)
            A(T[0:64, 2, HALF * h:HALF * h + HALF], aux_bank(name)[0:64], ACT.Copy).then_inc(used(name), 1)
        sqrt_of(stat[:, 8:11], 5)
        take_pieces(6)
        gate(XG, 0, 1)
        for t in range(2):
            for h in range(2):
                for src, dst in (("rqT", rqT), ("rkT", rkT)):
                    name = f"{src}{t}{h}"
                    aux_filled(act, name)
                    A(dst[0:64, 4 * h:4 * h + 4, :], aux_bank(name)[0:64].rearrange("p (h m) -> p h m", h=4), ACT.Copy).then_inc(used(name), 1)
                take_pieces(2)
                name = f"ro{t}{h}"
                aux_filled(act, name)
                A(U[:, t, HALF * h:HALF * h + HALF], aux_bank(name), ACT.Copy).then_inc(used(name), 1)
        for name, dst in (("rqT2", rqT), ("rkT2", rkT)):
            aux_filled(act, name)
            A(dst[0:64, :, 0:64], aux_bank(name)[0:64].rearrange("p (h m) -> p h m", h=8), ACT.Copy).then_inc(used(name), 1)
        take_pieces(2)
        aux_filled(act, "ro2")
        A(ro_s, aux_bank("ro2"), ACT.Copy).then_inc(used("ro2"), 1)
        gate(R, 6, 1)
        take_pieces(8)
        for h in range(2):
            name = f"rback{h}"
            aux_filled(act, name)
            A(U[0:64, 2, HALF * h:HALF * h + HALF], aux_bank(name)[0:64], ACT.Copy).then_inc(used(name), 1)
        for t, r in enumerate(ROWS):
            act.wait_ge(head_centred, t + 1)
            if t:
                act.wait_ge(mean_sq, 5 + t)
            A(squares[0:r], U[0:r, t, :], ACT.Square).then_inc(head_squared, 1)
            sqrt_of(stat[:, 16:24], 6 + t)
            if t == 0:
                gate(XC, 12, 1)
        take_transposed(1, TR_MERGED)
        act.wait_ge(state_stored, 16 * BATCH_S)
        for s, rows, t in (("p", P, 0), ("s", 64, 2)):
            for h in range(2):
                name = f"g1{s}{h}"
                aux_filled(act, name)
                A(V[0:rows, t, HALF * h:HALF * h + HALF], aux_bank(name)[0:rows], ACT.Copy).then_inc(used(name), 1)
        take_pieces(6)
        for t in (2, 0, 1):
            act.wait_ge(x1_ready, {2: 1, 0: 2, 1: 3}[t])
            A(W[0:ROWS[t], t, :], R[0:ROWS[t], t, :], ACT.Square, accum_out=stat[0:ROWS[t], t:t + 1]).then_inc(squared, 1)
        sqrt_of(stat[:, 0:3], 9)
        take_transposed(2, TR_NORM)
        for s, rows, t in (("p", P, 0), ("s", 64, 2)):
            for h in range(2):
                name = f"g2{s}{h}"
                aux_filled(act, name)
                A(V[0:rows, t, HALF * h:HALF * h + HALF], aux_bank(name)[0:rows], ACT.Copy).then_inc(used(name), 1)
        for t in range(3):
            act.wait_ge(top_ready, t + 1)
            A(stat[:, 72:76], stat[:, 64:68], ACT.Exp, bias=stat[:, 76:77], accum_out=stat[:, 77:78]).then_inc(top_exp, 1)
        aux_filled(act, "gT")
        A(gates_T[:, 0:TOKENS], aux_bank("gT")[0:NEXP, 0:TOKENS], ACT.Copy).then_inc(used("gT"), 1)
        for t, r in enumerate(ROWS):
            for h in range(2):
                name = f"b2{'abc'[t]}{h}"
                aux_filled(act, name)
                A(U[0:r, t, HALF * h:HALF * h + HALF], aux_bank(name)[0:r], ACT.Copy).then_inc(used(name), 1)

        def take_gathered(i):
            act.wait_ge(gathered, i)
            A(xg_s, ps[:, 3, :], ACT.Copy).then_inc(xg_rows, 1)

        def take_turned(i):
            act.wait_ge(turned, i)
            A(xgT, ps[:, 3, :].rearrange("p (c a s) -> p c a s", c=4, a=2), ACT.Copy).then_inc(xg_ready, 1)

        take_gathered(1)
        take_turned(1)
        act.wait_ge(moe_init, 1)
        act.sem_inc(y_ready, 1)
        act.sem_inc(gateT_ready, 1)
        n_blocks = act.value_load(table_i[0:1, MAX_BLOCKS:MAX_BLOCKS + 1], min_val=NEXP, max_val=MAX_BLOCKS - 1)
        with act.Fori(1, n_blocks + 1) as i:
            act.wait_ge(g_cut_ready, i)
            A(g_act, g_cut, ACT.Gelu_apprx_sigmoid).then_inc(g_act_ready, 1)
            take_gathered(i + 1)
            act.wait_ge(actT_done, i)
            A(actT, ps[:, 4, :].rearrange("p (c a s) -> p c a s", c=4, a=2), ACT.Copy).then_inc(actT_ready, 1)
            act.wait_ge(gateT_done, i)
            act.wait_ge(scattered, 3 * i)
            A(gateT[:, 0:TOKENS], ps[:, 5, 0:TOKENS], ACT.Copy).then_inc(gateT_ready, 1)
            take_turned(i + 1)
            act.wait_ge(unit_used, EXPERT_UNITS * i + 5)
            A(y_blk, ps[:, 2, :], ACT.Copy).then_inc(y_ready, 1)

    @block.vector
    def _(dve):
        X = nc.vector
        counts = {}

        def done(ins, signal=dve_step):
            counts[signal.name] = counts.get(signal.name, 0) + 1
            ins.then_inc(signal, 1)
            dve.wait_ge(signal, counts[signal.name])

        def rows(v, r, *shape):
            return v[0:r].to_broadcast([r, *shape])

        done(X.memset(stat[:, :], 1.0), stat_clean)
        def add_ada_bias(n):
            name = f"ada{n}"
            aux_filled(dve, name)
            X.tensor_tensor(mod[:, n, :], aux_bank(name)[:, 0:128], mod_bias[:, n // 4, 128 * (n % 4):128 * (n % 4) + 128], ALU.add).then_inc(used(name), 1)

        dve.wait_ge(mod_bias_in, 16 * 12)
        for n in range(ADA_FIRST):
            add_ada_bias(n)

        def root_mean_square(n):
            done(X.tensor_scalar(stat[:, 0:3], stat[:, 0:3], 1.0 / D, EPS, ALU.mult, ALU.add), mean_sq)
            dve.wait_ge(sqrt_done, n)
            done(X.reciprocal(stat[:, 4:7], stat[:, 0:3]))

        def modulated(gain, n):
            for q, t in enumerate((2, 0, 1)):
                r = ROWS[t]
                base = 4 if t == 2 else 0
                done(X.scalar_tensor_tensor(out=W[0:r, t, :], in0=R[0:r, t, :], scalar=stat[0:r, 4 + t:5 + t], in1=gain[0:r], op0=ALU.mult, op1=ALU.mult))
                if q < 2:
                    dve.wait_ge(bcast_ready, 2 * n + q + 1)
                scale = ps[0:r, base:base + 2, :].rearrange("p a b -> p (a b)")
                shift = ps[0:r, base + 2:base + 4, :].rearrange("p a b -> p (a b)")
                done(X.scalar_tensor_tensor(out=W[0:r, t, :], in0=scale, scalar=1.0, in1=W[0:r, t, :], op0=ALU.add, op1=ALU.mult))
                done(X.tensor_tensor(T[0:r, t, :], W[0:r, t, :], shift, ALU.add), h_ready)

        dve.wait_ge(squared, 3)
        root_mean_square(1)
        dve.wait_ge(ln_mix_in, 16)
        modulated(ln_gain, 0)

        dve.wait_ge(params_in, 16)
        for t, r in enumerate(ROWS):
            dve.wait_ge(z_used, 4 * AKV + (1, 2, 4)[t])
            q3 = R[0:r, t, :].rearrange("p (h e) -> p h e", h=QH)
            k3 = V[0:r, t, 0:256].rearrange("p (h e) -> p h e", h=KVH)
            sq = T[0:r, 1, :]
            done(X.tensor_tensor(sq, R[0:r, t, :], R[0:r, t, :], ALU.mult))
            done(X.tensor_reduce(stat[0:r, 24:40], sq.rearrange("p (h e) -> p h e", h=QH), AX.X, ALU.add))
            done(X.tensor_tensor(sq[:, 0:256], V[0:r, t, 0:256], V[0:r, t, 0:256], ALU.mult))
            done(X.tensor_reduce(stat[0:r, 40:44], sq[:, 0:256].rearrange("p (h e) -> p h e", h=KVH), AX.X, ALU.add))
            done(X.tensor_scalar(stat[0:r, 24:40], stat[0:r, 24:40], HD * EPS, None, ALU.add))
            done(X.tensor_scalar(stat[0:r, 40:44], stat[0:r, 40:44], 1.0 / HD, EPS, ALU.mult, ALU.add), mean_sq)
            dve.wait_ge(sqrt_done, 2 + t)
            done(X.reciprocal(stat[0:r, 24:44], stat[0:r, 24:44]))
            done(X.tensor_tensor(q3, q3, stat[0:r, 24:40].unsqueeze(2).to_broadcast([r, QH, HD]), ALU.mult))
            done(X.tensor_tensor(k3, k3, stat[0:r, 40:44].unsqueeze(2).to_broadcast([r, KVH, HD]), ALU.mult))
            done(X.tensor_tensor(V[0:r, t, 0:256], V[0:r, t, 0:256], param("k_gain")[0:r], ALU.mult), qk_normed)
            if t < 2:
                add_ada_bias(4 + t)

        softmaxes = [0]

        def softmax(count, width, sink, ada=None):
            softmaxes[0] += 1
            done(X.tensor_reduce(stat[:, 60:60 + count], probs[:, 0:count, 0:width], AX.X, ALU.max))
            done(X.tensor_tensor(stat[:, 60:60 + count], stat[:, 60:60 + count], sink, ALU.max))
            done(X.tensor_scalar(stat[:, 48:48 + count], stat[:, 60:60 + count], -1.0, None, ALU.mult))
            done(X.tensor_tensor(stat[:, 60:60 + count], sink, stat[:, 60:60 + count], ALU.subtract), max_ready)
            if ada is not None:
                add_ada_bias(ada)
            dve.wait_ge(exp_done, softmaxes[0])
            done(X.tensor_tensor(stat[:, 52:52 + count], stat[:, 52:52 + count], stat[:, 56:56 + count], ALU.add))
            done(X.reciprocal(stat[:, 68:68 + count], stat[:, 52:52 + count]))
            done(X.tensor_tensor(probs[:, 0:count, 0:width], probs[:, 0:count, 0:width],
                                 stat[:, 68:68 + count].unsqueeze(2).to_broadcast([P, count, width]), ALU.mult), probs_ready)

        window = const("window")
        for t in range(2):
            for g in range(KVH):
                if t == 0:
                    name = f"sc0{g}0"
                    aux_filled(dve, name)
                    X.tensor_tensor(probs[:, :, 0:P], aux_bank(name).rearrange("p (h k) -> p h k", h=4),
                                    window[:, P:2 * P].unsqueeze(1).to_broadcast([P, 4, P]), ALU.add).then_inc(used(name), 1)
                    aux_taken(dve, name)
                else:
                    for k in range(2):
                        name = f"sc1{g}{k}"
                        aux_filled(dve, name)
                        X.tensor_tensor(probs[:, 2 * k:2 * k + 2, :], aux_bank(name).rearrange("p (h k) -> p h k", h=2),
                                        window.unsqueeze(1).to_broadcast([P, 2, 2 * P]), ALU.add).then_inc(used(name), 1)
                        aux_taken(dve, name)
                softmax(4, P * (t + 1), param("sinks")[:, 4 * g:4 * g + 4], 6 + 4 * t + g if 4 * t + g < 6 else None)
                name = f"pv{t}{g}"
                aux_filled(dve, name)
                X.tensor_copy(T[:, t, 256 * g:256 * g + 256], aux_bank(name)[:, 0:256]).then_inc(used(name), 1)
                aux_taken(dve, name)
        for b in range(BATCH_S):
            name = f"sc2{b}"
            aux_filled(dve, name)
            done(X.tensor_tensor(probs[:, 0, 0:P], aux_bank(name)[:, 0:P], const("cache_mask"), ALU.add))
            X.tensor_tensor(probs[:, 0, P:192], aux_bank(name)[:, P:192], new_mask[:, b, :], ALU.add).then_inc(used(name), 1)
            aux_taken(dve, name)
            softmax(1, 192, param("sink_rows"))
        stats6 = stat[:, 80:92].rearrange("p (a b) -> p a b", a=2)
        dve.wait_ge(z_used, 4 * (CV1 + 1))
        for t, r in enumerate(ROWS):
            for h in range(2):
                done(X.bn_stats(stats6[0:r, h, :], XC[0:r, t, HALF * h:HALF * h + HALF]))
            done(X.bn_aggr(stat[0:r, 92:94], stats6[0:r]))
            done(X.tensor_copy(stat[0:r, 12 + t:13 + t], stat[0:r, 92:93]))
            done(X.tensor_scalar(stat[0:r, 8 + t:9 + t], stat[0:r, 93:94], EPS, None, ALU.add), mean_sq if t == 2 else dve_step)
        dve.wait_ge(sqrt_done, 5)
        done(X.reciprocal(stat[:, 8:11], stat[:, 8:11]))
        dve.wait_ge(gm_in, 64)
        for t, r in enumerate(ROWS):
            done(X.tensor_scalar(XC[0:r, t, :], XC[0:r, t, :], stat[0:r, 12 + t:13 + t], stat[0:r, 8 + t:9 + t], ALU.subtract, ALU.mult))
            done(X.tensor_tensor(XC[0:r, t, :], XC[0:r, t, :], gm_gain[0:r], ALU.mult))
            done(X.tensor_tensor(XC[0:r, t, :], XC[0:r, t, :], gm_bias[0:r], ALU.add), cv_ready)
        for t, r in enumerate(ROWS):
            bias = param("mix_bias_s" if t == 2 else "mix_bias")
            for h in range(2):
                name = f"mix{t}{h}"
                aux_filled(dve, name)
                tmp = mix_tmp[0:r, 0:HALF]
                X.tensor_tensor(tmp.rearrange("p (g c) -> p g c", g=4), aux_bank(name)[0:r].rearrange("p (g c) -> p g c", g=4),
                                bias[0:r, 4 * h:4 * h + 4].unsqueeze(2).to_broadcast([r, 4, 128]), ALU.add).then_inc(used(name), 1)
                aux_taken(dve, name)
                done(X.tensor_tensor(W[0:r, t, HALF * h:HALF * h + HALF], W[0:r, t, HALF * h:HALF * h + HALF], tmp, ALU.mult))

        dve.wait_ge(z_used, 4 * (RV1 + 1))
        for t, r in enumerate(ROWS):
            v = XQK[0:r, t, :].rearrange("p (h a f) -> p h a f", h=16, a=2)
            x1, x2 = v[:, :, 0, :], v[:, :, 1, :]
            c = cos[0:r, t, :].unsqueeze(1).to_broadcast([r, 16, 32])
            s = sin[0:r, t, :].unsqueeze(1).to_broadcast([r, 16, 32])
            tm = U[0:r, 0, :]
            ta = tm[:, 0:512].rearrange("p (h f) -> p h f", h=16)
            tb = tm[:, 512:1024].rearrange("p (h f) -> p h f", h=16)
            done(X.tensor_tensor(ta, x1, s, ALU.mult))
            done(X.tensor_tensor(tb, x2, s, ALU.mult))
            done(X.tensor_tensor(x1, x1, c, ALU.mult))
            done(X.tensor_tensor(x2, x2, c, ALU.mult))
            done(X.tensor_tensor(x1, x1, tb, ALU.subtract))
            done(X.tensor_tensor(x2, x2, ta, ALU.add))
            full = XQK[0:r, t, :].rearrange("p (h f) -> p h f", h=16)
            done(X.tensor_tensor(full, full, decay[0:r, t, :].unsqueeze(2).to_broadcast([r, 16, 64]), ALU.mult), roped)
        aux_taken(dve, "oback0")
        aux_taken(dve, "oback1")
        for t, r in enumerate(ROWS):
            dve.wait_ge(gate_ready, t + 1)
            done(X.tensor_tensor(T[0:r, t, :], T[0:r, t, :], XG[0:r, t, :], ALU.mult), ga_used)

        causal4 = const("causal").unsqueeze(1).to_broadcast([P, 4, 128])
        for t in range(2):
            for h in range(2):
                name = f"ra{t}{h}"
                aux_filled(dve, name)
                X.tensor_tensor(ra[:, h, :].rearrange("p (h m) -> p h m", h=4), aux_bank(name).rearrange("p (h m) -> p h m", h=4), causal4, ALU.mult).then_inc(used(name), 1)
            for h in range(2):
                name = f"rs{t}{h}"
                aux_filled(dve, name)
                st = state[0:64, 4 * h:4 * h + 4, :]
                src = aux_bank(name)[0:64].rearrange("p (h m) -> p h m", h=4)
                dec = const("chunk_decay")[0:64, 4 * h:4 * h + 4].unsqueeze(2).to_broadcast([64, 4, RDV])
                if t == 0:
                    X.tensor_tensor(st, src, dec, ALU.mult).then_inc(used(name), 1)
                else:
                    X.tensor_tensor(st, src, st, ALU.add).then_inc(used(name), 1)
                    aux_taken(dve, name)
                    done(X.tensor_tensor(st, st, dec, ALU.mult), state_ready)
        aux_filled(dve, "ra2")
        X.tensor_tensor(ra[0:64, 0, :].rearrange("p (h m) -> p h m", h=8), aux_bank("ra2")[0:64].rearrange("p (h m) -> p h m", h=8),
                        const("blockcausal")[0:64].unsqueeze(1).to_broadcast([64, 8, 64]), ALU.mult).then_inc(used("ra2"), 1)
        aux_taken(dve, "ro2")
        for b in range(BATCH_S):
            if b:
                dve.wait_ge(state_stored, 16 * b)
            name = f"ri{b}"
            aux_filled(dve, name)
            mine = ro_s.rearrange("p (h t) -> p h t", h=RH)[:, :, b * STEPS:(b + 1) * STEPS]
            X.tensor_tensor(mine, aux_bank(name)[:, 0:64].rearrange("p (h t) -> p h t", h=RH), mine, ALU.add).then_inc(used(name), 1)
            for h in range(2):
                name = f"rs2{b}{h}"
                aux_filled(dve, name)
                st = V[0:64, b % 2, HALF * h:HALF * h + HALF]
                new = V[0:64, 2, HALF * h:HALF * h + HALF]
                X.tensor_tensor(new, aux_bank(name)[0:64], st, ALU.add).then_inc(used(name), 1)
                aux_taken(dve, name)
                n4 = new.rearrange("p (h e) -> p h e", h=4)
                done(X.tensor_tensor(n4, n4, const("chunk_decay")[0:64, 8 + 4 * h:12 + 4 * h].unsqueeze(2).to_broadcast([64, 4, RDV]), ALU.mult), new_state)
        for t, r in enumerate(ROWS):
            dve.wait_ge(gate_ready, 3 + t + 1)
            done(X.tensor_tensor(W[0:r, t, :], W[0:r, t, :], R[0:r, t, :], ALU.mult))
            done(X.tensor_tensor(T[0:r, t, :], T[0:r, t, :], W[0:r, t, :], ALU.add), gmlp_merged)

        aux_taken(dve, "rback0")
        aux_taken(dve, "rback1")
        for t, r in enumerate(ROWS):
            o3 = U[0:r, t, :].rearrange("p (h e) -> p h e", h=RH)
            done(X.tensor_reduce(stat[0:r, 16:24], o3, AX.X, ALU.add))
            done(X.tensor_scalar(stat[0:r, 16:24], stat[0:r, 16:24], 1.0 / RDV, None, ALU.mult))
            done(X.tensor_tensor(o3, o3, stat[0:r, 16:24].unsqueeze(2).to_broadcast([r, RH, RDV]), ALU.subtract), head_centred)
            dve.wait_ge(head_squared, t + 1)
            done(X.tensor_reduce(stat[0:r, 16:24], squares[0:r].rearrange("p (h e) -> p h e", h=RH), AX.X, ALU.add))
            done(X.tensor_scalar(stat[0:r, 16:24], stat[0:r, 16:24], 1.0 / RDV, EPS, ALU.mult, ALU.add), mean_sq)
            dve.wait_ge(sqrt_done, 6 + t)
            done(X.reciprocal(stat[0:r, 16:24], stat[0:r, 16:24]))
            done(X.tensor_tensor(o3, o3, stat[0:r, 16:24].unsqueeze(2).to_broadcast([r, RH, RDV]), ALU.mult))
            dve.wait_ge(silu_scaled, t + 1)
            done(X.tensor_tensor(U[0:r, t, :], U[0:r, t, :], XG[0:r, t, :], ALU.mult), ret_scaled)
            dve.wait_ge(gate_ready, 6 + t + 1)
            done(X.tensor_tensor(U[0:r, t, :], U[0:r, t, :], XC[0:r, t, :], ALU.mult))
            done(X.tensor_tensor(T[0:r, t, :], T[0:r, t, :], U[0:r, t, :], ALU.add), merged)

        dve.wait_ge(x_again_in, 32)
        dve.wait_ge(z_used, 4 * (IN_UNITS + 2))
        for name in ("g1p0", "g1p1", "g1s0", "g1s1"):
            aux_taken(dve, name)
        for t in (2, 0, 1):
            r = ROWS[t]
            done(X.tensor_tensor(W[0:r, t, :], W[0:r, t, :], V[0:r, 2 if t == 2 else 0, :], ALU.mult))
            done(X.tensor_tensor(R[0:r, t, :], R[0:r, t, :], W[0:r, t, :], ALU.add), x1_ready)
        dve.wait_ge(squared, 6)
        root_mean_square(9)
        dve.wait_ge(ln_ffn_in, 16)
        modulated(ln_ffn, 1)

        dve.wait_ge(retention_stored, 16)
        dve.wait_ge(params_in, 16)
        done(X.memset(select_e, 0.0))
        done(X.memset(gate_e, 0.0))
        iota = const("iota")
        for t, r in enumerate(ROWS):
            name = f"lg{t}"
            aux_filled(dve, name)
            lg = rtmp[0:r, 0, :]
            X.tensor_tensor(lg, aux_bank(name)[0:r, 0:NEXP], param("router_b")[0:r], ALU.add).then_inc(used(name), 1)
            aux_taken(dve, name)
            done(X.max(stat[0:r, 64:72], lg))
            done(X.max_index(top_i[0:r], stat[0:r, 64:72], lg))
            done(X.tensor_copy(stat[0:r, 80:88], top_i[0:r]))
            done(X.tensor_scalar(stat[0:r, 76:77], stat[0:r, 64:65], -1.0, None, ALU.mult), top_ready)
            dve.wait_ge(top_exp, t + 1)
            done(X.reciprocal(stat[0:r, 77:78], stat[0:r, 77:78]))
            done(X.tensor_scalar(stat[0:r, 72:76], stat[0:r, 72:76], stat[0:r, 77:78], None, ALU.mult))
            for k in range(TOPK):
                hot = rtmp[0:r, 1, :]
                done(X.tensor_scalar(hot, iota[0:r, 0:NEXP], stat[0:r, 80 + k:81 + k], None, ALU.is_equal))
                done(X.tensor_tensor(select_e[0:r, t, :], select_e[0:r, t, :], hot, ALU.add))
                done(X.scalar_tensor_tensor(out=gate_e[0:r, t, :], in0=hot, scalar=stat[0:r, 72 + k:73 + k], in1=gate_e[0:r, t, :],
                                            op0=ALU.mult, op1=ALU.add), routed if k == TOPK - 1 else dve_step)
        done(X.memset(slot_of, -1.0))
        for t, r in enumerate(ROWS):
            name = f"pos{t}"
            aux_filled(dve, name)
            s = slot_of[0:r, t, :]
            X.scalar_tensor_tensor(out=s, in0=aux_bank(name)[0:r, 0:NEXP], scalar=1.0, in1=select_e[0:r, t, :], op0=ALU.add, op1=ALU.mult).then_inc(used(name), 1)
            aux_taken(dve, name)
            done(X.tensor_scalar(s, s, 1.0, None, ALU.subtract))
        aux_filled(dve, "cnt")
        counted = rtmp[:, 1, :]
        X.tensor_copy(counted, aux_bank("cnt")[:, 0:NEXP]).then_inc(used("cnt"), 1)
        aux_taken(dve, "cnt")
        done(X.tensor_scalar(n_of, counted, float(BLOCK), 1.0, ALU.is_gt, ALU.add))
        for m in range(2, TOKENS // BLOCK):
            done(X.scalar_tensor_tensor(out=n_of, in0=counted, scalar=float(BLOCK * m), in1=n_of, op0=ALU.is_gt, op1=ALU.add))
        done(X.tensor_tensor_scan(out=cum_of, data0=ones[:, 0:NEXP], data1=n_of, initial=0.0, op0=ALU.mult, op1=ALU.add))
        shape = [P, MAX_BLOCKS, NEXP]
        done(X.tensor_tensor(passed, iota.unsqueeze(2).to_broadcast(shape), cum_of.unsqueeze(1).to_broadcast(shape), ALU.is_ge))
        done(X.tensor_reduce(expert_of, passed, AX.X, ALU.add))
        done(X.tensor_scalar(expert_of, expert_of, float(NEXP - 1), None, ALU.min))
        done(X.tensor_tensor(passed, passed, n_of.unsqueeze(1).to_broadcast(shape), ALU.mult))
        done(X.tensor_reduce(slot_base, passed, AX.X, ALU.add))
        done(X.tensor_tensor(slot_base, iota, slot_base, ALU.subtract))
        done(X.tensor_scalar(slot_base, slot_base, float(BLOCK), None, ALU.mult))
        done(X.tensor_copy(table_i[0:1, 0:MAX_BLOCKS], expert_of[0:1, :]))
        done(X.tensor_copy(table_i[0:1, MAX_BLOCKS:MAX_BLOCKS + 1], cum_of[0:1, NEXP - 1:NEXP]))
        done(X.tensor_tensor(table_i[0:1, MAX_BLOCKS + 1:MAX_BLOCKS + 1 + NEXP], cum_of[0:1, :], n_of[0:1, :], ALU.subtract), table_ready)
        done(X.memset(y_blk, 0.0), added)
        done(X.memset(gateT, 0.0), moe_init)


        def pick_tokens(at, e, waited):
            X.tensor_scalar(sel_now[:, 0, :], slot_of[:, :, bass.ds(e, 1)].rearrange("p t a -> p (t a)"), slot_base[:, bass.ds(at, 1)], None, ALU.subtract).then_inc(moe_step, 1)
            X.tensor_copy(sel_now[:, 1, :], gate_e[:, :, bass.ds(e, 1)].rearrange("p t a -> p (t a)")).then_inc(moe_step, 1)
            dve.wait_ge(moe_step, waited)
            X.tensor_tensor(pick, iota.unsqueeze(1).to_broadcast([P, 3, BLOCK]), sel_now[:, 0, :].unsqueeze(2).to_broadcast([P, 3, BLOCK]), ALU.is_equal).then_inc(picked, 1)

        pick_tokens(0, 0, 2)
        n_blocks = dve.value_load(table_i[0:1, MAX_BLOCKS:MAX_BLOCKS + 1], min_val=NEXP, max_val=MAX_BLOCKS - 1)
        with dve.Fori(1, n_blocks + 1) as i:
            dve.wait_ge(picked, i)
            dve.wait_ge(unit_used, EXPERT_UNITS * i - 1)
            X.tensor_tensor(pick_gate, pick.unsqueeze(2).to_broadcast([P, 3, 2, BLOCK]),
                            sel_now[:, 1, :].unsqueeze(2).unsqueeze(3).to_broadcast([P, 3, 2, BLOCK]), ALU.mult).then_inc(gates_picked, 1)
            e_next = dve.value_load(table_i[0:1, bass.ds(i, 1)], min_val=0, max_val=NEXP - 1)
            dve.wait_ge(gates_picked, i)
            dve.wait_ge(gathered, i)
            pick_tokens(i, e_next, 2 * i + 2)
            dve.wait_ge(unit_used, EXPERT_UNITS * i + 1)
            X.tensor_scalar(g_cut, ps[:, 0, :], LIMIT, None, ALU.min).then_inc(g_cut_ready, 1)
            dve.wait_ge(unit_used, EXPERT_UNITS * i + 3)
            X.tensor_scalar(u_cut, ps[:, 1, :], LIMIT, -LIMIT, ALU.min, ALU.max).then_inc(dve_step, 1)
            dve.wait_ge(dve_step, i + counts["dve_step"])
            dve.wait_ge(g_act_ready, i)
            X.scalar_tensor_tensor(out=h_act, in0=u_cut, scalar=1.0, in1=g_act, op0=ALU.add, op1=ALU.mult).then_inc(act_ready, 1)
            for t, r in enumerate(ROWS):
                dve.wait_ge(scattered, 3 * i + t - 2)
                both = U[0:r, t, :].rearrange("p (a b) -> p a b", a=2)
                X.tensor_tensor(both, ps[0:r, 6:8, :], both, ALU.add).then_inc(added, 1)
        for t, r in enumerate(ROWS):
            dve.wait_ge(scattered, 3 * n_blocks + t + 1)
            both = U[0:r, t, :].rearrange("p (a b) -> p a b", a=2)
            X.tensor_tensor(both, ps[0:r, 6:8, :], both, ALU.add).then_inc(added, 1)
            dve.wait_ge(added, 3 * n_blocks + t + 2)
            X.tensor_tensor(U[0:r, t, :], U[0:r, t, :], V[0:r, 2 if t == 2 else 0, :], ALU.mult).then_inc(scaled, 1)
            dve.wait_ge(scaled, t + 1)
            X.tensor_tensor(R[0:r, t, :], R[0:r, t, :], U[0:r, t, :], ALU.add).then_inc(final_ready, 1)

    @block.tensor
    def _(pe):
        mm = nc.tensor.matmul

        def tr(out, in_, r, **kw):
            return nc.tensor.transpose(out, in_, ident[0:r, 0:r], **kw)

        def aux_free(name):
            n = AUX_AT[name]
            if n >= AUX_BANKS:
                pe.wait_ge(aux_used[n % AUX_BANKS], n // AUX_BANKS)

        def modulation(n):
            u, name = ada_unit(n), f"ada{n}"
            unit_arrived(pe, u)
            aux_free(name)
            wv = ring[:, u % DENSE_SLOTS, :].rearrange("p (k c) -> p k c", k=KD)
            for k in range(KD):
                for j in range(4):
                    last = mm(aux_bank(name)[32 * j:32 * j + 32, 0:128], silu_c[:, k, :], wv[:, k, 128 * j:128 * j + 128],
                              start=(k == 0), stop=(k == KD - 1), skip_group_check=True)
            last.then_inc(aux_ready, 1)

        def spread(n, bank, cols, r):
            for j in range(4):
                last = mm(bank[0:r, 128 * j:128 * j + 128], select[:, j, cols:cols + r], mod[:, n, :], start=True, stop=True)
            return last

        def spread_norm(shift, scale):
            for base, cols, r in ((4, P, 64), (0, 0, P)):
                for h in range(2):
                    spread(scale + h, ps[:, base + h, :], cols, r)
                for h in range(2):
                    last = spread(shift + h, ps[:, base + 2 + h, :], cols, r)
                last.then_inc(bcast_ready, 1)

        def transpose_all(buf, parts, ready, n):
            for q, (t, k0, nk) in enumerate(parts):
                if k0 == 0:
                    ready(t)
                if q == 4:
                    pe.wait_ge(xT_ready, 5 * n + 1)
                r = ROWS[t]
                for k in range(nk):
                    last = tr(ps[:, TR_BANKS[q], k * r:k * r + r], buf[0:r, t, (k0 + k) * P:(k0 + k + 1) * P], r)
                last.then_inc(tr_ready, 1)

        z_pieces = iter(range(3 * (IN_UNITS + OUT_UNITS)))

        def project(count):
            for _ in range(count):
                idx, t = divmod(next(z_pieces), 3)
                u = proj_unit(idx)
                wv = ring[:, u % DENSE_SLOTS, :].rearrange("p (k c) -> p k c", k=KD)
                banks = z_banks(idx)
                if t == 0:
                    unit_arrived(pe, u)
                    if idx >= 2:
                        pe.wait_ge(z_used, 4 * (idx - 1))
                if t < 2:
                    for k in range(KD):
                        last = mm(banks[t][0], xT[:, k, t * P:t * P + P], wv[:, k, :], start=(k == 0), stop=(k == KD - 1))
                else:
                    if idx >= 1:
                        pe.wait_ge(z_used, 4 * idx)
                    for k in range(KD):
                        for a in range(2):
                            last = mm(banks[2 + a][0], xT[:, k, 2 * P:TOKENS], wv[:, k, 256 * a:256 * a + 256],
                                      start=(k == 0), stop=(k == KD - 1), skip_group_check=True)
                last.then_inc(z_ready, 1)

        pe.wait_ge(silu_done, 1)
        for n in range(ADA_FIRST):
            modulation(n)
        pe.wait_ge(consts_in, 16)
        for n in range(ADA_FIRST):
            aux_taken(pe, f"ada{n}")
        spread_norm(0, 2)
        transpose_all(T, TR_NORM, lambda t: pe.wait_ge(h_ready, {2: 1, 0: 2, 1: 3}[t]), 0)
        pe.wait_ge(xT_ready, 5)
        project(9)
        modulation(4)
        modulation(5)

        for t, r in enumerate(ROWS):
            pe.wait_ge(qk_normed, t + 1)
            name = f"kT{t}"
            aux_free(name)
            for g in range(KVH):
                last = tr(aux_bank(name)[0:64, g * r:g * r + r], V[0:r, t, g * HD:(g + 1) * HD], r)
            last.then_inc(aux_ready, 1)

        def transpose_queries(t):
            n, r = (2, 64) if t == 2 else (4, P)
            for q in range(n):
                name = f"qT{t}{q}"
                aux_free(name)
                for m in range(QH // n):
                    h = q * (QH // n) + m
                    last = tr(aux_bank(name)[0:64, m * r:m * r + r], R[0:r, t, h * HD:(h + 1) * HD], r)
                last.then_inc(aux_ready, 1)
            for q in range(n):
                aux_taken(pe, f"qT{t}{q}")

        softmaxes = 0
        for t in range(3):
            aux_taken(pe, f"kT{t}")
        for t in range(2):
            transpose_queries(t)
            for g in range(KVH):
                for k in range(t + 1):
                    name = f"sc{t}{g}{k}"
                    aux_free(name)
                    n, width = (4, P) if t == 0 else (2, 2 * P)
                    for m in range(n):
                        last = mm(aux_bank(name)[:, m * width:(m + 1) * width], qTa[0:64, 4 * g + n * k + m, :],
                                  kTa[0:64, g, 0:width], start=True, stop=True)
                    last.then_inc(aux_ready, 1)
                if 4 * t + g < 6:
                    modulation(6 + 4 * t + g)
                project(2)
                softmaxes += 1
                pe.wait_ge(probs_ready, softmaxes)
                for k in range(t + 1):
                    name = f"pT{t}{g}{k}"
                    aux_free(name)
                    for h in range(GROUP):
                        last = tr(aux_bank(name)[:, h * P:h * P + P], probs[:, h, k * P:k * P + P], P)
                    last.then_inc(aux_ready, 1)
                name = f"pv{t}{g}"
                aux_free(name)
                for k in range(t + 1):
                    aux_taken(pe, f"pT{t}{g}{k}")
                for h in range(GROUP):
                    for k in range(t + 1):
                        last = mm(aux_bank(name)[:, h * HD:(h + 1) * HD], pT[:, k, h * P:h * P + P],
                                  V[:, k, 256 + g * HD:256 + (g + 1) * HD], start=(k == 0), stop=(k == t))
                last.then_inc(aux_ready, 1)
        transpose_queries(2)
        for b in range(BATCH_S):
            name = f"sc2{b}"
            aux_free(name)
            pe.wait_ge(cache_in[b % 2], 32 * (b // 2 + 1))
            keys = cache[0:64, b % 2, 0:512].rearrange("p (h r) -> p h r", h=KVH)
            for g in range(KVH):
                q = qTs[0:64, b, GROUP * g:GROUP * (g + 1), :].rearrange("p h t -> p (h t)")
                mm(aux_bank(name)[32 * g:32 * g + 32, 0:P], q, keys[:, g, :], start=True, stop=True, skip_group_check=True)
                last = mm(aux_bank(name)[32 * g:32 * g + 32, P:192], q, kTa[0:64, g, SEQ:TOKENS], start=True, stop=True, skip_group_check=True)
            last.then_inc(aux_ready, 1)
            project(1)
            softmaxes += 1
            pe.wait_ge(probs_ready, softmaxes)
            name = f"pT2{b}"
            aux_free(name)
            tr(aux_bank(name)[:, 0:P], probs[:, 0, 0:P], P)
            tr(aux_bank(name)[0:64, P:2 * P], probs[:, 0, P:192], P).then_inc(aux_ready, 1)
            name = f"pv2{b}"
            aux_free(name)
            aux_taken(pe, f"pT2{b}")
            for g in range(KVH):
                out = aux_bank(name)[0:64, 32 * g:32 * g + 32]
                mm(out, cache[:, b % 2, 512 + g * HD:512 + (g + 1) * HD], pT[:, 0, 32 * g:32 * g + 32], start=True, stop=False)
                last = mm(out, V[0:64, 2, 256 + g * HD:256 + (g + 1) * HD], pT[0:64, 1, 32 * g:32 * g + 32], start=False, stop=True)
            last.then_inc(aux_ready, 1)
        for h in range(2):
            name = f"oback{h}"
            aux_free(name)
            aux_taken(pe, f"pv2{BATCH_S - 1}")
            for m in range(8):
                last = tr(aux_bank(name)[0:64, m * HD:(m + 1) * HD], oT[0:64, 8 * h + m, :], 64)
            last.then_inc(aux_ready, 1)

        for t, r in enumerate(ROWS):
            project(1)
            pe.wait_ge(cv_ready, t + 1)
            pe.wait_ge(mixw_ready, 2)
            w = mixT_s if t == 2 else mixT
            for h in range(2):
                name = f"mix{t}{h}"
                aux_free(name)
                for g in range(4 * h, 4 * h + 4):
                    last = mm(aux_bank(name)[0:r, (g % 4) * P:(g % 4) * P + P], w[0:r, g, :], XC[0:r, t, g * P:(g + 1) * P], start=True, stop=True)
                last.then_inc(aux_ready, 1)
            project(1)
        pe.wait_ge(roped, 3)
        for t in range(2):
            for h in range(2):
                for kind, c0 in (("rqT", 0), ("rkT", HALF)):
                    name = f"{kind}{t}{h}"
                    aux_free(name)
                    for n in range(4):
                        c = c0 + (4 * h + n) * RDK
                        last = tr(aux_bank(name)[0:64, n * P:n * P + P], XQK[:, t, c:c + RDK], P)
                    last.then_inc(aux_ready, 1)
                project(1)
                name = f"ra{t}{h}"
                aux_free(name)
                aux_taken(pe, f"rqT{t}{h}")
                aux_taken(pe, f"rkT{t}{h}")
                for n in range(4):
                    last = mm(aux_bank(name)[:, n * P:n * P + P], rkT[0:64, 4 * h + n, :], rqT[0:64, 4 * h + n, :], start=True, stop=True)
                last.then_inc(aux_ready, 1)
                project(1)
                name = f"ro{t}{h}"
                aux_free(name)
                aux_taken(pe, f"ra{t}{h}")
                if t == 1:
                    aux_taken(pe, f"rs0{h}")
                for n in range(4):
                    hh = 4 * h + n
                    out = aux_bank(name)[:, n * P:n * P + P]
                    last = mm(out, ra[:, h, n * P:n * P + P], XV[:, t, hh * RDV:(hh + 1) * RDV], start=True, stop=(t == 0))
                    if t == 1:
                        last = mm(out, rqT[0:64, hh, :], state[0:64, hh, :], start=False, stop=True)
                last.then_inc(aux_ready, 1)
            for h in range(2):
                name = f"rs{t}{h}"
                aux_free(name)
                for n in range(4):
                    hh = 4 * h + n
                    last = mm(aux_bank(name)[0:64, n * P:n * P + P], XQK[:, t, HALF + hh * RDK:HALF + (hh + 1) * RDK],
                              XV[:, t, hh * RDV:(hh + 1) * RDV], start=True, stop=True)
                last.then_inc(aux_ready, 1)
        for name, c0 in (("rqT2", 0), ("rkT2", HALF)):
            aux_free(name)
            for n in range(RH):
                last = tr(aux_bank(name)[0:64, n * 64:n * 64 + 64], XQK[0:64, 2, c0 + n * RDK:c0 + (n + 1) * RDK], 64)
            last.then_inc(aux_ready, 1)
        project(1)
        aux_free("ra2")
        aux_taken(pe, "rqT2")
        aux_taken(pe, "rkT2")
        for n in range(RH):
            last = mm(aux_bank("ra2")[0:64, n * 64:n * 64 + 64], rkT[0:64, n, 0:64], rqT[0:64, n, 0:64], start=True, stop=True)
        last.then_inc(aux_ready, 1)
        project(1)
        aux_free("ro2")
        aux_taken(pe, "ra2")
        for n in range(RH):
            last = mm(aux_bank("ro2")[:, n * 64:n * 64 + 64], XV[0:64, 2, n * RDV:(n + 1) * RDV], ra[0:64, 0, n * 64:n * 64 + 64], start=True, stop=True)
        last.then_inc(aux_ready, 1)
        for b in range(BATCH_S):
            pe.wait_ge(state_in[b % 2], 16 * (b // 2 + 1))
            name = f"ri{b}"
            aux_free(name)
            for n in range(RH):
                last = mm(aux_bank(name)[:, n * STEPS:(n + 1) * STEPS], V[0:64, b % 2, n * RDV:(n + 1) * RDV],
                          rqT[0:64, n, b * STEPS:(b + 1) * STEPS], start=True, stop=True)
            last.then_inc(aux_ready, 1)
            pe.wait_ge(kd_ready, b + 1)
            for h in range(2):
                name = f"rs2{b}{h}"
                aux_free(name)
                for n in range(4):
                    hh = 4 * h + n
                    last = mm(aux_bank(name)[0:64, n * P:n * P + P], kd[0:64, hh * RDK:(hh + 1) * RDK],
                              XV[0:64, 2, hh * RDV:(hh + 1) * RDV], start=True, stop=True)
                last.then_inc(aux_ready, 1)
            project(1)
        aux_taken(pe, f"ri{BATCH_S - 1}")
        for h in range(2):
            name = f"rback{h}"
            aux_free(name)
            for n in range(4):
                hh = 4 * h + n
                last = tr(aux_bank(name)[0:64, n * P:n * P + P], ro_s[:, hh * 64:hh * 64 + 64], P)
            last.then_inc(aux_ready, 1)

        transpose_all(T, TR_MERGED, lambda t: pe.wait_ge(merged, t + 1), 1)
        pe.wait_ge(xT_ready, 10)

        def spread_gate(kind, first):
            for s, cols, r in (("p", 0, P), ("s", P, 64)):
                for h in range(2):
                    name = f"{kind}{s}{h}"
                    aux_free(name)
                    spread(first + h, aux_bank(name), cols, r).then_inc(aux_ready, 1)

        spread_gate("g1", 4)
        project(6)
        pe.wait_ge(z_used, 4 * (IN_UNITS + 2))
        for name in ("g1p0", "g1p1", "g1s0", "g1s1"):
            aux_taken(pe, name)
        spread_norm(6, 8)
        transpose_all(T, TR_NORM, lambda t: pe.wait_ge(h_ready, {2: 4, 0: 5, 1: 6}[t]), 2)
        pe.wait_ge(xT_ready, 15)
        spread_gate("g2", 10)

        pe.wait_ge(router_in, 16)
        for t, r in enumerate(ROWS):
            name = f"lg{t}"
            aux_free(name)
            for k in range(KD):
                last = mm(aux_bank(name)[0:r, 0:NEXP], xT[:, k, t * P:t * P + r], router_w[:, k, :], start=(k == 0), stop=(k == KD - 1))
            last.then_inc(aux_ready, 1)
        pe.wait_ge(routed, 3)
        for t, r in enumerate(ROWS):
            name = f"pos{t}"
            aux_free(name)
            for s in range(t + 1):
                w = const("before") if s == t else ones
                last = mm(aux_bank(name)[0:r, 0:NEXP], w[0:ROWS[s], 0:r], select_e[0:ROWS[s], s, :], start=(s == 0), stop=(s == t))
            last.then_inc(aux_ready, 1)
        aux_free("cnt")
        for s, r in enumerate(ROWS):
            last = mm(aux_bank("cnt")[:, 0:NEXP], ones[0:r, :], select_e[0:r, s, :], start=(s == 0), stop=(s == 2))
        last.then_inc(aux_ready, 1)
        aux_free("gT")
        for t, r in enumerate(ROWS):
            last = tr(aux_bank("gT")[0:NEXP, t * P:t * P + r], gate_e[0:r, t, :], r)
        last.then_inc(aux_ready, 1)
        aux_taken(pe, "gT")
        pe.wait_ge(b2_in, 16)
        for t, r in enumerate(ROWS):
            for h in range(2):
                name = f"b2{'abc'[t]}{h}"
                aux_free(name)
                mm(aux_bank(name)[0:r], gates_T[:, t * P:t * P + r], b2_sb[0:NEXP, HALF * h:HALF * h + HALF], start=True, stop=True).then_inc(aux_ready, 1)
        for t in range(3):
            for h in range(2):
                aux_taken(pe, f"b2{'abc'[t]}{h}")

        def gather(n):
            pe.wait_ge(picked, n)
            for t, r in enumerate(ROWS):
                for a in range(2):
                    last = mm(ps[64 * a:64 * a + 64, 3, :], pick[0:r, t, :], T[0:r, t, HALF * a:HALF * a + HALF],
                              start=(t == 0), stop=(t == 2), skip_group_check=True)
            last.then_inc(gathered, 1)

        def turn(n):
            pe.wait_ge(xg_rows, n)
            for c in range(4):
                last = tr(ps[:, 3, c * P:(c + 1) * P], xg_s[:, c * P:(c + 1) * P], P)
            last.then_inc(turned, 1)

        def scatter(n, t):
            pe.wait_ge(added, 3 * n + t - 2)
            for a in range(2):
                last = mm(ps[:, 6 + a, :], gateT[64 * a:64 * a + 64, t * P:(t + 1) * P], y_blk[64 * a:64 * a + 64, :], start=True, stop=True)
            last.then_inc(scattered, 1)

        def filled(j):
            return DENSE_UNITS // DENSE_SLOTS if j < DENSE_SLOTS else 0

        pe.wait_ge(moe_init, 1)
        gather(1)
        turn(1)
        pe.sem_inc(unit_used, EXPERT_UNITS - 1)
        n_blocks = pe.value_load(table_i[0:1, MAX_BLOCKS:MAX_BLOCKS + 1], min_val=NEXP, max_val=MAX_BLOCKS - 1)
        with pe.Fori(1, n_blocks + 1) as i:
            e = pe.value_load(table_i[0:1, bass.ds(i - 1, 1)], min_val=0, max_val=NEXP - 1)
            pe.wait_ge(xg_ready, i)
            for half in range(2):
                for j in (2 * half, 2 * half + 1):
                    pe.wait_ge(unit_in[j], 16 * e + 16 * (filled(j) + 1))
                    wv = ring[:, j, :].rearrange("p (k c) -> p k c", k=4)
                    for k in range(4):
                        for a in range(2):
                            last = mm(ps[64 * a:64 * a + 64, half, :], xgT[:, k, j % 2, :], wv[:, k, HALF * a:HALF * a + HALF],
                                      start=(j % 2 == 0 and k == 0), stop=False, skip_group_check=True)
                    if j % 2 == 0:
                        last.then_inc(unit_used, 1)
                pe.wait_ge(b1_in[half], 16 * e + 16)
                for a in range(2):
                    last = mm(ps[64 * a:64 * a + 64, half, :], ones[0:1, 0:64], W[0:1, half, HALF * a:HALF * a + HALF],
                              start=False, stop=True, skip_group_check=True)
                last.then_inc(unit_used, 1)
            pe.wait_ge(y_ready, i)
            pe.wait_ge(gateT_ready, i)
            scatter(i, 0)
            gather(i + 1)
            pe.wait_ge(act_ready, i)
            for c in range(4):
                last = tr(ps[:, 4, c * P:(c + 1) * P], h_act[:, c * P:(c + 1) * P], P)
            last.then_inc(actT_done, 1)
            pe.wait_ge(gates_picked, i)
            for t, r in enumerate(ROWS):
                last = tr(ps[:, 5, t * P:t * P + r], pick_gate[0:r, t, :, :], r)
            last.then_inc(gateT_done, 1)
            scatter(i, 1)
            scatter(i, 2)
            pe.wait_ge(actT_ready, i)
            for j in (4, 5):
                pe.wait_ge(unit_in[j], 16 * e + 16 * (filled(j) + 1))
                wv = ring[:, j, :].rearrange("p (k c) -> p k c", k=4)
                for k in range(4):
                    for a in range(2):
                        last = mm(ps[64 * a:64 * a + 64, 2, :], actT[:, k, j - 4, :], wv[:, k, HALF * a:HALF * a + HALF],
                                  start=(j == 4 and k == 0), stop=(j == 5 and k == 3), skip_group_check=True)
                last.then_inc(unit_used, 1)
                if j == 4:
                    turn(i + 1)
        pe.wait_ge(y_ready, n_blocks + 1)
        pe.wait_ge(gateT_ready, n_blocks + 1)
        for t in range(3):
            scatter(n_blocks + 1, t)


def shape_constants():
    c = {name: np.zeros((P, width), np.float32) for name, width in CONST_WIDTHS}
    p = np.arange(P)
    c["ident"][:] = np.eye(P)
    c["causal"][:] = p[:, None] <= p[None, :]
    q = np.arange(64)
    c["blockcausal"][:64] = (q[:, None] // STEPS == q[None, :] // STEPS) & (q[:, None] <= q[None, :])
    sel = np.zeros((P, 4, 192), np.float32)
    for j in range(4):
        sel[32 * j, j, :P] = 1
        sel[32 * j + 1 + q // STEPS, j, P + q] = 1
    c["select"][:] = sel.reshape(P, -1)
    pos = np.concatenate([np.arange(SEQ), PAST + q % STEPS, np.zeros(64)]).astype(np.float32)
    freq = np.float32(10000.0) ** (-np.arange(0, RDK, 2, dtype=np.float32) / np.float32(RDK))
    angle = (pos[:, None] * freq[None, :].astype(np.float32)).astype(np.float32).astype(np.float64).reshape(3, P, 32)
    c["cos"][:] = np.cos(angle).transpose(1, 0, 2).reshape(P, -1)
    c["sin"][:] = np.sin(angle).transpose(1, 0, 2).reshape(P, -1)
    gamma = 1.0 - 2.0 ** (-5.0 - np.arange(RH))
    in_chunk = np.concatenate([np.arange(P), np.arange(P), q % STEPS, np.zeros(64)])
    up = gamma[None] ** (in_chunk[:, None] + 1)
    decay = np.concatenate([up, RDK ** -0.5 / up], 1).reshape(3, P, 16)
    c["decay"][:] = decay.transpose(1, 0, 2).reshape(P, -1)
    c["chunk_decay"][:] = np.concatenate([gamma ** P, gamma ** STEPS])
    c["iota"][:] = np.arange(64)
    rel = p[:, None] + P - np.arange(2 * P)[None, :]
    c["window"][:] = np.where((rel >= 0) & (rel < P), 0, MASKED)
    step = p % STEPS
    c["cache_mask"][:] = np.where(p[None, :] > step[:, None], 0, MASKED)
    own = (q[None, None, :] // STEPS == np.arange(BATCH_S)[None, :, None]) & (q[None, None, :] % STEPS <= step[:, None, None])
    c["new_mask"][:] = np.where(own, 0, MASKED).reshape(P, -1)
    c["before"][:] = p[:, None] < p[None, :]
    c["ones"][:] = 1
    c["of_batch"][:64] = q[:, None] // STEPS == np.arange(BATCH_S)[None, :]
    return np.concatenate([c[name] for name, _ in CONST_WIDTHS], 1)


def lay_out(x):
    x = {k: np.asarray(v) for k, v in x.items()}
    f = np.float32
    c = np.zeros((32, D), f)
    c[0:1] = x["c_prompt"]
    c[1:1 + BATCH_S] = x["c_sample"]

    def units(w):
        return w.reshape(KD, P, -1, HALF).transpose(2, 1, 0, 3).reshape(-1, P, KD * HALF)

    w_ada = units(x["w_ada"][0])
    w_proj = np.concatenate([units(x["w_in"][0])[IN_ORDER], units(x["w_out"][0])])
    w1 = x["moe_w1"][0].reshape(NEXP, 2, 4, P, 2, D).transpose(0, 4, 1, 3, 2, 5).reshape(NEXP, 4, P, 4 * D)
    w2 = x["moe_w2"][0].reshape(NEXP, 2, 4, P, D).transpose(0, 1, 3, 2, 4).reshape(NEXP, 2, P, 4 * D)
    params = {name: np.zeros((P, width), f) for name, width in PARAM_WIDTHS}
    params["k_gain"][:] = np.tile(x["k_norm_g"][0], KVH)
    params["sinks"][:] = x["attn_sinks"][0]
    params["sink_rows"][:, 0] = np.repeat(x["attn_sinks"][0], STEPS)
    params["q_gain"][:, 0] = np.tile(x["q_norm_g"][0], 2)
    params["router_b"][:] = x["router_b"][0]
    params["mix_bias"][:] = x["gm_bs"][0].T
    params["mix_bias_s"][:] = np.tile(x["gm_bs"][0].T[:STEPS], (P // STEPS, 1))
    ws = x["gm_ws"][0].transpose(2, 0, 1)
    return {
        "c": np.ascontiguousarray(c.T.reshape(KD, P, 32).transpose(1, 0, 2)),
        "x_prompt": x["x_prompt"][0], "x_sample": x["x_sample"].reshape(-1, D),
        "consts": shape_constants(),
        "params": np.concatenate([params[name] for name, _ in PARAM_WIDTHS], 1),
        "w_dense": np.stack([w_ada[n] if kind == "ada" else w_proj[n] for kind, n in DENSE_ORDER]),
        "w_moe": np.concatenate([w1, w2], 1),
        "b_ada": x["b_ada"][0], "b1": x["moe_b1"][0].reshape(NEXP, 2, D), "b2": x["moe_b2"][0],
        "b_gate": x["b_gate"][0].reshape(3, D),
        "ln_mix_g": x["ln_mix_g"][0], "ln_ffn_g": x["ln_ffn_g"][0], "ret_norm_g": x["ret_norm_g"][0],
        "gm_ln_g": x["gm_ln_g"][0], "gm_ln_b": x["gm_ln_b"][0],
        "mixT": np.ascontiguousarray(ws),
        "mixT_s": np.ascontiguousarray(np.tile(ws[:STEPS, :, :STEPS], (BATCH_S, 1, BATCH_S))),
        "state": x["state_retention"][0],
        "cache_kT": np.ascontiguousarray(x["cache_attn_k"][0].transpose(0, 3, 2, 1)),
        "cache_v": x["cache_attn_v"][0].reshape(BATCH_S, P, KVH * HD),
        "router_w": np.ascontiguousarray(x["router_w"][0].reshape(KD, P, NEXP).transpose(1, 0, 2)),
    }


OUT_SHAPES = {
    "y_prompt": (SEQ, D), "y_sample": (BATCH_S * STEPS, D), "prompt_k": (P, KVH * HD), "prompt_v": (P, KVH * HD),
    "prompt_retention": (RH, RDK, RDV), "sample_k": (BATCH_S * STEPS, KVH * HD), "sample_v": (BATCH_S * STEPS, KVH * HD),
    "sample_retention": (BATCH_S, RH, RDK, RDV), "sample_gmlp_v": (BATCH_S * STEPS, D),
}


def kernel(**inputs):
    import concourse.bacc as bacc
    from concourse.bass_utils import run_bass_kernel_spmd

    arrays = lay_out(inputs)
    nc = bacc.Bacc("TRN2", target_bir_lowering=False, num_devices=1)
    ins = {name: nc.dram_tensor("in_" + name, a.shape, mybir.dt.from_np(a.dtype), kind="ExternalInput").ap() for name, a in arrays.items()}
    outs = {name: nc.dram_tensor("out_" + name, shape, FP32, kind="ExternalOutput").ap() for name, shape in OUT_SHAPES.items()}
    hybrid_step_kernel(nc, ins, outs)
    r = run_bass_kernel_spmd(nc, [{"in_" + name: a for name, a in arrays.items()}], core_ids=[0]).results[0]
    got = {name: r["out_" + name] for name in OUT_SHAPES}
    return (got["y_prompt"].reshape(1, SEQ, D), got["y_sample"].reshape(BATCH_S, STEPS, D),
            got["prompt_k"].reshape(1, 1, P, KVH, HD), got["prompt_v"].reshape(1, 1, P, KVH, HD),
            got["prompt_retention"].reshape(1, 1, RH, RDK, RDV),
            got["sample_k"].reshape(1, BATCH_S, STEPS, KVH, HD), got["sample_v"].reshape(1, BATCH_S, STEPS, KVH, HD),
            got["sample_retention"].reshape(1, BATCH_S, RH, RDK, RDV),
            got["sample_gmlp_v"].reshape(1, BATCH_S, STEPS, D))
```

```python
import numpy as np
import concourse.bass as bass
from concourse import mybir
from concourse.alu_op_type import AluOpType as ALU

ACT = mybir.ActivationFunctionType
AX = mybir.AxisListType
FP32 = mybir.dt.float32
I32 = mybir.dt.int32
U32 = mybir.dt.uint32
BF16 = mybir.dt.bfloat16

P = 128
D = 1024
KD = D // P
HALF = 512
BATCH_S, STEPS = 8, 8
SEQ = 256
TOKENS = SEQ + BATCH_S * STEPS
ROWS = [P, P, TOKENS - 2 * P]
HD, QH, KVH = 64, 16, 4
GROUP = QH // KVH
RH, RDK, RDV = 8, 64, 128
GG = 8
NEXP, TOPK = 32, 4
LIMIT = 7.0
PAST = 1024
EPS = 1e-6
MASKED = -1e30

SLOTS = 6
DENSE_SLOTS = 3
EXPERT_UNITS = 6
ADA_UNITS, IN_UNITS, OUT_UNITS = 12, 19, 2
DENSE_UNITS = ADA_UNITS + IN_UNITS + OUT_UNITS
AQ0, AQ1, AKV, CU0, CU1, CV0, CV1, RQ, RK, RV0, RV1, GA0, GA1, GC0, GC1, RG0, RG1, GB0, GB1 = range(IN_UNITS)
IN_ORDER = [0, 1, 2, 9, 10, 11, 12, 3, 4, 5, 6, 13, 14, 17, 18, 7, 8, 15, 16]
DENSE_ORDER = [("ada", 2), ("ada", 3), ("ada", 0), ("ada", 1), ("proj", AQ0), ("proj", AQ1), ("proj", AKV),
               ("ada", 4), ("ada", 5), ("ada", 6), ("proj", CU0), ("ada", 7), ("proj", CU1), ("ada", 8),
               ("ada", 9), ("proj", CV0), ("ada", 10), ("proj", CV1), ("ada", 11)]
DENSE_ORDER += [("proj", idx) for idx in range(RQ, IN_UNITS + OUT_UNITS)]


def ada_unit(n):
    return DENSE_ORDER.index(("ada", n))


def proj_unit(idx):
    return DENSE_ORDER.index(("proj", idx))


BLOCK = 64
MAX_BLOCKS = 64

CONST_WIDTHS = [("ident", 128), ("select", 4 * 192), ("causal", 128), ("blockcausal", 64),
                ("cos", 3 * 32), ("sin", 3 * 32), ("decay", 3 * 16), ("chunk_decay", 16),
                ("window", 256), ("cache_mask", 128), ("new_mask", 8 * 64),
                ("iota", 64), ("before", 128), ("ones", 128), ("of_batch", 8), ("row", 1), ("stack", 32)]
FIRST_CONSTS = 128 + 4 * 192
CONST_AT = {}
CONST_COLS = 0
for _name, _width in CONST_WIDTHS:
    CONST_AT[_name] = (CONST_COLS, CONST_COLS + _width)
    CONST_COLS += _width

PARAM_WIDTHS = [("k_gain", 256), ("sinks", 16), ("sink_rows", 1), ("q_gain", 1), ("router_b", 32),
                ("mix_bias", 8), ("mix_bias_s", 8)]
PARAM_AT = {}
PARAM_COLS = 0
for _name, _width in PARAM_WIDTHS:
    PARAM_AT[_name] = (PARAM_COLS, PARAM_COLS + _width)
    PARAM_COLS += _width

SAMPLE_PIECES = [2, 2, 1, 1, 1, 1, 0, 0]

AUX_FIRST, AUX_BANKS = 5, 3
HALVES = ["s0", "s1", "p0", "p1"]
AUX = ["ada2", "ada3"] + [f"gain0{x}" for x in HALVES] + ["ada0", "ada1"] + [f"shift0{x}" for x in HALVES]
AUX += ["ada4", "ada5", "kT0", "kT1", "kT2"]
for _t in range(2):
    AUX += [f"qT{_t}{q}" for q in range(4)]
    for _g in range(KVH):
        AUX += [f"sc{_t}{_g}{k}" for k in range(_t + 1)]
        AUX += [f"ada{6 + 4 * _t + _g}"] if 4 * _t + _g < 6 else []
        AUX += [f"pT{_t}{_g}{k}" for k in range(_t + 1)] + [f"pv{_t}{_g}"]
AUX += ["qT20", "qT21"]
for _b in range(BATCH_S):
    AUX += [f"sc2{_b}", f"pT2{_b}", f"pv2{_b}"]
AUX += ["oback0", "oback1"]
AUX += [f"mix{t}{h}" for t in range(3) for h in range(2)]
for _t in range(2):
    for _h in range(2):
        AUX += [f"rqT{_t}{_h}", f"rkT{_t}{_h}", f"ra{_t}{_h}", f"ro{_t}{_h}"]
    AUX += [f"rs{_t}{_h}" for _h in range(2)]
AUX += ["rqT2", "rkT2", "ra2", "ro2"]
for _b in range(BATCH_S):
    AUX += [f"ri{_b}", f"rs2{_b}0", f"rs2{_b}1"]
AUX += ["rback0", "rback1"]
AUX += [f"g1{s}{h}" for s in "ps" for h in range(2)]
AUX += [f"gain1{x}" for x in HALVES] + [f"shift1{x}" for x in HALVES]
AUX += ["lg0", "lg1", "lg2", "cnt", "pos0", "pos1", "pos2", "table", "gT"]
AUX_AT = {name: n for n, name in enumerate(AUX)}


def hybrid_step_kernel(nc, ins, outs):
    from contextlib import ExitStack
    with ExitStack() as ctx:
        build(nc, ctx, ins, outs)


def build(nc, ctx, ins, outs):
    def sb(name, shape, dt=FP32):
        return ctx.enter_context(nc.sbuf_tensor(name, shape, dt))

    def sem(name):
        return ctx.enter_context(nc.semaphore(name))

    ring = sb("ring", [P, SLOTS, 4096])
    xT = sb("xT", [P, KD, TOKENS])
    R = sb("R", [P, 3, D])
    T = sb("T", [P, 3, D])
    U = sb("U", [P, 3, D])
    V = sb("V", [P, 3, D])
    W = sb("W", [P, 3, D])
    spare = ring[:, DENSE_SLOTS:SLOTS, :].rearrange("p s c -> p (s c)")
    XQK, XV, XC, XG = (spare[:, n * 3 * D:(n + 1) * 3 * D].rearrange("p (t d) -> p t d", t=3) for n in range(4))
    mod = sb("mod", [P, ADA_UNITS, 128])
    consts = sb("consts", [P, CONST_COLS])
    params = sb("params", [P, PARAM_COLS])
    stat = sb("stat", [P, 96])
    ARENA = 5888
    arena = sb("arena", [P, ARENA])
    table_i = sb("table_i", [1, MAX_BLOCKS + 1 + NEXP], I32)
    top_i = sb("top_i", [P, 3, 8], U32)
    ps = ctx.enter_context(nc.psum_tensor("ps", [P, 8, HALF], FP32))

    def const(name):
        a, b = CONST_AT[name]
        return consts[:, a:b]

    def param(name):
        a, b = PARAM_AT[name]
        return params[:, a:b]

    ident = const("ident")
    select = const("select").rearrange("p (j m) -> p j m", j=4)
    cos = const("cos").rearrange("p (t f) -> p t f", t=3)
    sin = const("sin").rearrange("p (t f) -> p t f", t=3)
    decay = const("decay").rearrange("p (t h) -> p t h", t=3)
    new_mask = const("new_mask").rearrange("p (b k) -> p b k", b=BATCH_S)
    ones = const("ones")

    def cut(at, *shape):
        size = int(np.prod(shape))
        assert at + size <= ARENA, (at, size)
        v = arena[:, at:at + size]
        if len(shape) == 2:
            v = v.rearrange("p (a b) -> p a b", a=shape[0])
        if len(shape) == 3:
            v = v.rearrange("p (a b c) -> p a b c", a=shape[0], b=shape[1])
        return v

    silu_c = XG[:, 0, 0:KD * 32].rearrange("p (k b) -> p k b", k=KD)
    mod_bias = V[:, :, HALF:D]
    ln_gain = cut(1792, D)
    ln_ffn = cut(0, D)
    gains = {"s": (U[0:64, 1, :], 64), "p": (U[:, 0, :], P)}
    gm_gain = cut(0, D)
    gm_bias = cut(1024, D)
    mixT = cut(2048, GG, 128)
    mixT_s = cut(3072, GG, 64)
    mix_tmp = cut(3584, D)
    gate_bias = cut(5120, HALF)
    gate_bias_a = U[:, 2, :]
    rqT = cut(0, RH, 128)
    rkT = cut(1024, RH, 128)
    ra = cut(2048, 2, HALF)
    state = cut(3072, RH, RDV)
    kd = cut(4096, HALF)
    ro_s = cut(4608, HALF)
    ret_gain = XQK[:, 0, :]
    squares = cut(1024, D)
    kTa = cut(0, KVH, TOKENS)
    probs = cut(1280, 4, 256)
    pT = cut(2304, 2, HALF)
    oT = cut(3328, QH, BATCH_S * STEPS)
    cache = cut(4352, 2, 768)
    qTa = U[:, 0:2, :].rearrange("p a d -> p (a d)").rearrange("p (h t) -> p h t", h=QH)
    qTs = U[:, 0, :].rearrange("p (b h t) -> p b h t", b=BATCH_S, h=QH)
    router_w = cut(2048, KD, NEXP)
    select_e = cut(256, 3, NEXP)
    gate_e = cut(352, 3, NEXP)
    slot_of = cut(448, 3, NEXP)
    rtmp = cut(544, 3, NEXP)
    slot_base = cut(640, MAX_BLOCKS)
    of_block = cut(704, 2)
    n_of = cut(768, NEXP)
    cum_of = cut(800, NEXP)
    pick = cut(832, 3, BLOCK)
    pick_gate = cut(1024, 3, 2, BLOCK)
    sel_now = cut(1408, 2, 3)
    xgT = cut(1536, 4, 2, BLOCK)
    actT = cut(2048, 4, 2, BLOCK)
    gateT = cut(2560, 3 * P)
    y_blk = cut(2944, HALF)
    g_cut = cut(3456, HALF)
    g_act = cut(3968, HALF)
    u_cut = cut(4480, HALF)
    h_act = cut(4992, HALF)
    pick_e = cut(5504, BLOCK // 2).bitcast(BF16)
    b1_parts = consts[:, FIRST_CONSTS:FIRST_CONSTS + D].bitcast(BF16)
    b1_whole, b1_rest = V[:, 1, :], U[:, 2, :]
    passed = cut(4736, 2, NEXP)
    hot = cut(3456, 3, TOPK * NEXP)
    hot_gate = cut(3968, 3, TOPK * NEXP)
    top = cut(4480, 3, 8)
    top_at = cut(4512, 3, 8)
    top_gate = cut(4544, 3, TOPK)
    top_sum = cut(4560, 3)
    table_rows = cut(4608, 2, MAX_BLOCKS)
    xg_s = W[:, 2, 0:HALF]

    h_ready, summed = sem("h_ready"), sem("summed")
    unit_in = [sem(f"unit_in{s}") for s in range(SLOTS)]
    state_in = [sem(f"state_in{i}") for i in range(2)]
    cache_in = [sem(f"cache_in{i}") for i in range(2)]
    aux_used = [sem(f"aux_used{i}") for i in range(AUX_BANKS)]
    unit_used, c_in, x_in, consts_in, params_in, mod_bias_in = map(sem, (
        "unit_used", "c_in", "x_in", "consts_in", "params_in", "mod_bias_in"))
    ln_mix_in, gm_in, gate_bias_in, ret_gain_in, ln_ffn_in, x_again_in = map(sem, (
        "ln_mix_in", "gm_in", "gate_bias_in", "ret_gain_in", "ln_ffn_in", "x_again_in"))
    router_in, b2_in, stored, kv_stored, gmlp_stored, retention_stored = map(sem, (
        "router_in", "b2_in", "stored", "kv_stored", "gmlp_stored", "retention_stored"))
    stat_clean, ga_used, gmlp_merged, scaled, merged, silu_done = map(sem, (
        "stat_clean", "ga_used", "gmlp_merged", "scaled", "merged", "silu_done"))
    squared, mean_sq, sqrt_done, select_in, tr_ready, xT_ready = map(sem, (
        "squared", "mean_sq", "sqrt_done", "select_in", "tr_ready", "xT_ready"))
    z_ready, z_used, gates_ready, diag_ready, aux_ready, dve_step = map(sem, (
        "z_ready", "z_used", "gates_ready", "diag_ready", "aux_ready", "dve_step"))
    cv_ready, mixw_ready, gate_biased, gate_ready, roped, state_ready = map(sem, (
        "cv_ready", "mixw_ready", "gate_biased", "gate_ready", "roped", "state_ready"))
    kd_ready, head_centred, head_squared, silu_scaled, new_state, state_stored = map(sem, (
        "kd_ready", "head_centred", "head_squared", "silu_scaled", "new_state", "state_stored"))
    gate2_ready, gate2_taken, y_clean, sum_clean, qk_normed, max_ready = map(sem, (
        "gate2_ready", "gate2_taken", "y_clean", "sum_clean", "qk_normed", "max_ready"))
    exp_done, probs_ready, x1_ready, top_ready, top_exp, routed = map(sem, (
        "exp_done", "probs_ready", "x1_ready", "top_ready", "top_exp", "routed"))
    table_ready, picked, gates_picked, gathered, xg_ready, g_cut_ready = map(sem, (
        "table_ready", "picked", "gates_picked", "gathered", "xg_ready", "g_cut_ready"))
    g_act_ready, act_ready, actT_done, actT_ready, gateT_done, gateT_ready = map(sem, (
        "g_act_ready", "act_ready", "actT_done", "actT_ready", "gateT_done", "gateT_ready"))
    y_ready, added, final_ready, moe_step, scattered, xg_rows = map(sem, (
        "y_ready", "added", "final_ready", "moe_step", "scattered", "xg_rows"))
    turned, b1_in, b1_split, expert_picked = map(sem, (
        "turned", "b1_in", "b1_split", "expert_picked"))

    block = ctx.enter_context(nc.Block())

    def aux_bank(name):
        return ps[:, AUX_FIRST + AUX_AT[name] % AUX_BANKS, :]

    def aux_filled(eng, name):
        eng.wait_ge(aux_ready, AUX_AT[name] + 1)

    def aux_taken(eng, name):
        n = AUX_AT[name]
        eng.wait_ge(aux_used[n % AUX_BANKS], n // AUX_BANKS + 1)

    def used(name):
        return aux_used[AUX_AT[name] % AUX_BANKS]

    def unit_arrived(eng, u):
        eng.wait_ge(unit_in[u % DENSE_SLOTS], 16 * (u // DENSE_SLOTS + 1))

    def unit_consumed(eng, u):
        kind, n = DENSE_ORDER[u]
        if kind == "ada":
            eng.wait_ge(aux_ready, AUX_AT[f"ada{n}"] + 1)
        else:
            eng.wait_ge(z_ready, 3 * (n + 1))

    def z_banks(idx):
        s = idx % 2
        return [(ps[:, s, :], 0, 0, HALF), (ps[:, 2 + s, :], 1, 0, HALF),
                (ps[0:64, 4, 0:256], 2, 0, 256), (ps[64:128, 4, 0:256], 2, 256, 256)]

    FINAL_BANKS = [6, 0, 2]
    TR_BANKS = [4, 0, 1, 3, 2]
    TR_NORM = [(2, 0, 8), (0, 0, 4), (1, 0, 4), (0, 4, 4), (1, 4, 4)]
    TR_LATER = [(0, 0, 4), (0, 4, 4), (1, 0, 4), (1, 4, 4), (2, 0, 8)]

    @block.sync
    def _(sp):
        def load_unit(u):
            if u >= DENSE_SLOTS:
                unit_consumed(sp, u - DENSE_SLOTS)
            sp.dma_start(ring[:, u % DENSE_SLOTS, :], ins["w_dense"][u, :, :]).then_inc(unit_in[u % DENSE_SLOTS], 16)

        sp.dma_start(silu_c, ins["c"]).then_inc(c_in, 16)
        load_unit(0)
        for j in range(4):
            sp.dma_start(mod_bias[32 * j:32 * j + 32], ins["b_ada"][j].partition_broadcast(32)).then_inc(mod_bias_in, 16)
        load_unit(1)
        sp.dma_start(R[:, 0:2, :], ins["x_prompt"].rearrange("(t p) d -> p t d", p=P)).then_inc(x_in, 16)
        sp.dma_start(R[0:64, 2, :], ins["x_sample"]).then_inc(x_in, 16)
        sp.dma_start(consts[:, 0:FIRST_CONSTS], ins["consts"][:, 0:FIRST_CONSTS]).then_inc(select_in, 16)
        sp.dma_start(ln_gain, ins["ln_mix_g"].partition_broadcast(P)).then_inc(ln_mix_in, 16)
        load_unit(2)
        load_unit(3)
        load_unit(4)
        sp.dma_start(consts[:, FIRST_CONSTS:], ins["consts"][:, FIRST_CONSTS:]).then_inc(consts_in, 16)
        for u in range(5, DENSE_UNITS):
            load_unit(u)

        for j in (0, 3, 4, 5, 1, 2):
            if j < DENSE_SLOTS:
                unit_consumed(sp, DENSE_UNITS - DENSE_SLOTS + j)
            elif j == DENSE_SLOTS:
                sp.wait_ge(merged, 3)
            sp.dma_start(ring[:, j, :], ins["w_moe"][0, j, :, :]).then_inc(unit_in[j], 16)
        sp.wait_ge(table_ready, 1)
        with sp.Fori(1, NEXP) as e:
            before = sp.value_load(table_i[0:1, bass.ds(MAX_BLOCKS + 1 + e, 1)], min_val=1, max_val=MAX_BLOCKS)
            for j in range(EXPERT_UNITS):
                sp.wait_ge(unit_used, EXPERT_UNITS * before + j)
                sp.dma_start(ring[:, j, :], ins["w_moe"][bass.ds(e, 1), j, :, :].rearrange("a p n -> p (a n)")).then_inc(unit_in[j], 16)
        for t in range(2):
            sp.wait_ge(final_ready, t + 1)
            sp.dma_start(outs["y_prompt"][t * P:(t + 1) * P, :], R[:, t, :]).then_inc(stored, 16)
        sp.wait_ge(final_ready, 3)
        sp.dma_start(outs["y_sample"], R[0:64, 2, :]).then_inc(stored, 16)
        sp.wait_ge(stored, 48)
        sp.wait_ge(kv_stored, 64)
        sp.wait_ge(gmlp_stored, 16)
        sp.wait_ge(retention_stored, 16)
        sp.wait_ge(state_stored, 16 * BATCH_S)


    @block.gpsimd
    def _(pool):
        aux_filled(pool, "ada0")
        pool.dma_start(params[:, :], ins["params"]).then_inc(params_in, 16)
        pool.dma_start(gate_bias_a, ins["b_gate"][0].partition_broadcast(P)).then_inc(gate_bias_in, 16)

        def load_cache(b):
            pool.dma_start(cache[0:64, b % 2, 0:512].rearrange("p (h r) -> p h r", h=KVH), ins["cache_kT"][b]).then_inc(cache_in[b % 2], 16)
            pool.dma_start(cache[:, b % 2, 512:768], ins["cache_v"][b]).then_inc(cache_in[b % 2], 16)

        for b in range(2):
            load_cache(b)
        pool.wait_ge(qk_normed, 3)
        pool.dma_start(outs["prompt_k"], V[:, 1, 0:256]).then_inc(kv_stored, 16)
        pool.dma_start(outs["prompt_v"], V[:, 1, 256:512]).then_inc(kv_stored, 16)
        pool.dma_start(outs["sample_k"], V[0:64, 2, 0:256]).then_inc(kv_stored, 16)
        pool.dma_start(outs["sample_v"], V[0:64, 2, 256:512]).then_inc(kv_stored, 16)
        for b in range(2, BATCH_S):
            aux_filled(pool, f"pv2{b - 2}")
            load_cache(b)

        aux_filled(pool, "oback1")
        pool.dma_start(gm_gain, ins["gm_ln_g"].partition_broadcast(P)).then_inc(gm_in, 16)
        pool.dma_start(gm_bias, ins["gm_ln_b"].partition_broadcast(P)).then_inc(gm_in, 16)
        pool.dma_start(mixT, ins["mixT"]).then_inc(gm_in, 16)
        pool.dma_start(mixT_s[0:64], ins["mixT_s"]).then_inc(gm_in, 16)

        def load_gate_bias(row, half):
            pool.dma_start(gate_bias, ins["b_gate"][row, HALF * half:HALF * half + HALF].partition_broadcast(P)).then_inc(gate_bias_in, 16)

        def add_gate_bias(buf, half, chunk, n):
            pool.wait_ge(gate_bias_in, 16 * n)
            pool.wait_ge(z_used, 4 * (chunk + 1))
            for t, r in enumerate(ROWS):
                v = buf[0:r, t, HALF * half:HALF * half + HALF]
                nc.gpsimd.tensor_tensor(v, v, gate_bias[0:r], ALU.add).then_inc(gate_biased, 1)
            pool.wait_ge(gate_biased, 3 * n)

        def load_state(b):
            pool.dma_start(V[0:64, b % 2, :].rearrange("p (h e) -> p h e", h=RH),
                           ins["state"][b].rearrange("h d e -> d h e")).then_inc(state_in[b % 2], 16)

        pool.wait_ge(gate_bias_in, 16)
        load_gate_bias(2, 0)
        pool.wait_ge(kv_stored, 64)
        for b in range(2):
            load_state(b)
        pool.wait_ge(gm_in, 64)
        pool.wait_ge(consts_in, 16)
        nc.gpsimd.tensor_tensor(mixT, mixT, const("causal").unsqueeze(1).to_broadcast([P, GG, 128]), ALU.mult).then_inc(mixw_ready, 1)
        nc.gpsimd.tensor_tensor(mixT_s[0:64], mixT_s[0:64], const("blockcausal")[0:64].unsqueeze(1).to_broadcast([64, GG, 64]), ALU.mult).then_inc(mixw_ready, 1)
        pool.wait_ge(z_used, 4 * (GA1 + 1))
        for t, r in enumerate(ROWS):
            nc.gpsimd.tensor_tensor(XG[0:r, t, :], XG[0:r, t, :], gate_bias_a[0:r], ALU.add).then_inc(gate_biased, 1)
        pool.wait_ge(cv_ready, 3)
        pool.dma_start(outs["sample_gmlp_v"], XC[0:64, 2, :]).then_inc(gmlp_stored, 16)
        add_gate_bias(R, 0, GC0, 2)
        load_gate_bias(2, 1)
        add_gate_bias(R, 1, GC1, 3)
        load_gate_bias(1, 0)
        aux_filled(pool, "rs11")
        pool.dma_start(ret_gain, ins["ret_norm_g"].partition_broadcast(P)).then_inc(ret_gain_in, 16)
        for b in range(BATCH_S):
            if b >= 2:
                pool.wait_ge(new_state, 2 * (b - 1))
                load_state(b)
            if b == 0:
                pool.wait_ge(roped, 3)
            else:
                aux_filled(pool, f"rs2{b - 1}1")
            nc.gpsimd.tensor_scalar(kd[0:64], XQK[0:64, 2, HALF:D], const("of_batch")[0:64, b:b + 1], None, ALU.mult).then_inc(kd_ready, 1)
            if b >= 1:
                pool.wait_ge(new_state, 2 * b)
                pool.dma_start(outs["sample_retention"][b - 1].rearrange("h d e -> d h e"),
                               V[0:64, 2, :].rearrange("p (h e) -> p h e", h=RH)).then_inc(state_stored, 16)
            if b == 2:
                pool.wait_ge(z_used, 4 * (RG1 + 1))
                pool.wait_ge(ret_gain_in, 16)
                for t, r in enumerate(ROWS):
                    nc.gpsimd.tensor_tensor(XG[0:r, t, :], XG[0:r, t, :], ret_gain[0:r], ALU.mult).then_inc(silu_scaled, 1)
            if b == 5:
                add_gate_bias(XC, 0, GB0, 4)
                load_gate_bias(1, 1)
            if b == 6:
                add_gate_bias(XC, 1, GB1, 5)
        pool.wait_ge(new_state, 2 * BATCH_S)
        pool.dma_start(outs["sample_retention"][BATCH_S - 1].rearrange("h d e -> d h e"),
                       V[0:64, 2, :].rearrange("p (h e) -> p h e", h=RH)).then_inc(state_stored, 16)
        pool.dma_start(outs["prompt_retention"].rearrange("h d e -> d h e"), state[0:64]).then_inc(retention_stored, 16)
        pool.dma_start(ln_ffn, ins["ln_ffn_g"].partition_broadcast(P)).then_inc(ln_ffn_in, 16)
        pool.wait_ge(gmlp_merged, 3)
        pool.dma_start(R[:, 0:2, :], ins["x_prompt"].rearrange("(t p) d -> p t d", p=P)).then_inc(x_again_in, 16)
        pool.dma_start(R[0:64, 2, :], ins["x_sample"]).then_inc(x_again_in, 16)
        pool.wait_ge(merged, 3)
        pool.dma_start(router_w, ins["router_w"]).then_inc(router_in, 16)
        splits = [0]

        def split(ins):
            splits[0] += 1
            ins.then_inc(b1_split, 1)
            pool.wait_ge(b1_split, splits[0])

        for half in range(2):
            for g in range(3):
                pool.dma_start(b1_whole[32 * g:32 * g + NEXP], ins["b1"][:, half, :]).then_inc(b1_in, 16)
            pool.wait_ge(b1_in, 48 * (half + 1))
            parts = b1_parts[:, D * half:D * half + D]
            split(nc.gpsimd.tensor_copy(parts[0:96], b1_whole[0:96]))
            split(nc.gpsimd.tensor_tensor(b1_rest[0:96], b1_whole[0:96], parts[0:96], ALU.subtract))
            split(nc.gpsimd.tensor_copy(parts[32:64], b1_rest[32:64]))
            split(nc.gpsimd.tensor_copy(parts[64:96], b1_rest[64:96]))
            split(nc.gpsimd.tensor_tensor(b1_rest[64:96], b1_rest[64:96], parts[64:96], ALU.subtract))
            split(nc.gpsimd.tensor_copy(parts[64:96], b1_rest[64:96]))
        pool.wait_ge(retention_stored, 16)
        nc.gpsimd.memset(y_blk, 0.0).then_inc(y_clean, 1)
        pool.wait_ge(y_clean, 1)
        for a in range(2):
            pool.dma_start(y_blk[64 * a:64 * a + NEXP], ins["b2"][:, HALF * a:HALF * a + HALF]).then_inc(b2_in, 16)
        pool.wait_ge(h_ready, 3)
        nc.gpsimd.memset(U[:, :, :], 0.0).then_inc(sum_clean, 1)

    @block.scalar
    def _(act):
        A = nc.scalar.activation

        def sqrt_of(cols, n, r=P):
            act.wait_ge(mean_sq, n)
            A(cols, cols, ACT.Sqrt).then_inc(sqrt_done, 1)

        def take_transposed(n, parts, first=0, last=5):
            for q in range(first, last):
                t, k0, nk = parts[q]
                act.wait_ge(tr_ready, 5 * n + q + 1)
                r = ROWS[t]
                A(xT[:, k0:k0 + nk, t * P:t * P + r], ps[:, TR_BANKS[q], :].rearrange("p (k m) -> p k m", m=r), ACT.Copy).then_inc(xT_ready, 1)

        into = {AQ0: (R, 0, ACT.Copy), AQ1: (R, HALF, ACT.Copy), AKV: (V, 0, ACT.Copy),
                CU0: (W, 0, ACT.Gelu_apprx_tanh), CU1: (W, HALF, ACT.Gelu_apprx_tanh),
                CV0: (XC, 0, ACT.Gelu_apprx_tanh), CV1: (XC, HALF, ACT.Gelu_apprx_tanh),
                RQ: (XQK, 0, ACT.Copy), RK: (XQK, HALF, ACT.Copy), RV0: (XV, 0, ACT.Copy), RV1: (XV, HALF, ACT.Copy),
                GA0: (XG, 0, ACT.Copy), GA1: (XG, HALF, ACT.Copy), GC0: (R, 0, ACT.Copy), GC1: (R, HALF, ACT.Copy),
                RG0: (XG, 0, ACT.Silu), RG1: (XG, HALF, ACT.Silu), GB0: (XC, 0, ACT.Copy), GB1: (XC, HALF, ACT.Copy),
                IN_UNITS: (W, 0, ACT.Copy), IN_UNITS + 1: (W, HALF, ACT.Copy)}
        z_pieces = iter(range(3 * (IN_UNITS + OUT_UNITS)))

        def take_pieces(count):
            for _ in range(count):
                n = next(z_pieces)
                idx, t = divmod(n, 3)
                buf, c0, func = into[idx]
                if n == 3 * RG0:
                    act.wait_ge(ga_used, 3)
                if n == 3 * GB0:
                    act.wait_ge(gmlp_stored, 16)
                for src, tile, c, w in z_banks(idx):
                    if tile == t:
                        act.wait_ge(z_ready, n + 1)
                        A(buf[0:ROWS[t], t, c0 + c:c0 + c + w], src, func).then_inc(z_used, 1)

        def gate(buf, biased, per_tile):
            for t, r in enumerate(ROWS):
                act.wait_ge(gate_biased, biased + t + 1)
                A(buf[0:r, t, :], buf[0:r, t, :], ACT.Sigmoid).then_inc(gate_ready, 1)

        act.wait_ge(c_in, 16)
        A(silu_c, silu_c, ACT.Silu).then_inc(silu_done, 1)
        act.wait_ge(x_in, 32)
        act.wait_ge(stat_clean, 1)
        for t in (2, 0, 1):
            A(W[0:ROWS[t], t, :], R[0:ROWS[t], t, :], ACT.Square, accum_out=stat[0:ROWS[t], t:t + 1]).then_inc(squared, 1)
        sqrt_of(stat[:, 0:3], 1)
        take_transposed(0, TR_NORM)
        take_pieces(6)
        for t in range(3):
            sqrt_of(stat[:, 24:40], 2 + t)
            take_pieces(1)
        for t in range(3):
            sqrt_of(stat[:, 40:44], 5 + t)

        def take_kT(t):
            name = f"kT{t}"
            aux_filled(act, name)
            A(kTa[0:64, :, t * P:t * P + ROWS[t]], aux_bank(name)[0:64, 0:4 * ROWS[t]].rearrange("p (h m) -> p h m", h=4), ACT.Copy).then_inc(used(name), 1)

        def take_qT(t):
            n = 2 if t == 2 else 4
            for q in range(n):
                name = f"qT{t}{q}"
                aux_filled(act, name)
                heads = slice(q * (QH // n), (q + 1) * (QH // n))
                if t == 2:
                    dst = qTs[0:64].rearrange("p b h t -> p h b t")[:, heads]
                    src = aux_bank(name)[0:64].rearrange("p (h b t) -> p h b t", b=BATCH_S, t=STEPS)
                else:
                    dst = qTa[0:64, heads, :]
                    src = aux_bank(name)[0:64].rearrange("p (h m) -> p h m", m=P)
                A(dst, src, ACT.Copy, scale=param("q_gain")[0:64]).then_inc(used(name), 1)

        softmaxes = [0]

        def softmax(count, width):
            softmaxes[0] += 1
            act.wait_ge(max_ready, softmaxes[0])
            for h in range(count):
                A(probs[:, h, 0:width], probs[:, h, 0:width], ACT.Exp, bias=stat[:, 48 + h:49 + h], accum_out=stat[:, 52 + h:53 + h])
            A(stat[:, 56:56 + count], stat[:, 60:60 + count], ACT.Exp).then_inc(exp_done, 1)

        for t in range(3):
            take_kT(t)
        for t in range(2):
            take_qT(t)
            for g in range(KVH):
                softmax(4, P * (t + 1))
                take_pieces(2)
                for k in range(t + 1):
                    name = f"pT{t}{g}{k}"
                    aux_filled(act, name)
                    A(pT[:, k, :], aux_bank(name), ACT.Copy).then_inc(used(name), 1)
        take_qT(2)
        for b in range(BATCH_S):
            softmax(1, 192)
            take_pieces(1)
            name = f"pT2{b}"
            aux_filled(act, name)
            A(pT[0:64, 1, 0:P], aux_bank(name)[0:64, P:2 * P], ACT.Copy)
            A(pT[:, 0, 0:P], aux_bank(name)[:, 0:P], ACT.Copy).then_inc(used(name), 1)
            name = f"pv2{b}"
            aux_filled(act, name)
            A(oT[0:64, :, b * STEPS:(b + 1) * STEPS], aux_bank(name)[0:64, 0:P].rearrange("p (h t) -> p h t", h=QH), ACT.Copy).then_inc(used(name), 1)
        for h in range(2):
            name = f"oback{h}"
            aux_filled(act, name)
            A(T[0:64, 2, HALF * h:HALF * h + HALF], aux_bank(name)[0:64], ACT.Copy).then_inc(used(name), 1)
        sqrt_of(stat[:, 8:11], 8)
        take_pieces(6)
        gate(XG, 0, 1)
        for t in range(2):
            for h in range(2):
                for src, dst in (("rqT", rqT), ("rkT", rkT)):
                    name = f"{src}{t}{h}"
                    aux_filled(act, name)
                    A(dst[0:64, 4 * h:4 * h + 4, :], aux_bank(name)[0:64].rearrange("p (h m) -> p h m", h=4), ACT.Copy).then_inc(used(name), 1)
                take_pieces(2)
                name = f"ro{t}{h}"
                aux_filled(act, name)
                A(U[:, t, HALF * h:HALF * h + HALF], aux_bank(name), ACT.Copy).then_inc(used(name), 1)
        for name, dst in (("rqT2", rqT), ("rkT2", rkT)):
            aux_filled(act, name)
            A(dst[0:64, :, 0:64], aux_bank(name)[0:64].rearrange("p (h m) -> p h m", h=8), ACT.Copy).then_inc(used(name), 1)
        take_pieces(2)
        aux_filled(act, "ro2")
        A(ro_s, aux_bank("ro2"), ACT.Copy).then_inc(used("ro2"), 1)
        gate(R, 6, 1)

        def square_heads(t):
            act.wait_ge(head_centred, t + 1)
            if t:
                act.wait_ge(mean_sq, 8 + t)
            A(squares[0:ROWS[t]], U[0:ROWS[t], t, :], ACT.Square).then_inc(head_squared, 1)
            sqrt_of(stat[:, 16:24], 9 + t)

        for b in range(BATCH_S):
            take_pieces(SAMPLE_PIECES[b])
            if b in (1, 3):
                square_heads(b // 2)
        gate(XC, 12, 1)
        for h in range(2):
            name = f"rback{h}"
            aux_filled(act, name)
            A(U[0:64, 2, HALF * h:HALF * h + HALF], aux_bank(name)[0:64], ACT.Copy).then_inc(used(name), 1)
        square_heads(2)
        take_transposed(1, TR_LATER, 0, 4)
        act.wait_ge(state_stored, 16 * BATCH_S)
        for s, rows, t in (("p", P, 0), ("s", 64, 2)):
            for h in range(2):
                name = f"g1{s}{h}"
                aux_filled(act, name)
                A(V[0:rows, t, HALF * h:HALF * h + HALF], aux_bank(name)[0:rows], ACT.Copy).then_inc(used(name), 1)
        take_pieces(2)
        take_transposed(1, TR_LATER, 4)
        for x in HALVES:
            name = f"shift1{x}"
            aux_filled(act, name)
            cols = slice(HALF * int(x[1]), HALF * int(x[1]) + HALF)
            if x[0] == "s":
                A(T[0:64, 2, cols], aux_bank(name)[0:64], ACT.Copy).then_inc(used(name), 1)
            else:
                A(T[:, 0, cols], aux_bank(name), ACT.Copy)
                A(T[:, 1, cols], aux_bank(name), ACT.Copy).then_inc(used(name), 1)
        for t, pieces in enumerate((2, 1, 1)):
            take_pieces(pieces)
            if t == 2:
                take_transposed(2, TR_LATER, 0, 4)
            act.wait_ge(x1_ready, t + 1)
            A(W[0:ROWS[t], t, :], R[0:ROWS[t], t, :], ACT.Square, accum_out=stat[0:ROWS[t], t:t + 1]).then_inc(squared, 1)
            sqrt_of(stat[:, t:t + 1], 12 + t)
        take_transposed(2, TR_LATER, 4)
        act.wait_ge(top_ready, 1)
        A(top_gate, top_gate, ACT.Exp).then_inc(top_exp, 1)
        for bank, (rows, t) in enumerate(((P, 0), (P, 0), (64, 2), (64, 2))):
            act.wait_ge(gate2_ready, bank + 1)
            A(V[0:rows, t, HALF * (bank % 2):HALF * (bank % 2) + HALF], ps[0:rows, bank, :], ACT.Copy).then_inc(gate2_taken, 1)

        def take_gathered(i):
            act.wait_ge(gathered, i)
            A(xg_s, ps[:, 3, :], ACT.Copy).then_inc(xg_rows, 1)

        def take_turned(i):
            act.wait_ge(turned, i)
            A(xgT, ps[:, 3, :].rearrange("p (c a s) -> p c a s", c=4, a=2), ACT.Copy).then_inc(xg_ready, 1)

        take_gathered(1)
        take_turned(1)
        aux_filled(act, "gT")
        A(gateT[:, 0:TOKENS], aux_bank("gT")[:, 0:TOKENS], ACT.Copy).then_inc(used("gT"), 1)
        aux_taken(act, "gT")
        act.sem_inc(gateT_ready, 1)
        act.wait_ge(b2_in, 32)
        act.sem_inc(y_ready, 1)
        n_blocks = act.value_load(table_i[0:1, MAX_BLOCKS:MAX_BLOCKS + 1], min_val=NEXP, max_val=MAX_BLOCKS - 1)
        with act.Fori(1, n_blocks + 1) as i:
            act.wait_ge(g_cut_ready, i)
            A(g_act, g_cut, ACT.Gelu_apprx_sigmoid).then_inc(g_act_ready, 1)
            take_gathered(i + 1)
            act.wait_ge(actT_done, i)
            A(actT, ps[:, 4, :].rearrange("p (c a s) -> p c a s", c=4, a=2), ACT.Copy).then_inc(actT_ready, 1)
            act.wait_ge(gateT_done, i)
            act.wait_ge(scattered, 3 * i)
            A(gateT[:, 0:TOKENS], ps[:, 5, 0:TOKENS], ACT.Copy).then_inc(gateT_ready, 1)
            take_turned(i + 1)
            act.wait_ge(unit_used, EXPERT_UNITS * i + 5)
            A(y_blk, ps[:, 2, :], ACT.Copy).then_inc(y_ready, 1)

    @block.vector
    def _(dve):
        X = nc.vector
        counts = {}

        def done(ins, signal=dve_step):
            counts[signal.name] = counts.get(signal.name, 0) + 1
            ins.then_inc(signal, 1)
            dve.wait_ge(signal, counts[signal.name])

        done(X.memset(stat[:, :], 1.0), stat_clean)

        def add_ada_bias(n):
            name = f"ada{n}"
            aux_filled(dve, name)
            X.tensor_tensor(mod[:, n, :], aux_bank(name)[:, 0:128], mod_bias[:, n // 4, 128 * (n % 4):128 * (n % 4) + 128], ALU.add).then_inc(used(name), 1)

        def root_mean_square(tiles, n):
            mean, root = stat[:, tiles], stat[:, 4 + tiles.start:4 + tiles.stop]
            done(X.tensor_scalar(mean, mean, 1.0 / D, EPS, ALU.mult, ALU.add), mean_sq)
            dve.wait_ge(sqrt_done, n)
            done(X.reciprocal(root, mean))

        def scale_gain(gain, n):
            for s, (out, r) in gains.items():
                for h in range(2):
                    name = f"gain{n}{s}{h}"
                    cols = slice(HALF * h, HALF * h + HALF)
                    aux_filled(dve, name)
                    X.scalar_tensor_tensor(out=out[:, cols], in0=aux_bank(name)[0:r], scalar=1.0, in1=gain[0:r, cols],
                                           op0=ALU.add, op1=ALU.mult).then_inc(used(name), 1)
            for x in HALVES:
                aux_taken(dve, f"gain{n}{x}")

        def normalise(t):
            r = ROWS[t]
            done(X.scalar_tensor_tensor(out=W[0:r, t, :], in0=R[0:r, t, :], scalar=stat[0:r, 4 + t:5 + t],
                                        in1=gains["s" if t == 2 else "p"][0][0:r], op0=ALU.mult, op1=ALU.mult))

        def shift():
            for x, tiles in (("s0", (2,)), ("s1", (2,)), ("p0", (0, 1)), ("p1", (0, 1))):
                name = f"shift0{x}"
                cols = slice(HALF * int(x[1]), HALF * int(x[1]) + HALF)
                aux_filled(dve, name)
                for t in tiles:
                    r = ROWS[t]
                    ins = X.tensor_tensor(T[0:r, t, cols], W[0:r, t, cols], aux_bank(name)[0:r], ALU.add)
                    if t == tiles[-1]:
                        ins.then_inc(used(name), 1)
                    else:
                        done(ins)

        dve.wait_ge(mod_bias_in, 64)
        add_ada_bias(2)
        add_ada_bias(3)
        dve.wait_ge(squared, 3)
        root_mean_square(slice(0, 3), 1)
        dve.wait_ge(ln_mix_in, 16)
        scale_gain(ln_gain, 0)
        for t in (2, 0, 1):
            normalise(t)
        add_ada_bias(0)
        add_ada_bias(1)
        shift()
        for x in HALVES:
            aux_taken(dve, f"shift0{x}")

        dve.wait_ge(params_in, 16)

        def head_rms(x, cols, scale, eps, n):
            r, heads, _ = x.shape
            sq = T[0:r, 1, 0:heads * HD].rearrange("p (h e) -> p h e", h=heads)
            done(X.tensor_tensor(sq, x, x, ALU.mult))
            done(X.tensor_reduce(cols[0:r], sq, AX.X, ALU.add))
            done(X.tensor_scalar(cols[0:r], cols[0:r], scale, eps, ALU.mult, ALU.add), mean_sq)
            dve.wait_ge(sqrt_done, n)
            done(X.reciprocal(cols[0:r], cols[0:r]))
            done(X.tensor_tensor(x, x, cols[0:r].unsqueeze(2).to_broadcast([r, heads, HD]), ALU.mult))

        for t, r in enumerate(ROWS):
            dve.wait_ge(z_used, 4 * AQ1 + (1, 2, 4)[t])
            head_rms(R[0:r, t, :].rearrange("p (h e) -> p h e", h=QH), stat[:, 24:40], 1.0, HD * EPS, 2 + t)
        for t, r in enumerate(ROWS):
            dve.wait_ge(z_used, 4 * AKV + (1, 2, 4)[t])
            head_rms(V[0:r, t, 0:256].rearrange("p (h e) -> p h e", h=KVH), stat[:, 40:44], 1.0 / HD, EPS, 5 + t)
            done(X.tensor_tensor(V[0:r, t, 0:256], V[0:r, t, 0:256], param("k_gain")[0:r], ALU.mult), qk_normed)
            if t < 2:
                add_ada_bias(4 + t)

        softmaxes = [0]

        def softmax(count, width, sink, ada=None):
            softmaxes[0] += 1
            done(X.tensor_reduce(stat[:, 60:60 + count], probs[:, 0:count, 0:width], AX.X, ALU.max))
            done(X.tensor_tensor(stat[:, 60:60 + count], stat[:, 60:60 + count], sink, ALU.max))
            done(X.tensor_scalar(stat[:, 48:48 + count], stat[:, 60:60 + count], -1.0, None, ALU.mult))
            done(X.tensor_tensor(stat[:, 60:60 + count], sink, stat[:, 60:60 + count], ALU.subtract), max_ready)
            if ada is not None:
                add_ada_bias(ada)
            dve.wait_ge(exp_done, softmaxes[0])
            done(X.tensor_tensor(stat[:, 52:52 + count], stat[:, 52:52 + count], stat[:, 56:56 + count], ALU.add))
            done(X.reciprocal(stat[:, 68:68 + count], stat[:, 52:52 + count]))
            done(X.tensor_tensor(probs[:, 0:count, 0:width], probs[:, 0:count, 0:width],
                                 stat[:, 68:68 + count].unsqueeze(2).to_broadcast([P, count, width]), ALU.mult), probs_ready)

        window = const("window")
        for t in range(2):
            for g in range(KVH):
                if t == 0:
                    name = f"sc0{g}0"
                    aux_filled(dve, name)
                    X.tensor_tensor(probs[:, :, 0:P], aux_bank(name).rearrange("p (h k) -> p h k", h=4),
                                    window[:, P:2 * P].unsqueeze(1).to_broadcast([P, 4, P]), ALU.add).then_inc(used(name), 1)
                    aux_taken(dve, name)
                else:
                    for k in range(2):
                        name = f"sc1{g}{k}"
                        aux_filled(dve, name)
                        X.tensor_tensor(probs[:, 2 * k:2 * k + 2, :], aux_bank(name).rearrange("p (h k) -> p h k", h=2),
                                        window.unsqueeze(1).to_broadcast([P, 2, 2 * P]), ALU.add).then_inc(used(name), 1)
                        aux_taken(dve, name)
                softmax(4, P * (t + 1), param("sinks")[:, 4 * g:4 * g + 4], 6 + 4 * t + g if 4 * t + g < 6 else None)
                name = f"pv{t}{g}"
                aux_filled(dve, name)
                X.tensor_copy(T[:, t, 256 * g:256 * g + 256], aux_bank(name)[:, 0:256]).then_inc(used(name), 1)
                aux_taken(dve, name)
        for b in range(BATCH_S):
            name = f"sc2{b}"
            aux_filled(dve, name)
            done(X.tensor_tensor(probs[:, 0, 0:P], aux_bank(name)[:, 0:P], const("cache_mask"), ALU.add))
            X.tensor_tensor(probs[:, 0, P:192], aux_bank(name)[:, P:192], new_mask[:, b, :], ALU.add).then_inc(used(name), 1)
            aux_taken(dve, name)
            softmax(1, 192, param("sink_rows"))
        def mix(t):
            r = ROWS[t]
            bias = param("mix_bias_s" if t == 2 else "mix_bias")
            for h in range(2):
                name = f"mix{t}{h}"
                aux_filled(dve, name)
                tmp = mix_tmp[0:r, 0:HALF]
                X.tensor_tensor(tmp.rearrange("p (g c) -> p g c", g=4), aux_bank(name)[0:r].rearrange("p (g c) -> p g c", g=4),
                                bias[0:r, 4 * h:4 * h + 4].unsqueeze(2).to_broadcast([r, 4, 128]), ALU.add).then_inc(used(name), 1)
                aux_taken(dve, name)
                done(X.tensor_tensor(W[0:r, t, HALF * h:HALF * h + HALF], W[0:r, t, HALF * h:HALF * h + HALF], tmp, ALU.mult))

        def rotate(t):
            r = ROWS[t]
            v = XQK[0:r, t, :].rearrange("p (h a f) -> p h a f", h=16, a=2)
            x1, x2 = v[:, :, 0, :], v[:, :, 1, :]
            c = cos[0:r, t, :].unsqueeze(1).to_broadcast([r, 16, 32])
            s = sin[0:r, t, :].unsqueeze(1).to_broadcast([r, 16, 32])
            tm = U[0:r, 0, :]
            ta = tm[:, 0:512].rearrange("p (h f) -> p h f", h=16)
            tb = tm[:, 512:1024].rearrange("p (h f) -> p h f", h=16)
            done(X.tensor_tensor(ta, x1, s, ALU.mult))
            done(X.tensor_tensor(tb, x2, s, ALU.mult))
            done(X.tensor_tensor(x1, x1, c, ALU.mult))
            done(X.tensor_tensor(x2, x2, c, ALU.mult))
            done(X.tensor_tensor(x1, x1, tb, ALU.subtract))
            done(X.tensor_tensor(x2, x2, ta, ALU.add))
            full = XQK[0:r, t, :].rearrange("p (h f) -> p h f", h=16)
            done(X.tensor_tensor(full, full, decay[0:r, t, :].unsqueeze(2).to_broadcast([r, 16, 64]), ALU.mult), roped)

        stats6 = stat[:, 80:92].rearrange("p (a b) -> p a b", a=2)
        dve.wait_ge(z_used, 4 * (CV1 + 1))
        for t, r in enumerate(ROWS):
            for h in range(2):
                done(X.bn_stats(stats6[0:r, h, :], XC[0:r, t, HALF * h:HALF * h + HALF]))
            done(X.bn_aggr(stat[0:r, 92:94], stats6[0:r]))
            done(X.tensor_copy(stat[0:r, 12 + t:13 + t], stat[0:r, 92:93]))
            done(X.tensor_scalar(stat[0:r, 8 + t:9 + t], stat[0:r, 93:94], EPS, None, ALU.add), mean_sq if t == 2 else dve_step)
        dve.wait_ge(sqrt_done, 8)
        done(X.reciprocal(stat[:, 8:11], stat[:, 8:11]))
        dve.wait_ge(z_used, 4 * (RK + 1))
        rotate(0)
        dve.wait_ge(gm_in, 64)
        for t, r in enumerate(ROWS):
            done(X.tensor_scalar(XC[0:r, t, :], XC[0:r, t, :], stat[0:r, 12 + t:13 + t], stat[0:r, 8 + t:9 + t], ALU.subtract, ALU.mult))
            done(X.tensor_tensor(XC[0:r, t, :], XC[0:r, t, :], gm_gain[0:r], ALU.mult))
            done(X.tensor_tensor(XC[0:r, t, :], XC[0:r, t, :], gm_bias[0:r], ALU.add), cv_ready)
        for t in range(3):
            if t < 2:
                rotate(t + 1)
            mix(t)
        aux_taken(dve, "oback0")
        aux_taken(dve, "oback1")
        for t, r in enumerate(ROWS):
            dve.wait_ge(gate_ready, t + 1)
            done(X.tensor_tensor(T[0:r, t, :], T[0:r, t, :], XG[0:r, t, :], ALU.mult), ga_used)

        causal4 = const("causal").unsqueeze(1).to_broadcast([P, 4, 128])
        for t in range(2):
            for h in range(2):
                name = f"ra{t}{h}"
                aux_filled(dve, name)
                X.tensor_tensor(ra[:, h, :].rearrange("p (h m) -> p h m", h=4), aux_bank(name).rearrange("p (h m) -> p h m", h=4), causal4, ALU.mult).then_inc(used(name), 1)
            for h in range(2):
                name = f"rs{t}{h}"
                aux_filled(dve, name)
                st = state[0:64, 4 * h:4 * h + 4, :]
                src = aux_bank(name)[0:64].rearrange("p (h m) -> p h m", h=4)
                dec = const("chunk_decay")[0:64, 4 * h:4 * h + 4].unsqueeze(2).to_broadcast([64, 4, RDV])
                if t == 0:
                    X.tensor_tensor(st, src, dec, ALU.mult).then_inc(used(name), 1)
                else:
                    X.tensor_tensor(st, src, st, ALU.add).then_inc(used(name), 1)
                    aux_taken(dve, name)
                    done(X.tensor_tensor(st, st, dec, ALU.mult), state_ready)
        aux_filled(dve, "ra2")
        X.tensor_tensor(ra[0:64, 0, :].rearrange("p (h m) -> p h m", h=8), aux_bank("ra2")[0:64].rearrange("p (h m) -> p h m", h=8),
                        const("blockcausal")[0:64].unsqueeze(1).to_broadcast([64, 8, 64]), ALU.mult).then_inc(used("ra2"), 1)

        def head_norm(t):
            r = ROWS[t]
            o3 = U[0:r, t, :].rearrange("p (h e) -> p h e", h=RH)
            done(X.tensor_reduce(stat[0:r, 16:24], o3, AX.X, ALU.add))
            done(X.tensor_scalar(stat[0:r, 16:24], stat[0:r, 16:24], 1.0 / RDV, None, ALU.mult))
            done(X.tensor_tensor(o3, o3, stat[0:r, 16:24].unsqueeze(2).to_broadcast([r, RH, RDV]), ALU.subtract), head_centred)
            dve.wait_ge(head_squared, t + 1)
            done(X.tensor_reduce(stat[0:r, 16:24], squares[0:r].rearrange("p (h e) -> p h e", h=RH), AX.X, ALU.add))
            done(X.tensor_scalar(stat[0:r, 16:24], stat[0:r, 16:24], 1.0 / RDV, EPS, ALU.mult, ALU.add), mean_sq)
            dve.wait_ge(sqrt_done, 9 + t)
            done(X.reciprocal(stat[0:r, 16:24], stat[0:r, 16:24]))
            done(X.tensor_tensor(o3, o3, stat[0:r, 16:24].unsqueeze(2).to_broadcast([r, RH, RDV]), ALU.mult))

        def merge_gmlp(t):
            r = ROWS[t]
            dve.wait_ge(gate_ready, 3 + t + 1)
            done(X.tensor_tensor(W[0:r, t, :], W[0:r, t, :], R[0:r, t, :], ALU.mult))
            done(X.tensor_tensor(T[0:r, t, :], T[0:r, t, :], W[0:r, t, :], ALU.add), gmlp_merged)

        def silu_times(t):
            r = ROWS[t]
            dve.wait_ge(silu_scaled, t + 1)
            done(X.tensor_tensor(U[0:r, t, :], U[0:r, t, :], XG[0:r, t, :], ALU.mult))

        aux_taken(dve, "ro2")
        for b in range(BATCH_S):
            if b:
                dve.wait_ge(state_stored, 16 * b)
            name = f"ri{b}"
            aux_filled(dve, name)
            mine = ro_s.rearrange("p (h t) -> p h t", h=RH)[:, :, b * STEPS:(b + 1) * STEPS]
            X.tensor_tensor(mine, aux_bank(name)[:, 0:64].rearrange("p (h t) -> p h t", h=RH), mine, ALU.add).then_inc(used(name), 1)
            for h in range(2):
                name = f"rs2{b}{h}"
                aux_filled(dve, name)
                st = V[0:64, b % 2, HALF * h:HALF * h + HALF]
                new = V[0:64, 2, HALF * h:HALF * h + HALF]
                X.tensor_tensor(new, aux_bank(name)[0:64], st, ALU.add).then_inc(used(name), 1)
                aux_taken(dve, name)
                n4 = new.rearrange("p (h e) -> p h e", h=4)
                done(X.tensor_tensor(n4, n4, const("chunk_decay")[0:64, 8 + 4 * h:12 + 4 * h].unsqueeze(2).to_broadcast([64, 4, RDV]), ALU.mult), new_state)
            if b in (1, 3):
                aux_taken(dve, f"ro{b // 2}0")
                aux_taken(dve, f"ro{b // 2}1")
                head_norm(b // 2)
            if b in (0, 2, 4):
                merge_gmlp(b // 2)
            if b in (5, 6):
                silu_times(b - 5)

        def merge_retention(t):
            r = ROWS[t]
            dve.wait_ge(gate_ready, 6 + t + 1)
            done(X.tensor_tensor(U[0:r, t, :], U[0:r, t, :], XC[0:r, t, :], ALU.mult))
            done(X.tensor_tensor(T[0:r, t, :], T[0:r, t, :], U[0:r, t, :], ALU.add), merged)

        merge_retention(0)
        merge_retention(1)
        aux_taken(dve, "rback0")
        aux_taken(dve, "rback1")
        head_norm(2)
        silu_times(2)
        merge_retention(2)

        dve.wait_ge(x_again_in, 32)
        for name in ("g1p0", "g1p1", "g1s0", "g1s1"):
            aux_taken(dve, name)
        dve.wait_ge(ln_ffn_in, 16)
        scale_gain(ln_ffn, 1)
        for x in HALVES:
            aux_taken(dve, f"shift1{x}")

        def residual(t, h):
            r = ROWS[t]
            cols = slice(HALF * h, HALF * h + HALF)
            dve.wait_ge(z_used, 4 * (IN_UNITS + h) + (1, 2, 4)[t])
            done(X.tensor_tensor(W[0:r, t, cols], W[0:r, t, cols], V[0:r, 2 if t == 2 else 0, cols], ALU.mult))
            done(X.tensor_tensor(R[0:r, t, cols], R[0:r, t, cols], W[0:r, t, cols], ALU.add), x1_ready if h else dve_step)

        for t in range(3):
            residual(t, 0)
        for t, r in enumerate(ROWS):
            residual(t, 1)
            dve.wait_ge(squared, 3 + t + 1)
            root_mean_square(slice(t, t + 1), 12 + t)
            normalise(t)
            done(X.tensor_tensor(T[0:r, t, :], W[0:r, t, :], T[0:r, t, :], ALU.add), h_ready)

        dve.wait_ge(retention_stored, 16)
        dve.wait_ge(params_in, 16)
        iota = const("iota")

        def pick_slots():
            X.tensor_tensor(pick, iota.unsqueeze(1).to_broadcast([P, 3, BLOCK]), sel_now[:, 0, :].unsqueeze(2).to_broadcast([P, 3, BLOCK]), ALU.is_equal).then_inc(picked, 1)

        logits = rtmp
        done(X.memset(logits, 0.0))
        done(X.memset(slot_of, -1.0))
        done(X.memset(pick_gate, 0.0))
        done(X.memset(gateT, 0.0), added)
        for t, r in enumerate(ROWS):
            name = f"lg{t}"
            aux_filled(dve, name)
            X.tensor_tensor(logits[0:r, t, :], aux_bank(name)[0:r, 0:NEXP], param("router_b")[0:r], ALU.add).then_inc(used(name), 1)
        for t in range(3):
            aux_taken(dve, f"lg{t}")
            done(X.max(top[:, t, :], logits[:, t, :]))
        done(X.tensor_tensor(top_gate, top[:, :, 0:TOPK], top[:, :, 0:1].to_broadcast([P, 3, TOPK]), ALU.subtract), top_ready)
        for t in range(3):
            done(X.max_index(top_i[:, t, :], top[:, t, :], logits[:, t, :]))
        done(X.tensor_copy(top_at, top_i[:, :, :]))
        choices = [P, 3, TOPK, NEXP]
        hot4 = hot.rearrange("p t (k e) -> p t k e", k=TOPK)
        hot_gate4 = hot_gate.rearrange("p t (k e) -> p t k e", k=TOPK)
        done(X.tensor_tensor(hot4, iota[:, 0:NEXP].unsqueeze(1).unsqueeze(1).to_broadcast(choices),
                             top_at[:, :, 0:TOPK].unsqueeze(3).to_broadcast(choices), ALU.is_equal))
        done(X.tensor_reduce(select_e, hot.rearrange("p t (k e) -> p t e k", k=TOPK), AX.X, ALU.add), routed)
        aux_filled(dve, "cnt")
        counted = rtmp[:, 1, :]
        X.tensor_copy(counted, aux_bank("cnt")[:, 0:NEXP]).then_inc(used("cnt"), 1)
        aux_taken(dve, "cnt")
        done(X.tensor_scalar(n_of, counted, float(BLOCK), 1.0, ALU.is_gt, ALU.add))
        for m in range(2, TOKENS // BLOCK):
            done(X.scalar_tensor_tensor(out=n_of, in0=counted, scalar=float(BLOCK * m), in1=n_of, op0=ALU.is_gt, op1=ALU.add))
        done(X.tensor_tensor_scan(out=cum_of, data0=ones[:, 0:NEXP], data1=n_of, initial=0.0, op0=ALU.mult, op1=ALU.add))
        done(X.tensor_scalar(passed[:, 0, :], cum_of, const("row"), None, ALU.is_le))
        done(X.tensor_tensor(passed[:, 1, :], passed[:, 0, :], n_of, ALU.mult))
        done(X.tensor_reduce(of_block, passed, AX.X, ALU.add))
        done(X.tensor_scalar(of_block[:, 0:1], of_block[:, 0:1], float(NEXP - 1), None, ALU.min))
        done(X.tensor_scalar(of_block[:, 1:2], of_block[:, 1:2], const("row"), -float(BLOCK), ALU.subtract, ALU.mult))
        done(X.tensor_tensor(table_rows, ident[:, 0:MAX_BLOCKS].unsqueeze(1).to_broadcast([P, 2, MAX_BLOCKS]),
                             of_block.unsqueeze(2).to_broadcast([P, 2, MAX_BLOCKS]), ALU.mult), diag_ready)
        for t, r in enumerate(ROWS):
            name = f"pos{t}"
            aux_filled(dve, name)
            s = slot_of[0:r, t, :]
            X.scalar_tensor_tensor(out=s, in0=aux_bank(name)[0:r, 0:NEXP], scalar=1.0, in1=select_e[0:r, t, :], op0=ALU.add, op1=ALU.mult).then_inc(used(name), 1)
            aux_taken(dve, name)
            done(X.tensor_scalar(s, s, 1.0, None, ALU.subtract))
        done(X.tensor_copy(sel_now[:, 0, :], slot_of[:, :, 0]))
        pick_slots()
        aux_filled(dve, "table")
        table = aux_bank("table")[:, 0:2 * MAX_BLOCKS].rearrange("p (a g) -> p a g", a=2)
        done(X.tensor_copy(slot_base, table[:, 1, :]))
        X.tensor_copy(table_i[0:1, 0:MAX_BLOCKS], table[0:1, 0, :]).then_inc(used("table"), 1)
        aux_taken(dve, "table")
        done(X.tensor_copy(table_i[0:1, MAX_BLOCKS:MAX_BLOCKS + 1], cum_of[0:1, NEXP - 1:NEXP]))
        done(X.tensor_tensor(table_i[0:1, MAX_BLOCKS + 1:MAX_BLOCKS + 1 + NEXP], cum_of[0:1, :], n_of[0:1, :], ALU.subtract), table_ready)
        dve.wait_ge(top_exp, 1)
        done(X.tensor_reduce(top_sum, top_gate, AX.X, ALU.add))
        done(X.reciprocal(top_sum, top_sum))
        done(X.tensor_tensor(top_gate, top_gate, top_sum.unsqueeze(2).to_broadcast([P, 3, TOPK]), ALU.mult))
        done(X.tensor_tensor(hot_gate4, hot4, top_gate.unsqueeze(3).to_broadcast(choices), ALU.mult))
        done(X.tensor_reduce(gate_e, hot_gate.rearrange("p t (k e) -> p t e k", k=TOPK), AX.X, ALU.add))
        done(X.tensor_copy(pick_gate[:, :, :, 0:NEXP], gate_e.unsqueeze(2).to_broadcast([P, 3, 2, NEXP])), gates_ready)
        done(X.tensor_copy(sel_now[:, 1, :], gate_e[:, :, 0]))


        def pick_tokens(at, e, waited):
            X.tensor_scalar(sel_now[:, 0, :], slot_of[:, :, bass.ds(e, 1)].rearrange("p t a -> p (t a)"), slot_base[:, bass.ds(at, 1)], None, ALU.subtract).then_inc(moe_step, 1)
            X.tensor_copy(sel_now[:, 1, :], gate_e[:, :, bass.ds(e, 1)].rearrange("p t a -> p (t a)")).then_inc(moe_step, 1)
            dve.wait_ge(moe_step, waited)
            pick_slots()

        def pick_expert(e):
            X.tensor_copy(pick_e[0:96], const("stack")[0:96, bass.ds(e, 1)].to_broadcast([96, BLOCK])).then_inc(expert_picked, 1)

        pick_expert(0)
        dve.wait_ge(sum_clean, 1)
        n_blocks = dve.value_load(table_i[0:1, MAX_BLOCKS:MAX_BLOCKS + 1], min_val=NEXP, max_val=MAX_BLOCKS - 1)
        with dve.Fori(1, n_blocks + 1) as i:
            dve.wait_ge(picked, i)
            dve.wait_ge(unit_used, EXPERT_UNITS * i - 1)
            X.tensor_tensor(pick_gate, pick.unsqueeze(2).to_broadcast([P, 3, 2, BLOCK]),
                            sel_now[:, 1, :].unsqueeze(2).unsqueeze(3).to_broadcast([P, 3, 2, BLOCK]), ALU.mult).then_inc(gates_picked, 1)
            e_next = dve.value_load(table_i[0:1, bass.ds(i, 1)], min_val=0, max_val=NEXP - 1)
            dve.wait_ge(gates_picked, i)
            dve.wait_ge(gathered, i)
            pick_tokens(i, e_next, 2 * i)
            dve.wait_ge(unit_used, EXPERT_UNITS * i + 1)
            X.tensor_scalar(g_cut, ps[:, 0, :], LIMIT, None, ALU.min).then_inc(g_cut_ready, 1)
            dve.wait_ge(unit_used, EXPERT_UNITS * i + 3)
            X.tensor_scalar(u_cut, ps[:, 1, :], LIMIT, -LIMIT, ALU.min, ALU.max).then_inc(dve_step, 1)
            pick_expert(e_next)
            dve.wait_ge(dve_step, i + counts["dve_step"])
            dve.wait_ge(g_act_ready, i)
            X.scalar_tensor_tensor(out=h_act, in0=u_cut, scalar=1.0, in1=g_act, op0=ALU.add, op1=ALU.mult).then_inc(act_ready, 1)
            for t, r in enumerate(ROWS):
                dve.wait_ge(scattered, 3 * i + t - 2)
                both = U[0:r, t, :].rearrange("p (a b) -> p a b", a=2)
                X.tensor_tensor(both, ps[0:r, 6:8, :], both, ALU.add).then_inc(added, 1)
        dve.wait_ge(added, 3 * n_blocks + 1)
        for t, r in enumerate(ROWS):
            X.tensor_tensor(U[0:r, t, :], U[0:r, t, :], V[0:r, 2 if t == 2 else 0, :], ALU.mult).then_inc(scaled, 1)
            dve.wait_ge(scaled, t + 1)
            X.tensor_tensor(R[0:r, t, :], R[0:r, t, :], U[0:r, t, :], ALU.add).then_inc(summed, 1)
            dve.wait_ge(summed, t + 1)
        for t, r in enumerate(ROWS):
            dve.wait_ge(scattered, 3 * n_blocks + t + 1)
            first = FINAL_BANKS[t]
            X.tensor_tensor(U[0:r, t, :].rearrange("p (a b) -> p a b", a=2), ps[0:r, first:first + 2, :],
                            V[0:r, 2 if t == 2 else 0, :].rearrange("p (a b) -> p a b", a=2), ALU.mult).then_inc(scaled, 1)
            dve.wait_ge(scaled, 3 + t + 1)
            X.tensor_tensor(R[0:r, t, :], R[0:r, t, :], U[0:r, t, :], ALU.add).then_inc(final_ready, 1)

    @block.tensor
    def _(pe):
        mm = nc.tensor.matmul

        def tr(out, in_, r, **kw):
            return nc.tensor.transpose(out, in_, ident[0:r, 0:r], **kw)

        def aux_free(name):
            n = AUX_AT[name]
            if n >= AUX_BANKS:
                pe.wait_ge(aux_used[n % AUX_BANKS], n // AUX_BANKS)

        def modulation(n):
            u, name = ada_unit(n), f"ada{n}"
            unit_arrived(pe, u)
            aux_free(name)
            wv = ring[:, u % DENSE_SLOTS, :].rearrange("p (k c) -> p k c", k=KD)
            for k in range(KD):
                for j in range(4):
                    last = mm(aux_bank(name)[32 * j:32 * j + 32, 0:128], silu_c[:, k, :], wv[:, k, 128 * j:128 * j + 128],
                              start=(k == 0), stop=(k == KD - 1), skip_group_check=True)
            last.then_inc(aux_ready, 1)

        def spread(n, bank, cols, r):
            for j in range(4):
                last = mm(bank[0:r, 128 * j:128 * j + 128], select[:, j, cols:cols + r], mod[:, n, :], start=True, stop=True)
            return last

        def spread_halves(kind, first, halves):
            for x in halves:
                name = f"{kind}{x}"
                aux_free(name)
                cols, r = (P, 64) if x[0] == "s" else (0, P)
                spread(first + int(x[1]), aux_bank(name), cols, r).then_inc(aux_ready, 1)

        def shifted(t, k0):
            for x in (("s0", "s1") if t == 2 else (f"p{k0 // 4}",)):
                aux_taken(pe, f"shift0{x}")

        def transpose_all(buf, parts, ready, n, first=0, last=5):
            for q in range(first, last):
                t, k0, nk = parts[q]
                ready(t, k0)
                r = ROWS[t]
                for k in range(nk):
                    tr_last = tr(ps[:, TR_BANKS[q], k * r:k * r + r], buf[0:r, t, (k0 + k) * P:(k0 + k + 1) * P], r)
                tr_last.then_inc(tr_ready, 1)

        z_pieces = iter(range(3 * (IN_UNITS + OUT_UNITS)))

        def project(count):
            for _ in range(count):
                idx, t = divmod(next(z_pieces), 3)
                u = proj_unit(idx)
                wv = ring[:, u % DENSE_SLOTS, :].rearrange("p (k c) -> p k c", k=KD)
                banks = z_banks(idx)
                if t == 0:
                    unit_arrived(pe, u)
                    if idx >= 2:
                        pe.wait_ge(z_used, 4 * (idx - 1))
                if t < 2:
                    for k in range(KD):
                        last = mm(banks[t][0], xT[:, k, t * P:t * P + P], wv[:, k, :], start=(k == 0), stop=(k == KD - 1))
                else:
                    if idx >= 1:
                        pe.wait_ge(z_used, 4 * idx)
                    for k in range(KD):
                        for a in range(2):
                            last = mm(banks[2 + a][0], xT[:, k, 2 * P:TOKENS], wv[:, k, 256 * a:256 * a + 256],
                                      start=(k == 0), stop=(k == KD - 1), skip_group_check=True)
                last.then_inc(z_ready, 1)

        pe.wait_ge(silu_done, 1)
        for kind, chunks in (("gain0", (2, 3)), ("shift0", (0, 1))):
            for n in chunks:
                modulation(n)
            pe.wait_ge(select_in, 16)
            for n in chunks:
                aux_taken(pe, f"ada{n}")
            spread_halves(kind, chunks[0], HALVES)
        transpose_all(T, TR_NORM, shifted, 0)
        pe.wait_ge(xT_ready, 5)
        project(9)
        modulation(4)
        modulation(5)

        pe.wait_ge(consts_in, 16)
        for t, r in enumerate(ROWS):
            pe.wait_ge(qk_normed, t + 1)
            name = f"kT{t}"
            aux_free(name)
            for g in range(KVH):
                last = tr(aux_bank(name)[0:64, g * r:g * r + r], V[0:r, t, g * HD:(g + 1) * HD], r)
            last.then_inc(aux_ready, 1)

        def transpose_queries(t):
            n, r = (2, 64) if t == 2 else (4, P)
            for q in range(n):
                name = f"qT{t}{q}"
                aux_free(name)
                for m in range(QH // n):
                    h = q * (QH // n) + m
                    last = tr(aux_bank(name)[0:64, m * r:m * r + r], R[0:r, t, h * HD:(h + 1) * HD], r)
                last.then_inc(aux_ready, 1)
            for q in range(n):
                aux_taken(pe, f"qT{t}{q}")

        softmaxes = 0
        for t in range(3):
            aux_taken(pe, f"kT{t}")
        for t in range(2):
            transpose_queries(t)
            for g in range(KVH):
                for k in range(t + 1):
                    name = f"sc{t}{g}{k}"
                    aux_free(name)
                    n, width = (4, P) if t == 0 else (2, 2 * P)
                    for m in range(n):
                        last = mm(aux_bank(name)[:, m * width:(m + 1) * width], qTa[0:64, 4 * g + n * k + m, :],
                                  kTa[0:64, g, 0:width], start=True, stop=True)
                    last.then_inc(aux_ready, 1)
                if 4 * t + g < 6:
                    modulation(6 + 4 * t + g)
                project(2)
                softmaxes += 1
                pe.wait_ge(probs_ready, softmaxes)
                for k in range(t + 1):
                    name = f"pT{t}{g}{k}"
                    aux_free(name)
                    for h in range(GROUP):
                        last = tr(aux_bank(name)[:, h * P:h * P + P], probs[:, h, k * P:k * P + P], P)
                    last.then_inc(aux_ready, 1)
                name = f"pv{t}{g}"
                aux_free(name)
                for k in range(t + 1):
                    aux_taken(pe, f"pT{t}{g}{k}")
                for h in range(GROUP):
                    for k in range(t + 1):
                        last = mm(aux_bank(name)[:, h * HD:(h + 1) * HD], pT[:, k, h * P:h * P + P],
                                  V[:, k, 256 + g * HD:256 + (g + 1) * HD], start=(k == 0), stop=(k == t))
                last.then_inc(aux_ready, 1)
        transpose_queries(2)
        for b in range(BATCH_S):
            name = f"sc2{b}"
            aux_free(name)
            pe.wait_ge(cache_in[b % 2], 32 * (b // 2 + 1))
            keys = cache[0:64, b % 2, 0:512].rearrange("p (h r) -> p h r", h=KVH)
            for g in range(KVH):
                q = qTs[0:64, b, GROUP * g:GROUP * (g + 1), :].rearrange("p h t -> p (h t)")
                mm(aux_bank(name)[32 * g:32 * g + 32, 0:P], q, keys[:, g, :], start=True, stop=True, skip_group_check=True)
                last = mm(aux_bank(name)[32 * g:32 * g + 32, P:192], q, kTa[0:64, g, SEQ:TOKENS], start=True, stop=True, skip_group_check=True)
            last.then_inc(aux_ready, 1)
            project(1)
            softmaxes += 1
            pe.wait_ge(probs_ready, softmaxes)
            name = f"pT2{b}"
            aux_free(name)
            tr(aux_bank(name)[:, 0:P], probs[:, 0, 0:P], P)
            tr(aux_bank(name)[0:64, P:2 * P], probs[:, 0, P:192], P).then_inc(aux_ready, 1)
            name = f"pv2{b}"
            aux_free(name)
            aux_taken(pe, f"pT2{b}")
            for g in range(KVH):
                out = aux_bank(name)[0:64, 32 * g:32 * g + 32]
                mm(out, cache[:, b % 2, 512 + g * HD:512 + (g + 1) * HD], pT[:, 0, 32 * g:32 * g + 32], start=True, stop=False)
                last = mm(out, V[0:64, 2, 256 + g * HD:256 + (g + 1) * HD], pT[0:64, 1, 32 * g:32 * g + 32], start=False, stop=True)
            last.then_inc(aux_ready, 1)
        for h in range(2):
            name = f"oback{h}"
            aux_free(name)
            aux_taken(pe, f"pv2{BATCH_S - 1}")
            for m in range(8):
                last = tr(aux_bank(name)[0:64, m * HD:(m + 1) * HD], oT[0:64, 8 * h + m, :], 64)
            last.then_inc(aux_ready, 1)

        for t, r in enumerate(ROWS):
            project(1)
            pe.wait_ge(cv_ready, t + 1)
            pe.wait_ge(mixw_ready, 2)
            w = mixT_s if t == 2 else mixT
            for h in range(2):
                name = f"mix{t}{h}"
                aux_free(name)
                for g in range(4 * h, 4 * h + 4):
                    last = mm(aux_bank(name)[0:r, (g % 4) * P:(g % 4) * P + P], w[0:r, g, :], XC[0:r, t, g * P:(g + 1) * P], start=True, stop=True)
                last.then_inc(aux_ready, 1)
            project(1)
        pe.wait_ge(roped, 3)
        for t in range(2):
            for h in range(2):
                for kind, c0 in (("rqT", 0), ("rkT", HALF)):
                    name = f"{kind}{t}{h}"
                    aux_free(name)
                    for n in range(4):
                        c = c0 + (4 * h + n) * RDK
                        last = tr(aux_bank(name)[0:64, n * P:n * P + P], XQK[:, t, c:c + RDK], P)
                    last.then_inc(aux_ready, 1)
                project(1)
                name = f"ra{t}{h}"
                aux_free(name)
                aux_taken(pe, f"rqT{t}{h}")
                aux_taken(pe, f"rkT{t}{h}")
                for n in range(4):
                    last = mm(aux_bank(name)[:, n * P:n * P + P], rkT[0:64, 4 * h + n, :], rqT[0:64, 4 * h + n, :], start=True, stop=True)
                last.then_inc(aux_ready, 1)
                project(1)
                name = f"ro{t}{h}"
                aux_free(name)
                aux_taken(pe, f"ra{t}{h}")
                if t == 1:
                    aux_taken(pe, f"rs0{h}")
                for n in range(4):
                    hh = 4 * h + n
                    out = aux_bank(name)[:, n * P:n * P + P]
                    last = mm(out, ra[:, h, n * P:n * P + P], XV[:, t, hh * RDV:(hh + 1) * RDV], start=True, stop=(t == 0))
                    if t == 1:
                        last = mm(out, rqT[0:64, hh, :], state[0:64, hh, :], start=False, stop=True)
                last.then_inc(aux_ready, 1)
            for h in range(2):
                name = f"rs{t}{h}"
                aux_free(name)
                for n in range(4):
                    hh = 4 * h + n
                    last = mm(aux_bank(name)[0:64, n * P:n * P + P], XQK[:, t, HALF + hh * RDK:HALF + (hh + 1) * RDK],
                              XV[:, t, hh * RDV:(hh + 1) * RDV], start=True, stop=True)
                last.then_inc(aux_ready, 1)
        for name, c0 in (("rqT2", 0), ("rkT2", HALF)):
            aux_free(name)
            for n in range(RH):
                last = tr(aux_bank(name)[0:64, n * 64:n * 64 + 64], XQK[0:64, 2, c0 + n * RDK:c0 + (n + 1) * RDK], 64)
            last.then_inc(aux_ready, 1)
        project(1)
        aux_free("ra2")
        aux_taken(pe, "rqT2")
        aux_taken(pe, "rkT2")
        for n in range(RH):
            last = mm(aux_bank("ra2")[0:64, n * 64:n * 64 + 64], rkT[0:64, n, 0:64], rqT[0:64, n, 0:64], start=True, stop=True)
        last.then_inc(aux_ready, 1)
        project(1)
        aux_free("ro2")
        aux_taken(pe, "ra2")
        for n in range(RH):
            last = mm(aux_bank("ro2")[:, n * 64:n * 64 + 64], XV[0:64, 2, n * RDV:(n + 1) * RDV], ra[0:64, 0, n * 64:n * 64 + 64], start=True, stop=True)
        last.then_inc(aux_ready, 1)
        for b in range(BATCH_S):
            pe.wait_ge(state_in[b % 2], 16 * (b // 2 + 1))
            name = f"ri{b}"
            aux_free(name)
            for n in range(RH):
                last = mm(aux_bank(name)[:, n * STEPS:(n + 1) * STEPS], V[0:64, b % 2, n * RDV:(n + 1) * RDV],
                          rqT[0:64, n, b * STEPS:(b + 1) * STEPS], start=True, stop=True)
            last.then_inc(aux_ready, 1)
            pe.wait_ge(kd_ready, b + 1)
            for h in range(2):
                name = f"rs2{b}{h}"
                aux_free(name)
                for n in range(4):
                    hh = 4 * h + n
                    last = mm(aux_bank(name)[0:64, n * P:n * P + P], kd[0:64, hh * RDK:(hh + 1) * RDK],
                              XV[0:64, 2, hh * RDV:(hh + 1) * RDV], start=True, stop=True)
                last.then_inc(aux_ready, 1)
            project(SAMPLE_PIECES[b])
        aux_taken(pe, f"ri{BATCH_S - 1}")
        for h in range(2):
            name = f"rback{h}"
            aux_free(name)
            for n in range(4):
                hh = 4 * h + n
                last = tr(aux_bank(name)[0:64, n * P:n * P + P], ro_s[:, hh * 64:hh * 64 + 64], P)
            last.then_inc(aux_ready, 1)


        def is_merged(t, k0):
            pe.wait_ge(merged, t + 1)

        transpose_all(T, TR_LATER, is_merged, 1, 0, 4)
        spread_halves("g1", 4, ("p0", "p1", "s0", "s1"))
        pe.wait_ge(xT_ready, 9)
        project(2)
        transpose_all(T, TR_LATER, is_merged, 1, 4)
        spread_halves("gain1", 8, HALVES)
        spread_halves("shift1", 6, HALVES)
        pe.wait_ge(xT_ready, 10)
        project(4)
        pe.wait_ge(z_used, 4 * (IN_UNITS + 2))

        def is_normed(t, k0):
            pe.wait_ge(h_ready, t + 1)

        def router_logits(t):
            r, name = ROWS[t], f"lg{t}"
            aux_free(name)
            for k in range(KD):
                last = mm(aux_bank(name)[0:r, 0:NEXP], xT[:, k, t * P:t * P + r], router_w[:, k, :], start=(k == 0), stop=(k == KD - 1))
            last.then_inc(aux_ready, 1)

        transpose_all(T, TR_LATER, is_normed, 2, 0, 4)
        pe.wait_ge(router_in, 16)
        for t in range(2):
            pe.wait_ge(xT_ready, 10 + 2 * (t + 1))
            router_logits(t)
        transpose_all(T, TR_LATER, is_normed, 2, 4)
        pe.wait_ge(xT_ready, 15)
        router_logits(2)
        for bank, (cols, r) in enumerate(((0, P), (0, P), (P, 64), (P, 64))):
            spread(10 + bank % 2, ps[:, bank, :], cols, r).then_inc(gate2_ready, 1)
        pe.wait_ge(routed, 1)
        aux_free("cnt")
        for s, r in enumerate(ROWS):
            last = mm(aux_bank("cnt")[:, 0:NEXP], ones[0:r, :], select_e[0:r, s, :], start=(s == 0), stop=(s == 2))
        last.then_inc(aux_ready, 1)
        for t, r in enumerate(ROWS):
            name = f"pos{t}"
            aux_free(name)
            for s in range(t + 1):
                w = const("before") if s == t else ones
                last = mm(aux_bank(name)[0:r, 0:NEXP], w[0:ROWS[s], 0:r], select_e[0:ROWS[s], s, :], start=(s == 0), stop=(s == t))
            last.then_inc(aux_ready, 1)
        pe.wait_ge(diag_ready, 1)
        aux_free("table")
        mm(aux_bank("table")[:, 0:2 * MAX_BLOCKS], ones[0:MAX_BLOCKS, :], table_rows[0:MAX_BLOCKS].rearrange("p a g -> p (a g)"),
           start=True, stop=True).then_inc(aux_ready, 1)

        def gather(n):
            pe.wait_ge(picked, n)
            for t, r in enumerate(ROWS):
                for a in range(2):
                    last = mm(ps[64 * a:64 * a + 64, 3, :], pick[0:r, t, :], T[0:r, t, HALF * a:HALF * a + HALF],
                              start=(t == 0), stop=(t == 2), skip_group_check=True)
            last.then_inc(gathered, 1)

        def turn(n):
            pe.wait_ge(xg_rows, n)
            for c in range(4):
                last = tr(ps[:, 3, c * P:(c + 1) * P], xg_s[:, c * P:(c + 1) * P], P)
            last.then_inc(turned, 1)

        def scatter_tile(t, first):
            for a in range(2):
                last = mm(ps[:, first + a, :], gateT[64 * a:64 * a + 64, t * P:(t + 1) * P], y_blk[64 * a:64 * a + 64, :], start=True, stop=True)
            last.then_inc(scattered, 1)

        def scatter(n, t):
            pe.wait_ge(added, 3 * n + t - 2)
            scatter_tile(t, 6)

        def filled(j):
            return DENSE_UNITS // DENSE_SLOTS if j < DENSE_SLOTS else 0

        pe.wait_ge(gate2_taken, 4)
        gather(1)
        turn(1)
        pe.wait_ge(gates_ready, 1)
        aux_free("gT")
        for t, r in enumerate(ROWS):
            last = tr(aux_bank("gT")[:, t * P:t * P + r], pick_gate[0:r, t, :, :], r)
        last.then_inc(aux_ready, 1)
        for name in ("pos2", "table", "gT"):
            aux_taken(pe, name)
        pe.wait_ge(b1_split, 12)
        pe.sem_inc(unit_used, EXPERT_UNITS - 1)
        n_blocks = pe.value_load(table_i[0:1, MAX_BLOCKS:MAX_BLOCKS + 1], min_val=NEXP, max_val=MAX_BLOCKS - 1)
        with pe.Fori(1, n_blocks + 1) as i:
            e = pe.value_load(table_i[0:1, bass.ds(i - 1, 1)], min_val=0, max_val=NEXP - 1)
            pe.wait_ge(xg_ready, i)
            pe.wait_ge(expert_picked, i)
            for half in range(2):
                for j in (2 * half, 2 * half + 1):
                    pe.wait_ge(unit_in[j], 16 * e + 16 * (filled(j) + 1))
                    wv = ring[:, j, :].rearrange("p (k c) -> p k c", k=4)
                    for k in range(4):
                        for a in range(2):
                            last = mm(ps[64 * a:64 * a + 64, half, :], xgT[:, k, j % 2, :], wv[:, k, HALF * a:HALF * a + HALF],
                                      start=(j % 2 == 0 and k == 0), stop=False, skip_group_check=True)
                    if j % 2 == 0:
                        last.then_inc(unit_used, 1)
                for a in range(2):
                    last = mm(ps[64 * a:64 * a + 64, half, :], pick_e[0:96], b1_parts[0:96, D * half + HALF * a:D * half + HALF * a + HALF],
                              start=False, stop=True, skip_group_check=True)
                last.then_inc(unit_used, 1)
            pe.wait_ge(y_ready, i)
            pe.wait_ge(gateT_ready, i)
            scatter(i, 0)
            gather(i + 1)
            pe.wait_ge(act_ready, i)
            for c in range(4):
                last = tr(ps[:, 4, c * P:(c + 1) * P], h_act[:, c * P:(c + 1) * P], P)
            last.then_inc(actT_done, 1)
            pe.wait_ge(gates_picked, i)
            for t, r in enumerate(ROWS):
                last = tr(ps[:, 5, t * P:t * P + r], pick_gate[0:r, t, :, :], r)
            last.then_inc(gateT_done, 1)
            scatter(i, 1)
            pe.wait_ge(actT_ready, i)
            for j in (4, 5):
                pe.wait_ge(unit_in[j], 16 * e + 16 * (filled(j) + 1))
                wv = ring[:, j, :].rearrange("p (k c) -> p k c", k=4)
                for k in range(4):
                    for a in range(2):
                        last = mm(ps[64 * a:64 * a + 64, 2, :], actT[:, k, j - 4, :], wv[:, k, HALF * a:HALF * a + HALF],
                                  start=(j == 4 and k == 0), stop=(j == 5 and k == 3), skip_group_check=True)
                last.then_inc(unit_used, 1)
                if j == 4:
                    turn(i + 1)
                    scatter(i, 2)
        pe.wait_ge(y_ready, n_blocks + 1)
        pe.wait_ge(gateT_ready, n_blocks + 1)
        pe.wait_ge(added, 3 * n_blocks + 1)
        for t in range(3):
            scatter_tile(t, FINAL_BANKS[t])


def shape_constants():
    c = {name: np.zeros((P, width), np.float32) for name, width in CONST_WIDTHS}
    p = np.arange(P)
    c["ident"][:] = np.eye(P)
    c["causal"][:] = p[:, None] <= p[None, :]
    q = np.arange(64)
    c["blockcausal"][:64] = (q[:, None] // STEPS == q[None, :] // STEPS) & (q[:, None] <= q[None, :])
    sel = np.zeros((P, 4, 192), np.float32)
    for j in range(4):
        sel[32 * j, j, :P] = 1
        sel[32 * j + 1 + q // STEPS, j, P + q] = 1
    c["select"][:] = sel.reshape(P, -1)
    pos = np.concatenate([np.arange(SEQ), PAST + q % STEPS, np.zeros(64)]).astype(np.float32)
    freq = np.float32(10000.0) ** (-np.arange(0, RDK, 2, dtype=np.float32) / np.float32(RDK))
    angle = (pos[:, None] * freq[None, :].astype(np.float32)).astype(np.float32).astype(np.float64).reshape(3, P, 32)
    c["cos"][:] = np.cos(angle).transpose(1, 0, 2).reshape(P, -1)
    c["sin"][:] = np.sin(angle).transpose(1, 0, 2).reshape(P, -1)
    gamma = 1.0 - 2.0 ** (-5.0 - np.arange(RH))
    in_chunk = np.concatenate([np.arange(P), np.arange(P), q % STEPS, np.zeros(64)])
    up = gamma[None] ** (in_chunk[:, None] + 1)
    decay = np.concatenate([up, RDK ** -0.5 / up], 1).reshape(3, P, 16)
    c["decay"][:] = decay.transpose(1, 0, 2).reshape(P, -1)
    c["chunk_decay"][:] = np.concatenate([gamma ** P, gamma ** STEPS])
    c["iota"][:] = np.arange(64)
    rel = p[:, None] + P - np.arange(2 * P)[None, :]
    c["window"][:] = np.where((rel >= 0) & (rel < P), 0, MASKED)
    step = p % STEPS
    c["cache_mask"][:] = np.where(p[None, :] > step[:, None], 0, MASKED)
    own = (q[None, None, :] // STEPS == np.arange(BATCH_S)[None, :, None]) & (q[None, None, :] % STEPS <= step[:, None, None])
    c["new_mask"][:] = np.where(own, 0, MASKED).reshape(P, -1)
    c["before"][:] = p[:, None] < p[None, :]
    c["ones"][:] = 1
    c["row"][:, 0] = p
    c["stack"][:] = p[:, None] % NEXP == np.arange(NEXP)
    c["of_batch"][:64] = q[:, None] // STEPS == np.arange(BATCH_S)[None, :]
    return np.concatenate([c[name] for name, _ in CONST_WIDTHS], 1)


def lay_out(x):
    x = {k: np.asarray(v) for k, v in x.items()}
    f = np.float32
    c = np.zeros((32, D), f)
    c[0:1] = x["c_prompt"]
    c[1:1 + BATCH_S] = x["c_sample"]

    def units(w):
        return w.reshape(KD, P, -1, HALF).transpose(2, 1, 0, 3).reshape(-1, P, KD * HALF)

    w_ada = units(x["w_ada"][0])
    w_proj = np.concatenate([units(x["w_in"][0])[IN_ORDER], units(x["w_out"][0])])
    w1 = x["moe_w1"][0].reshape(NEXP, 2, 4, P, 2, D).transpose(0, 4, 1, 3, 2, 5).reshape(NEXP, 4, P, 4 * D)
    w2 = x["moe_w2"][0].reshape(NEXP, 2, 4, P, D).transpose(0, 1, 3, 2, 4).reshape(NEXP, 2, P, 4 * D)
    params = {name: np.zeros((P, width), f) for name, width in PARAM_WIDTHS}
    params["k_gain"][:] = np.tile(x["k_norm_g"][0], KVH)
    params["sinks"][:] = x["attn_sinks"][0]
    params["sink_rows"][:, 0] = np.repeat(x["attn_sinks"][0], STEPS)
    params["q_gain"][:, 0] = np.tile(x["q_norm_g"][0], 2)
    params["router_b"][:] = x["router_b"][0]
    params["mix_bias"][:] = x["gm_bs"][0].T
    params["mix_bias_s"][:] = np.tile(x["gm_bs"][0].T[:STEPS], (P // STEPS, 1))
    ws = x["gm_ws"][0].transpose(2, 0, 1)
    return {
        "c": np.ascontiguousarray(c.T.reshape(KD, P, 32).transpose(1, 0, 2)),
        "x_prompt": x["x_prompt"][0], "x_sample": x["x_sample"].reshape(-1, D),
        "consts": shape_constants(),
        "params": np.concatenate([params[name] for name, _ in PARAM_WIDTHS], 1),
        "w_dense": np.stack([w_ada[n] if kind == "ada" else w_proj[n] for kind, n in DENSE_ORDER]),
        "w_moe": np.concatenate([w1, w2], 1),
        "b_ada": np.ascontiguousarray(x["b_ada"][0].reshape(3, 4, 4, 128).transpose(2, 0, 1, 3).reshape(4, 3, HALF)), "b1": x["moe_b1"][0].reshape(NEXP, 2, D), "b2": x["moe_b2"][0],
        "b_gate": x["b_gate"][0].reshape(3, D),
        "ln_mix_g": x["ln_mix_g"][0], "ln_ffn_g": x["ln_ffn_g"][0], "ret_norm_g": x["ret_norm_g"][0],
        "gm_ln_g": x["gm_ln_g"][0], "gm_ln_b": x["gm_ln_b"][0],
        "mixT": np.ascontiguousarray(ws),
        "mixT_s": np.ascontiguousarray(np.tile(ws[:STEPS, :, :STEPS], (BATCH_S, 1, BATCH_S))),
        "state": x["state_retention"][0],
        "cache_kT": np.ascontiguousarray(x["cache_attn_k"][0].transpose(0, 3, 2, 1)),
        "cache_v": x["cache_attn_v"][0].reshape(BATCH_S, P, KVH * HD),
        "router_w": np.ascontiguousarray(x["router_w"][0].reshape(KD, P, NEXP).transpose(1, 0, 2)),
    }


OUT_SHAPES = {
    "y_prompt": (SEQ, D), "y_sample": (BATCH_S * STEPS, D), "prompt_k": (P, KVH * HD), "prompt_v": (P, KVH * HD),
    "prompt_retention": (RH, RDK, RDV), "sample_k": (BATCH_S * STEPS, KVH * HD), "sample_v": (BATCH_S * STEPS, KVH * HD),
    "sample_retention": (BATCH_S, RH, RDK, RDV), "sample_gmlp_v": (BATCH_S * STEPS, D),
}


def kernel(**inputs):
    import concourse.bacc as bacc
    from concourse.bass_utils import run_bass_kernel_spmd

    arrays = lay_out(inputs)
    nc = bacc.Bacc("TRN2", target_bir_lowering=False, num_devices=1)
    ins = {name: nc.dram_tensor("in_" + name, a.shape, mybir.dt.from_np(a.dtype), kind="ExternalInput").ap() for name, a in arrays.items()}
    outs = {name: nc.dram_tensor("out_" + name, shape, FP32, kind="ExternalOutput").ap() for name, shape in OUT_SHAPES.items()}
    hybrid_step_kernel(nc, ins, outs)
    r = run_bass_kernel_spmd(nc, [{"in_" + name: a for name, a in arrays.items()}], core_ids=[0]).results[0]
    got = {name: r["out_" + name] for name in OUT_SHAPES}
    return (got["y_prompt"].reshape(1, SEQ, D), got["y_sample"].reshape(BATCH_S, STEPS, D),
            got["prompt_k"].reshape(1, 1, P, KVH, HD), got["prompt_v"].reshape(1, 1, P, KVH, HD),
            got["prompt_retention"].reshape(1, 1, RH, RDK, RDV),
            got["sample_k"].reshape(1, BATCH_S, STEPS, KVH, HD), got["sample_v"].reshape(1, BATCH_S, STEPS, KVH, HD),
            got["sample_retention"].reshape(1, BATCH_S, RH, RDK, RDV),
            got["sample_gmlp_v"].reshape(1, BATCH_S, STEPS, D))
```
